# Optimizing a Trainium2 kernel written in Bass

```python
import jax
import jax.numpy as jnp
from jax import lax
import numpy as np
import math

D_MODEL = 1024
BATCH = 1
SEQ = 512
DEPTH = 1

CTX_LEN = 256
GRID_W = 64
HEAD_DIM = 64
BRANCH_WIDTH = 512
N_BRANCH = 3
A_HEADS = 8
A_KV_HEADS = 2
WINDOW = 128
B_HEADS = 8
B_KV_HEADS = 2
C_HEADS = 4
C_DK = 128
C_DV = 128
CHUNK = 64
BLOCK = 128
D_FF = 2816
CONV_W = 3
ROPE_THETA = 10000.0
AXIS_ROPE_DIM = HEAD_DIM // 2
N_MOD = 6
EPS = 1e-6
NEG_BIG = -1e30
PROJ_SIZES = (A_HEADS * HEAD_DIM, A_KV_HEADS * HEAD_DIM, A_KV_HEADS * HEAD_DIM,
              B_HEADS * HEAD_DIM, B_KV_HEADS * HEAD_DIM, B_KV_HEADS * HEAD_DIM,
              C_HEADS * C_DK, C_HEADS * C_DK, C_HEADS * C_DK, C_HEADS * C_DV, C_HEADS * C_DV,
              N_BRANCH * D_MODEL)
PROJ_WIDTH = sum(PROJ_SIZES)


def rms_norm(t, g):
    tf = t.astype(jnp.float32)
    y = tf * lax.rsqrt(jnp.mean(tf * tf, axis=-1, keepdims=True) + EPS)
    return (y * g.astype(jnp.float32)).astype(t.dtype)

def axial_rope(n):
    rows = n // GRID_W
    row = jnp.repeat(jnp.arange(rows), GRID_W).astype(jnp.float32)
    col = jnp.tile(jnp.arange(GRID_W), rows).astype(jnp.float32)
    inv = ROPE_THETA ** (-jnp.arange(0, AXIS_ROPE_DIM, 2, dtype=jnp.float32) / AXIS_ROPE_DIM)
    ang = jnp.concatenate([row[:, None] * inv, col[:, None] * inv], axis=-1)
    return jnp.cos(ang), jnp.sin(ang)

def apply_rope(t, cos, sin):
    t1, t2 = t[..., 0::2], t[..., 1::2]
    c = cos[None, :, None, :].astype(t.dtype)
    s = sin[None, :, None, :].astype(t.dtype)
    return jnp.stack([t1 * c - t2 * s, t1 * s + t2 * c], axis=-1).reshape(t.shape)

def features(h, w_in, qn, kn, rope):
    B_, L, _ = h.shape
    split_at = np.cumsum(PROJ_SIZES)[:-1].tolist()
    aq, ak, av, bq, bk, bv, cq, cf, cb, ci, cg, gates = jnp.split(h @ w_in, split_at, axis=-1)
    heads = lambda t, n: t.reshape(B_, L, n, HEAD_DIM)
    aq, ak, av = heads(aq, A_HEADS), heads(ak, A_KV_HEADS), heads(av, A_KV_HEADS)
    bq = rms_norm(heads(bq, B_HEADS), qn)
    bk = rms_norm(heads(bk, B_KV_HEADS), kn)
    bv = heads(bv, B_KV_HEADS)
    if rope is not None:
        cos, sin = rope
        aq, ak, bq, bk = [apply_rope(t, cos, sin) for t in (aq, ak, bq, bk)]
    return aq, ak, av, bq, bk, bv, cq, cf, cb, ci, cg, gates

def dense_attn(q, k, v, sink=None):
    B_, Lq, HQ, hd = q.shape
    KV = k.shape[2]
    G = HQ // KV
    s = jnp.einsum('bqkgd,bjkd->bkgqj', q.reshape(B_, Lq, KV, G, hd), k).astype(jnp.float32) * hd ** -0.5
    if sink is not None:
        s_sink = jnp.broadcast_to(sink.astype(jnp.float32).reshape(1, KV, G, 1, 1), s.shape[:-1] + (1,))
        s = jnp.concatenate([s, s_sink], axis=-1)
    p = jax.nn.softmax(s, axis=-1)[..., :k.shape[1]].astype(v.dtype)
    return jnp.einsum('bkgqj,bjkd->bqkgd', p, v).reshape(B_, Lq, HQ * hd)

def window_attn(q, k, v, ck, cv, sink):
    B_, S, HQ, hd = q.shape
    KV = k.shape[2]
    G = HQ // KV
    nb = S // BLOCK
    n_ctx = ck.shape[1]
    qb = q.reshape(B_, nb, BLOCK, KV, G, hd)

    def band(t):
        tp = jnp.pad(t, ((0, 0), (BLOCK, BLOCK), (0, 0), (0, 0))).reshape(B_, nb + 2, BLOCK, KV, hd)
        return jnp.concatenate([tp[:, :-2], tp[:, 1:-1], tp[:, 2:]], axis=2)

    kb, vb = band(k), band(v)
    scale = hd ** -0.5
    s_loc = jnp.einsum('bnqkgd,bnjkd->bkgnqj', qb, kb).astype(jnp.float32) * scale
    blk = jnp.arange(nb)[:, None, None]
    qpos = blk * BLOCK + jnp.arange(BLOCK)[None, :, None]
    kpos = (blk - 1) * BLOCK + jnp.arange(3 * BLOCK)[None, None, :]
    valid = (jnp.abs(kpos - qpos) <= WINDOW) & (kpos >= 0) & (kpos < S)
    s_loc = jnp.where(valid, s_loc, NEG_BIG)
    s_ctx = jnp.einsum('bnqkgd,bjkd->bkgnqj', qb, ck).astype(jnp.float32) * scale
    s_sink = jnp.broadcast_to(sink.astype(jnp.float32).reshape(1, KV, G, 1, 1, 1), s_ctx.shape[:-1] + (1,))
    p = jax.nn.softmax(jnp.concatenate([s_ctx, s_loc, s_sink], axis=-1), axis=-1).astype(v.dtype)
    o = (jnp.einsum('bkgnqj,bjkd->bnqkgd', p[..., :n_ctx], cv)
         + jnp.einsum('bkgnqj,bnjkd->bnqkgd', p[..., n_ctx:n_ctx + 3 * BLOCK], vb))
    return o.reshape(B_, S, HQ * hd)

def global_attn(q, k, v, ck, cv):
    B_, S, HQ, hd = q.shape
    nb = S // BLOCK
    k_all = jnp.concatenate([ck, k], axis=1)
    v_all = jnp.concatenate([cv, v], axis=1)
    qb = jnp.moveaxis(q.reshape(B_, nb, BLOCK, HQ, hd), 1, 0)
    o = lax.map(lambda qblk: dense_attn(qblk, k_all, v_all), qb)
    return jnp.moveaxis(o, 0, 1).reshape(B_, S, HQ * hd)

def layer_lower_bounds(raw):
    p = jax.nn.softmax(raw.astype(jnp.float32), axis=0)
    return jnp.clip(jnp.cumsum(p, axis=0) - p[0], 0.0, 1.0)

def hgrn_forget(z, lb):
    log_f = jax.nn.log_sigmoid(z) + jnp.log1p(lb * jnp.exp(-z))
    k = (1.0 - lb) * jax.nn.sigmoid(-z)
    return k, log_f

def gla_chunk_scan(q, k, v, log_f, s0):
    B_, L, H, _ = q.shape
    nc = L // CHUNK
    to_chunks = lambda t: t.reshape(B_, nc, CHUNK, H, t.shape[-1]).transpose(1, 0, 3, 2, 4)
    tri = jnp.tril(jnp.ones((CHUNK, CHUNK), dtype=bool))[:, :, None]

    def step(s, inp):
        qi, ki, vi, fi = inp
        a = jnp.cumsum(fi, axis=2)
        o_inter = jnp.einsum('bhtd,bhde->bhte', qi * jnp.exp(a), s)
        diff = a[:, :, :, None, :] - a[:, :, None, :, :]
        decay = jnp.exp(jnp.where(tri, diff, NEG_BIG))
        scores = jnp.einsum('bhtd,bhjd,bhtjd->bhtj', qi, ki, decay)
        o_intra = jnp.einsum('bhtj,bhje->bhte', scores, vi)
        a_last = a[:, :, -1, :]
        s_new = (jnp.exp(a_last)[..., None] * s
                 + jnp.einsum('bhjd,bhje->bhde', ki * jnp.exp(a_last[:, :, None, :] - a), vi))
        return s_new, o_inter + o_intra

    s_fin, o = lax.scan(step, s0, (to_chunks(q), to_chunks(k), to_chunks(v), to_chunks(log_f)))
    return o.transpose(1, 0, 3, 2, 4).reshape(B_, L, H, v.shape[-1]), s_fin

def hgrn2_bidir(cq, cf, cb, ci, cg, lb_f, lb_b, gn, s0_f, s0_b):
    B_, L = cq.shape[:2]
    q = jax.nn.silu(cq.astype(jnp.float32)).reshape(B_, L, C_HEADS, C_DK)
    v = ci.astype(jnp.float32).reshape(B_, L, C_HEADS, C_DV)
    k_f, lf_f = hgrn_forget(cf.astype(jnp.float32).reshape(B_, L, C_HEADS, C_DK), lb_f.reshape(C_HEADS, C_DK))
    k_b, lf_b = hgrn_forget(cb.astype(jnp.float32).reshape(B_, L, C_HEADS, C_DK), lb_b.reshape(C_HEADS, C_DK))
    rev = lambda t: jnp.flip(t, axis=1)
    o_f, s_f = gla_chunk_scan(q, k_f, v, lf_f, s0_f)
    o_b, s_b = gla_chunk_scan(rev(q), rev(k_b), rev(v), rev(lf_b), s0_b)
    o = rms_norm(o_f + rev(o_b), gn) * jax.nn.silu(cg.astype(jnp.float32)).reshape(B_, L, C_HEADS, C_DV)
    return o.reshape(B_, L, C_HEADS * C_DV).astype(cq.dtype), s_f, s_b

def merge_branches(ya, yb, yc, gates, w_branch, w_out):
    B_, L = ya.shape[:2]
    ys = jnp.stack([ya, yb, yc], axis=2)
    up = jnp.einsum('blnw,nwd->blnd', ys, w_branch)
    g = jax.nn.sigmoid(gates.reshape(B_, L, N_BRANCH, -1))
    return jnp.sum(g * up, axis=2) @ w_out

def dwconv(u, w, b):
    y = lax.conv_general_dilated(u, w[:, None, :], window_strides=(1,),
                                 padding=((CONV_W // 2, CONV_W // 2),),
                                 dimension_numbers=('NWC', 'WIO', 'NWC'),
                                 feature_group_count=u.shape[-1])
    return y + b

def conv_ffn(h, w_up, w_dw, b_dw, w_down):
    a, g = jnp.split(dwconv(h @ w_up, w_dw, b_dw), 2, axis=-1)
    return (a * jax.nn.silu(g)) @ w_down

def first_inputs(seed: int = 0) -> dict:
    key = jax.random.key(seed)
    ks = jax.random.split(key, 22)
    nrm = lambda k, shape, s: jax.random.normal(k, shape, jnp.float32) * s
    L = DEPTH
    return {
        'x': nrm(ks[0], (BATCH, SEQ, D_MODEL), 1.0),
        'c': nrm(ks[1], (BATCH, D_MODEL), 1.0),
        'ctx': nrm(ks[2], (BATCH, CTX_LEN, D_MODEL), 1.0),
        'c_ctx': nrm(ks[3], (D_MODEL,), 1.0),
        'w_mod': nrm(ks[4], (L, D_MODEL, N_MOD * D_MODEL), 0.5 * D_MODEL ** -0.5),
        'b_mod': nrm(ks[5], (L, N_MOD * D_MODEL), 0.02),
        'norm_mix': 1.0 + nrm(ks[6], (L, D_MODEL), 0.05),
        'norm_ffn': 1.0 + nrm(ks[7], (L, D_MODEL), 0.05),
        'w_in': nrm(ks[8], (L, D_MODEL, PROJ_WIDTH), D_MODEL ** -0.5),
        'sink_a': nrm(ks[9], (L, A_HEADS), 0.5),
        'qn_b': 1.0 + nrm(ks[10], (L, HEAD_DIM), 0.05),
        'kn_b': 1.0 + nrm(ks[11], (L, HEAD_DIM), 0.05),
        'lb_fwd': nrm(ks[12], (L, C_HEADS * C_DK), 1.0),
        'lb_bwd': nrm(ks[13], (L, C_HEADS * C_DK), 1.0),
        'gn_c': 1.0 + nrm(ks[14], (L, C_DV), 0.05),
        'w_branch': nrm(ks[15], (L, N_BRANCH, BRANCH_WIDTH, D_MODEL), BRANCH_WIDTH ** -0.5),
        'w_out': nrm(ks[16], (L, D_MODEL, D_MODEL), D_MODEL ** -0.5),
        'w_up': nrm(ks[17], (L, D_MODEL, 2 * D_FF), D_MODEL ** -0.5),
        'w_dw': nrm(ks[18], (L, CONV_W, 2 * D_FF), CONV_W ** -0.5),
        'b_dw': nrm(ks[19], (L, 2 * D_FF), 0.02),
        'w_down': nrm(ks[20], (L, D_FF, D_MODEL), D_FF ** -0.5),
        'norm_final': 1.0 + nrm(ks[21], (D_MODEL,), 0.05),
    }

def first_block(x, c, ctx, c_ctx, w_mod, b_mod, norm_mix, norm_ffn, w_in, sink_a, qn_b, kn_b,
              lb_fwd, lb_bwd, gn_c, w_branch, w_out, w_up, w_dw, b_dw, w_down, norm_final):
    B_, S, D = x.shape
    rope = axial_rope(S)
    lbf = layer_lower_bounds(lb_fwd)
    lbb = layer_lower_bounds(lb_bwd)
    s0 = jnp.zeros((B_, C_HEADS, C_DK, C_DV), jnp.float32)
    for l in range(DEPTH):
        last = l == DEPTH - 1
        m_lat = (jax.nn.silu(c) @ w_mod[l] + b_mod[l]).reshape(B_, 1, N_MOD, D)
        m_ctx = (jax.nn.silu(c_ctx) @ w_mod[l] + b_mod[l]).reshape(N_MOD, D)

        h_lat = rms_norm(x, norm_mix[l]) * (1.0 + m_lat[:, :, 1]) + m_lat[:, :, 0]
        h_ctx = rms_norm(ctx, norm_mix[l]) * (1.0 + m_ctx[1]) + m_ctx[0]
        aq, ak, av, bq, bk, bv, cq, cf, cb, ci, cg, gates = features(h_lat, w_in[l], qn_b[l], kn_b[l], rope)
        caq, cak, cav, cbq, cbk, cbv, ccq, ccf, ccb, cci, ccg, cgates = features(h_ctx, w_in[l], qn_b[l], kn_b[l], None)

        yc_ctx, s_f, s_b = hgrn2_bidir(ccq, ccf, ccb, cci, ccg, lbf[l], lbb[l], gn_c[l], s0, s0)
        yc = hgrn2_bidir(cq, cf, cb, ci, cg, lbf[l], lbb[l], gn_c[l], s_f, s_b)[0]
        ya = window_attn(aq, ak, av, cak, cav, sink_a[l])
        yb = global_attn(bq, bk, bv, cbk, cbv)
        x_mix = x + m_lat[:, :, 2] * merge_branches(ya, yb, yc, gates, w_branch[l], w_out[l])

        h = rms_norm(x_mix, norm_ffn[l]) * (1.0 + m_lat[:, :, 4]) + m_lat[:, :, 3]
        x = x_mix + m_lat[:, :, 5] * conv_ffn(h, w_up[l], w_dw[l], b_dw[l], w_down[l])

        if not last:
            ya_c = dense_attn(caq, cak, cav, sink_a[l])
            yb_c = dense_attn(cbq, cbk, cbv)
            ctx_mix = ctx + m_ctx[2] * merge_branches(ya_c, yb_c, yc_ctx, cgates, w_branch[l], w_out[l])
            hc = rms_norm(ctx_mix, norm_ffn[l]) * (1.0 + m_ctx[4]) + m_ctx[3]
            ctx = ctx_mix + m_ctx[5] * conv_ffn(hc, w_up[l], w_dw[l], b_dw[l], w_down[l])
    return rms_norm(x, norm_final)


DEPTH_2 = 2

N_MEM = 256
ROPE_THETA_2 = 500000.0
Q_BLOCK = 128

MLA_HEADS = 8
MLA_NOPE = 64
MLA_ROPE = 32
MLA_V = 64
MLA_Q_LORA = 384
MLA_KV_LORA = 256

SGU_GROUPS = 4
SGU_GROUP_DIM = 64
SGU_WIDTH = SGU_GROUPS * SGU_GROUP_DIM
SGU_CHUNK = 128

DIFF_HEADS = 4
DIFF_QK_DIM = 32
DIFF_V_DIM = 2 * DIFF_QK_DIM
DIFF_ROT = (2 * DIFF_QK_DIM) // 4 // 2

MIX_WIDTH = MLA_HEADS * MLA_V + SGU_WIDTH + DIFF_HEADS * DIFF_V_DIM

P_CQ = MLA_Q_LORA
P_CKV = MLA_KV_LORA
P_KR = MLA_ROPE
P_SGU = 2 * SGU_WIDTH
P_DQ = DIFF_HEADS * 2 * DIFF_QK_DIM
P_DK = DIFF_HEADS * 2 * DIFF_QK_DIM
P_DV = DIFF_HEADS * DIFF_V_DIM
IN_WIDTH = P_CQ + P_CKV + P_KR + P_SGU + P_DQ + P_DK + P_DV
IN_SPLIT = (P_CQ, P_CQ + P_CKV, P_CQ + P_CKV + P_KR, P_CQ + P_CKV + P_KR + P_SGU,
            P_CQ + P_CKV + P_KR + P_SGU + P_DQ, P_CQ + P_CKV + P_KR + P_SGU + P_DQ + P_DK)

X_HEADS = 4
X_HEAD_DIM = D_MODEL // X_HEADS

CONV_WIDTH = 3


def rms_norm_2(x, g):
    xf = x.astype(jnp.float32)
    y = xf * lax.rsqrt(jnp.mean(xf * xf, axis=-1, keepdims=True) + EPS)
    return (y * g.astype(jnp.float32)).astype(x.dtype)

def layer_norm(x, g):
    xf = x.astype(jnp.float32)
    mu = jnp.mean(xf, axis=-1, keepdims=True)
    xc = xf - mu
    y = xc * lax.rsqrt(jnp.mean(xc * xc, axis=-1, keepdims=True) + EPS)
    return (y * g.astype(jnp.float32)).astype(x.dtype)

def rope_tables(positions, rot_dim):
    inv_freq = ROPE_THETA_2 ** (-jnp.arange(0, rot_dim, 2, dtype=jnp.float32) / rot_dim)
    ang = positions.astype(jnp.float32)[..., None] * inv_freq
    return jnp.cos(ang), jnp.sin(ang)

def apply_rope_2(x, cos, sin):
    bshape = cos.shape[:2] + (1,) * (x.ndim - 3) + cos.shape[-1:]
    c = cos.reshape(bshape)
    s = sin.reshape(bshape)
    xf = x.astype(jnp.float32)
    x1, x2 = jnp.split(xf, 2, axis=-1)
    return jnp.concatenate([x1 * c - x2 * s, x2 * c + x1 * s], axis=-1).astype(x.dtype)

def partial_rope(x, cos, sin, rot):
    return jnp.concatenate([apply_rope_2(x[..., :rot], cos, sin), x[..., rot:]], axis=-1)

def to_query_blocks(q):
    b, s = q.shape[:2]
    return jnp.moveaxis(q.reshape((b, s // Q_BLOCK, Q_BLOCK) + q.shape[2:]), 1, 0)

def from_query_blocks(o):
    nb, b, qb = o.shape[:3]
    return jnp.moveaxis(o, 0, 1).reshape((b, nb * qb) + o.shape[3:])

def blocked_attention(q, k, v, scale):
    def block(qb):
        s = jnp.einsum('bqhd,bkhd->bhqk', qb, k).astype(jnp.float32) * scale
        p = jax.nn.softmax(s, axis=-1).astype(v.dtype)
        return jnp.einsum('bhqk,bkhd->bqhd', p, v)
    return from_query_blocks(lax.map(block, to_query_blocks(q)))

def mla_group(cq, ckv, kr, g_cq, g_ckv, w_uq, w_ukv, cos, sin):
    b, s, _ = cq.shape
    q = (rms_norm_2(cq, g_cq) @ w_uq).reshape(b, s, MLA_HEADS, MLA_NOPE + MLA_ROPE)
    q = jnp.concatenate([q[..., :MLA_NOPE], apply_rope_2(q[..., MLA_NOPE:], cos, sin)], axis=-1)
    kv = (rms_norm_2(ckv, g_ckv) @ w_ukv).reshape(b, s, MLA_HEADS, MLA_NOPE + MLA_V)
    k_nope, v = kv[..., :MLA_NOPE], kv[..., MLA_NOPE:]
    k_rope = apply_rope_2(kr[:, :, None, :], cos, sin)
    k = jnp.concatenate([k_nope, jnp.broadcast_to(k_rope, (b, s, MLA_HEADS, MLA_ROPE))], axis=-1)
    o = blocked_attention(q, k, v, (MLA_NOPE + MLA_ROPE) ** -0.5)
    return o.reshape(b, s, MLA_HEADS * MLA_V)

def sgu_group(z, g_sgu, w_s, b_s):
    b, s, _ = z.shape
    nc = s // SGU_CHUNK
    z = jax.nn.gelu(z, approximate=True)
    u, v = jnp.split(z, 2, axis=-1)
    u = u.reshape(b, nc, SGU_CHUNK, SGU_GROUPS, SGU_GROUP_DIM)
    v = layer_norm(v.reshape(b, nc, SGU_CHUNK, SGU_GROUPS, SGU_GROUP_DIM), g_sgu)
    mixed = jnp.einsum('gts,bnsgc->bntgc', w_s, v) + b_s.T[:, :, None]
    return (u * mixed).reshape(b, s, SGU_WIDTH)

def diff_group(dq, dk, dv, lam, lam_init, g_sub, cos, sin):
    b, s, _ = dq.shape
    q = partial_rope(dq.reshape(b, s, DIFF_HEADS, 2, DIFF_QK_DIM), cos, sin, 2 * DIFF_ROT)
    k = partial_rope(dk.reshape(b, s, DIFF_HEADS, 2, DIFF_QK_DIM), cos, sin, 2 * DIFF_ROT)
    v = dv.reshape(b, s, DIFF_HEADS, DIFF_V_DIM)
    scale = DIFF_QK_DIM ** -0.5

    def block(qb):
        sc = jnp.einsum('bqhcd,bkhcd->bhcqk', qb, k).astype(jnp.float32) * scale
        p = jax.nn.softmax(sc, axis=-1)
        a = (p[:, :, 0] - lam * p[:, :, 1]).astype(v.dtype)
        return jnp.einsum('bhqk,bkhe->bqhe', a, v)

    o = from_query_blocks(lax.map(block, to_query_blocks(q)))
    o = rms_norm_2(o, g_sub) * (1.0 - lam_init)
    return o.reshape(b, s, DIFF_HEADS * DIFF_V_DIM)

def memory_cross_attention(h, mem_n, w_q, w_kv, w_o):
    b, s, _ = h.shape
    m = mem_n.shape[1]
    q = (h @ w_q).reshape(b, s, X_HEADS, X_HEAD_DIM)
    kv = (mem_n @ w_kv).reshape(b, m, 2, X_HEADS, X_HEAD_DIM)
    k, v = kv[:, :, 0], kv[:, :, 1]
    sc = jnp.einsum('bqhd,bkhd->bhqk', q, k).astype(jnp.float32) * (X_HEAD_DIM ** -0.5)
    p = jax.nn.softmax(sc, axis=-1).astype(v.dtype)
    o = jnp.einsum('bhqk,bkhd->bqhd', p, v).reshape(b, s, D_MODEL)
    return o @ w_o

def conv_ffn_2(h, w_up, conv_w, conv_b, w_down):
    a = h @ w_up
    a = lax.conv_general_dilated(
        a, conv_w[:, None, :], window_strides=(1,),
        padding=((CONV_WIDTH // 2, CONV_WIDTH // 2),),
        dimension_numbers=('NWC', 'WIO', 'NWC'),
        feature_group_count=2 * D_FF) + conv_b
    g, u = jnp.split(a, 2, axis=-1)
    return (jax.nn.gelu(g, approximate=True) * u) @ w_down

def second_inputs(seed: int = 0) -> dict:
    key = jax.random.key(seed)
    ks = iter(jax.random.split(key, 40))

    def nrm(shape, scale):
        return jax.random.normal(next(ks), shape, jnp.float32) * scale

    def gain(dim_shape):
        return 1.0 + nrm((DEPTH_2,) + dim_shape, 0.05)

    x = nrm((BATCH, SEQ, D_MODEL), 1.0)
    mem = nrm((BATCH, N_MEM, D_MODEL), 1.0)
    offsets = jax.random.randint(next(ks), (BATCH, 1), 0, 4096, dtype=jnp.int32)
    positions = offsets + jnp.arange(SEQ, dtype=jnp.int32)[None, :]
    return {
        'x': x, 'mem': mem, 'positions': positions,
        'mix_pre_g': gain((D_MODEL,)),
        'mix_post_g': gain((D_MODEL,)),
        'w_in': nrm((DEPTH_2, D_MODEL, IN_WIDTH), D_MODEL ** -0.5),
        'mla_cq_g': gain((MLA_Q_LORA,)),
        'mla_ckv_g': gain((MLA_KV_LORA,)),
        'mla_w_uq': nrm((DEPTH_2, MLA_Q_LORA, MLA_HEADS * (MLA_NOPE + MLA_ROPE)), MLA_Q_LORA ** -0.5),
        'mla_w_ukv': nrm((DEPTH_2, MLA_KV_LORA, MLA_HEADS * (MLA_NOPE + MLA_V)), MLA_KV_LORA ** -0.5),
        'sgu_norm_g': gain((SGU_GROUPS, SGU_GROUP_DIM)),
        'sgu_w_s': nrm((DEPTH_2, SGU_GROUPS, SGU_CHUNK, SGU_CHUNK), SGU_CHUNK ** -0.5),
        'sgu_b_s': gain((SGU_GROUPS, SGU_CHUNK)),
        'diff_lam_q1': nrm((DEPTH_2, DIFF_QK_DIM), 0.1),
        'diff_lam_k1': nrm((DEPTH_2, DIFF_QK_DIM), 0.1),
        'diff_lam_q2': nrm((DEPTH_2, DIFF_QK_DIM), 0.1),
        'diff_lam_k2': nrm((DEPTH_2, DIFF_QK_DIM), 0.1),
        'diff_sub_g': gain((DIFF_V_DIM,)),
        'w_mix_out': nrm((DEPTH_2, MIX_WIDTH, D_MODEL), MIX_WIDTH ** -0.5),
        'mem_pre_g': gain((D_MODEL,)),
        'mem_post_g': gain((D_MODEL,)),
        'mem_kv_g': gain((D_MODEL,)),
        'mem_w_q': nrm((DEPTH_2, D_MODEL, D_MODEL), D_MODEL ** -0.5),
        'mem_w_kv': nrm((DEPTH_2, D_MODEL, 2 * D_MODEL), D_MODEL ** -0.5),
        'mem_w_o': nrm((DEPTH_2, D_MODEL, D_MODEL), D_MODEL ** -0.5),
        'ffn_pre_g': gain((D_MODEL,)),
        'ffn_post_g': gain((D_MODEL,)),
        'ffn_w_up': nrm((DEPTH_2, D_MODEL, 2 * D_FF), D_MODEL ** -0.5),
        'ffn_conv_w': nrm((DEPTH_2, CONV_WIDTH, 2 * D_FF), CONV_WIDTH ** -0.5),
        'ffn_conv_b': nrm((DEPTH_2, 2 * D_FF), 0.01),
        'ffn_w_down': nrm((DEPTH_2, D_FF, D_MODEL), D_FF ** -0.5),
    }

def second_block(x, mem, positions,
              mix_pre_g, mix_post_g, w_in, mla_cq_g, mla_ckv_g, mla_w_uq, mla_w_ukv,
              sgu_norm_g, sgu_w_s, sgu_b_s,
              diff_lam_q1, diff_lam_k1, diff_lam_q2, diff_lam_k2, diff_sub_g, w_mix_out,
              mem_pre_g, mem_post_g, mem_kv_g, mem_w_q, mem_w_kv, mem_w_o,
              ffn_pre_g, ffn_post_g, ffn_w_up, ffn_conv_w, ffn_conv_b, ffn_w_down):
    cos_a, sin_a = rope_tables(positions, MLA_ROPE)
    cos_d, sin_d = rope_tables(positions, 2 * DIFF_ROT)
    f32 = jnp.float32
    for l in range(DEPTH_2):
        lam_init = 0.8 - 0.6 * math.exp(-0.3 * l)
        h = rms_norm_2(x, mix_pre_g[l])
        proj = h @ w_in[l]
        cq, ckv, kr, z, dq, dk, dv = jnp.split(proj, IN_SPLIT, axis=-1)
        out_a = mla_group(cq, ckv, kr, mla_cq_g[l], mla_ckv_g[l], mla_w_uq[l], mla_w_ukv[l], cos_a, sin_a)
        out_b = sgu_group(z, sgu_norm_g[l], sgu_w_s[l], sgu_b_s[l])
        lam = (jnp.exp(jnp.sum(diff_lam_q1[l].astype(f32) * diff_lam_k1[l].astype(f32)))
               - jnp.exp(jnp.sum(diff_lam_q2[l].astype(f32) * diff_lam_k2[l].astype(f32)))
               + lam_init)
        out_c = diff_group(dq, dk, dv, lam, lam_init, diff_sub_g[l], cos_d, sin_d)
        mix = jnp.concatenate([out_a, out_b, out_c], axis=-1) @ w_mix_out[l]
        x = x + rms_norm_2(mix, mix_post_g[l])
        h = rms_norm_2(x, mem_pre_g[l])
        mem_n = rms_norm_2(mem, mem_kv_g[l])
        x = x + rms_norm_2(memory_cross_attention(h, mem_n, mem_w_q[l], mem_w_kv[l], mem_w_o[l]), mem_post_g[l])
        h = rms_norm_2(x, ffn_pre_g[l])
        x = x + rms_norm_2(conv_ffn_2(h, ffn_w_up[l], ffn_conv_w[l], ffn_conv_b[l], ffn_w_down[l]), ffn_post_g[l])
    return x


def setup_inputs(seed=0):
    out = dict(first_inputs(seed))
    for name, value in second_inputs(seed + 1).items():
        if name != "x":
            out[name + "_2"] = value
    return out


def reference(
    x, c, ctx, c_ctx, w_mod, b_mod, norm_mix, norm_ffn, w_in, sink_a, qn_b, kn_b, lb_fwd,
    lb_bwd, gn_c, w_branch, w_out, w_up, w_dw, b_dw, w_down, norm_final, mem_2, positions_2,
    mix_pre_g_2, mix_post_g_2, w_in_2, mla_cq_g_2, mla_ckv_g_2, mla_w_uq_2, mla_w_ukv_2,
    sgu_norm_g_2, sgu_w_s_2, sgu_b_s_2, diff_lam_q1_2, diff_lam_k1_2, diff_lam_q2_2,
    diff_lam_k2_2, diff_sub_g_2, w_mix_out_2, mem_pre_g_2, mem_post_g_2, mem_kv_g_2, mem_w_q_2,
    mem_w_kv_2, mem_w_o_2, ffn_pre_g_2, ffn_post_g_2, ffn_w_up_2, ffn_conv_w_2, ffn_conv_b_2,
    ffn_w_down_2,
):
    x = first_block(
        x, c, ctx, c_ctx, w_mod, b_mod, norm_mix, norm_ffn, w_in, sink_a, qn_b, kn_b, lb_fwd,
        lb_bwd, gn_c, w_branch, w_out, w_up, w_dw, b_dw, w_down, norm_final,
    )
    return second_block(
        x, mem_2, positions_2, mix_pre_g_2, mix_post_g_2, w_in_2, mla_cq_g_2, mla_ckv_g_2,
        mla_w_uq_2, mla_w_ukv_2, sgu_norm_g_2, sgu_w_s_2, sgu_b_s_2, diff_lam_q1_2,
        diff_lam_k1_2, diff_lam_q2_2, diff_lam_k2_2, diff_sub_g_2, w_mix_out_2, mem_pre_g_2,
        mem_post_g_2, mem_kv_g_2, mem_w_q_2, mem_w_kv_2, mem_w_o_2, ffn_pre_g_2, ffn_post_g_2,
        ffn_w_up_2, ffn_conv_w_2, ffn_conv_b_2, ffn_w_down_2,
    )


_drawn_inputs = setup_inputs


def setup_inputs(seed=0):
    import zlib

    import numpy as np

    out = dict(_drawn_inputs(seed))
    spreads = {}
    factors = {'norm_mix': 4.802,
     'sink_a': 8.0,
     'qn_b': 8.0,
     'kn_b': 8.0,
     'gn_c': 6.491,
     'b_dw': 4.158,
     'mla_cq_g_2': 8.0,
     'mla_ckv_g_2': 4.38,
     'diff_lam_k1_2': 4.438,
     'diff_lam_k2_2': 3.819,
     'ffn_conv_b_2': 5.833,
     'sgu_norm_g_2': 3.589,
     'sgu_b_s_2': 3.56,
     'diff_sub_g_2': 2.933}
    for name, (base, spread) in spreads.items():
        noise = np.random.default_rng([zlib.crc32(name.encode()), seed]).standard_normal(out[name].shape)
        drawn = base * np.exp(spread * noise) if base else spread * noise
        out[name] = jnp.asarray(drawn.astype(out[name].dtype))
    for name, factor in factors.items():
        out[name] = (out[name] * factor).astype(out[name].dtype)
    return out
```

```python
from contextlib import ExitStack

import numpy as np

import concourse.bass as bass
from concourse import mybir

F32 = mybir.dt.float32
I32 = mybir.dt.int32
ALU = mybir.AluOpType
ACT = mybir.ActivationFunctionType
AX = mybir.AxisListType

P = 128
D = 1024
KT = D // P
T = 512
TB = T // P
CT = 256
CB = CT // P
ALLT = CT + T
FF = 2816
FT = FF // P
HD = 64
EPS = 1e-6
NEG_BIG = -1e30
LAYERS = 2
MEM = 256
GRID_W = 64
THETA_1, THETA_2 = 10000.0, 500000.0
CHUNK = 64
LEVELS = 7
C_HEADS = 4

SLAB = 16
RING = 4
MOD_TILES = 6 * KT
QKV_BLOCKS = 6 * KT
B1_AT = {}
_at = 0
for _name, _n in (("mod", MOD_TILES * KT), ("A", QKV_BLOCKS), ("B", QKV_BLOCKS), ("C", 16 * KT),
                  ("cg", 4 * KT), ("merge", KT * 3 * (KT + 4)), ("out", KT * KT), ("up", 2 * FT * KT),
                  ("down", KT * FT)):
    B1_AT[_name] = _at
    _at += _n
B1_SLABS = _at // SLAB
assert _at == B1_SLABS * SLAB
B2_AT = {}
_at = 0
for _name, _n in (("in", 16 * KT), ("uq", 8 * 3), ("uk", 8 * 2), ("uv", 4 * 2), ("mix", KT * KT),
                  ("mq", KT * KT), ("mk", KT * KT), ("mv", KT * KT), ("mo", KT * KT),
                  ("up", 2 * FT * KT), ("down", KT * FT)):
    B2_AT[_name] = _at
    _at += _n
B2_SLABS = _at // SLAB
assert _at == B2_SLABS * SLAB and B2_SLABS % RING == 0
for _at in (B1_AT["up"], B2_AT["up"]):
    assert _at % SLAB == 0 and 2 * KT == SLAB
SLABS = B1_SLABS + LAYERS * B2_SLABS
PER_LAYER = {'params_loaded_2': 16, 'lam_dots_2': 1, 'lam_exp_2': 1, 'square_ready_2': 63, 'square_summed_2': 63, 'scale_ready_2': 11, 'normed_2': 63, 'tile_done_2': 84, 'out_by_act_2': 56, 'out_by_dve_2': 28, 'rotated_2': 13, 'by_cos_2': 13, 'by_sin_2': 13, 'roped_2': 13, 'centered_2': 1, 'sgu_square_ready_2': 1, 'var_ready_2': 1, 'rstd_ready_2': 1, 'gate_ready_2': 1, 'chunks_mixed_2': 1, 'staged_2': 10, 'scored_2': 64, 'max_ready_2': 64, 'exp_done_2': 64, 'diag_ready_2': 64, 'turned0_2': 64, 'turned1_2': 64, 'probs_out0_2': 64, 'probs_out1_2': 64, 'summed_2': 10, 'sum_read_2': 16, 'pair_done_2': 22, 'center_ready_2': 22, 'banks_free_2': 26, 'acted_2': 22, 'gated_2': 24}


def columns(fields):
    at, places = 0, {}
    for name, n in fields:
        places[name] = at
        at += n
    return places, at


CONST, CONST_W = columns([
    ("ident", P), ("ones", P), ("ones64", P), ("rot1", P), ("rot_mla", P), ("rot_diff", P),
    ("mask_prev", P), ("mask_next", P), ("levels", 2 * (LEVELS + 1) * P), ("reset", 2 * ALLT),
    ("cos1", T), ("sin1", T), ("freq", 2), ("eps", 1), ("half_pi", 1), ("one", 1)])
PAR1, PAR1_W = columns([
    ("c", 2 * KT), ("b_mod", MOD_TILES), ("norm_mix", KT), ("norm_ffn", KT), ("qn", 1), ("kn", 1),
    ("lb", 2 * C_HEADS), ("gn", 1), ("conv_w", 3 * 2 * FT), ("conv_b", 2 * FT), ("norm_final", KT),
    ("sink", 8)])
PAR2, PAR2_W = columns([
    ("mix_pre", KT), ("mix_post", KT), ("cq_g", 3), ("ckv_g", 2), ("sub_g", 1), ("mem_pre", KT),
    ("mem_post", KT), ("mem_kv", KT), ("ffn_pre", KT), ("ffn_post", KT), ("conv_w", 3 * 2 * FT),
    ("conv_b", 2 * FT), ("lam", 4 * 32), ("lam_init", 1), ("one_less_lam", 1), ("sgu_g", 256),
    ("sgu_b", 2 * P), ("sgu_w", 4 * P)])


def build_program(nc, stream, xT_in, ctxT_in, memT_in, pos_in, const_in, par1_in, par2_in, out, upto=99):
    stack = ExitStack()
    with stack:
        def sb(name, shape, dt=F32):
            return stack.enter_context(nc.sbuf_tensor(name, shape, dt))

        ring = sb("ring", [P, RING, SLAB, P])
        xT = sb("xT", [P, KT, T])
        hT = sb("hT", [P, KT, T])
        const = sb("const", [P, CONST_W])
        par1 = sb("par1", [P, PAR1_W])
        small = sb("small", [P, 256])
        bank = stack.enter_context(nc.psum_tensor("bank", [P, 8, 512], F32))

        def con(name, n=P, at=0):
            return const[:, CONST[name] + at:CONST[name] + at + n]

        def p1(name, n=1, at=0):
            return par1[:, PAR1[name] + at:PAR1[name] + at + n]

        layer = [None]

        roles, used_here = {}, {}

        class Signal:

            def __init__(self, role, count):
                role = role if layer[0] is None else f"{role}_2"
                if role not in roles:
                    roles[role] = stack.enter_context(nc.semaphore(role))
                self.sem, self.start = roles[role], used_here.get(role, 0)
                self.per_layer = 0 if layer[0] is None else PER_LAYER[role]
                used_here[role] = self.start + count

            def at(self, n):
                n = n + self.start
                return n if layer[0] is None else n + layer[0] * self.per_layer

        slab_loaded = [stack.enter_context(nc.semaphore(f"slab_loaded{r}")) for r in range(RING)]
        slab_begun = stack.enter_context(nc.semaphore("slab_begun"))

        class Stream:
            base, fed, begun, pending = 0, 0, 0, False

            def slabs_before(self):
                return self.base if layer[0] is None else layer[0] * B2_SLABS + self.base

            def need(self, pe, block):
                slab = block // SLAB
                if slab >= self.begun:
                    assert slab == self.begun
                    turn = (self.base + slab) // RING + 1
                    if layer[0] is not None:
                        turn = layer[0] * (B2_SLABS // RING) + turn
                    pe.wait_ge(slab_loaded[(self.base + slab) % RING], turn * 16)
                    self.begun += 1
                    self.pending = True

            def block(self, b, n=1):
                slab, at = divmod(b, SLAB)
                assert at + n <= SLAB
                return ring[:, (self.base + slab) % RING, at:at + n, :].rearrange("p b n -> p (b n)")

            def mm(self, pe, block, out, lhsT, rhs, start, stop):
                self.need(pe, block)
                ins = nc.tensor.matmul(out, lhsT, rhs, start=start, stop=stop)
                if self.pending:
                    ins.then_inc(slab_begun, 1)
                    self.pending = False
                return ins

            def feed(self, sp, last):
                upto_slab = min(last, self.begun + RING - 1)
                while self.fed < upto_slab:
                    s = self.fed
                    g = self.base + s
                    if layer[0] is not None or g >= RING:
                        v = g - RING + 2
                        sp.wait_ge(slab_begun, v if layer[0] is None else layer[0] * B2_SLABS + v)
                    if layer[0] is None:
                        src = stream[g]
                    else:
                        src = stream[bass.ds(layer[0] * B2_SLABS + g, 1)].rearrange("o p n -> p (o n)")
                    sp.dma_start(ring[:, g % RING, :, :].rearrange("p b n -> p (b n)"), src)\
                        .then_inc(slab_loaded[g % RING], 16)
                    self.fed += 1

        ws = Stream()
        ws.limit = B1_SLABS

        def stage(name, tensor=None, scalar=None, vector=None, gpsimd=None, sync=None):
            with nc.Block() as block:
                if tensor:
                    @block.tensor
                    def _(pe):
                        tensor(pe)

                @block.sync
                def _(sp):
                    if sync:
                        sync(sp)
                    ws.feed(sp, ws.limit)
                if scalar:
                    @block.scalar
                    def _(act):
                        scalar(act)
                if vector:
                    @block.vector
                    def _(dve):
                        vector(dve)
                if gpsimd:
                    @block.gpsimd
                    def _(pool):
                        gpsimd(pool)

        def bcast(ap, n):
            return ap.rearrange("p (k o) -> p k o", o=1).to_broadcast([P, ap.shape[1], n])

        def linear(name, tiles, banks=8, sync=None):
            n_act = sum(t[0] == "act" for t in tiles)
            tile_done = Signal("tile_done", len(tiles))
            out_by = {"act": Signal("out_by_act", n_act),
                      "dve": Signal("out_by_dve", len(tiles) - n_act)}
            ordinal, seen = [], {"act": 0, "dve": 0}
            for t in tiles:
                seen[t[0]] += 1
                ordinal.append(seen[t[0]])

            def tensor(pe):
                n = 0
                while n < len(tiles):
                    cols, products = tiles[n][1:3]
                    members = 1 if callable(products) else len(products["tokens"])
                    for m in range(n, n + members):
                        if m >= banks:
                            pe.wait_ge(out_by[tiles[m - banks][0]].sem, out_by[tiles[m - banks][0]].at(ordinal[m - banks]))
                    outs = [bank[:, m % banks, 0:cols] for m in range(n, n + members)]
                    if members == 1:
                        products(pe, outs[0]).then_inc(tile_done.sem, 1)
                    else:
                        kts, width = products["kts"], products["width"]
                        for k in range(kts):
                            b = products["at"] + k * width
                            for out_ap, lhsT in zip(outs, products["tokens"]):
                                last = ws.mm(pe, b, out_ap, lhsT(k), ws.block(b, width), k == 0, k == kts - 1)
                                if k == kts - 1:
                                    last.then_inc(tile_done.sem, 1)
                    n += members

            def read_out(which):
                def program(eng):
                    for n, (engine, cols, _, out_fn, *before) in enumerate(tiles):
                        if engine == which:
                            for b in before:
                                eng.wait_ge(out_by[tiles[b][0]].sem, out_by[tiles[b][0]].at(ordinal[b]))
                            eng.wait_ge(tile_done.sem, tile_done.at(n + 1))
                            out_fn(eng, bank[:, n % banks, 0:cols]).then_inc(out_by[which].sem, 1)
                return program

            stage(name, tensor=tensor, scalar=read_out("act"), vector=read_out("dve"), sync=sync)

        def weights_still(at, kts, rhs):
            def products(pe, out_ap):
                for k in range(kts):
                    last = ws.mm(pe, at + k, out_ap, ws.block(at + k), rhs(k), k == 0, k == kts - 1)
                return last
            return products

        def weights_moving(at, kts, n, lhsT, step=None):
            def products(pe, out_ap):
                for k in range(kts):
                    b = at + k * (step or n)
                    last = ws.mm(pe, b, out_ap, lhsT(k), ws.block(b, n), k == 0, k == kts - 1)
                return last
            return products

        def value_group(at, kts, n, tokens):
            return dict(at=at, kts=kts, width=n, tokens=tokens)

        def act_copy(dst, func=ACT.Copy):
            return lambda act, ps: nc.scalar.activation(dst, ps, func)

        def dve_copy(dst):
            return lambda dve, ps: nc.vector.tensor_copy(dst, ps)

        def norms(name, jobs, squares, scales, sync=None):
            total = sum(j["tiles"] for j in jobs)
            square_ready = Signal("square_ready", total)
            square_summed = Signal("square_summed", total)
            scale_ready = Signal("scale_ready", len(jobs))
            normed = Signal("normed", total)
            starts = []
            at = 0
            for j in jobs:
                starts.append(at)
                at += j["tiles"]

            def scalar(act):
                def square(n):
                    j = jobs[n]
                    for k in range(j["tiles"]):
                        q = starts[n] + k
                        if q >= 8:
                            act.wait_ge(square_summed.sem, square_summed.at(q - 7))
                        nc.scalar.activation(squares[:, q % 8, 0:j["cols"]], j["src"](k), ACT.Square)\
                            .then_inc(square_ready.sem, 1)
                square(0)
                for n, j in enumerate(jobs):
                    if n + 1 < len(jobs):
                        square(n + 1)
                    act.wait_ge(square_summed.sem, square_summed.at(starts[n] + j["tiles"]))
                    if n >= 2:
                        act.wait_ge(normed.sem, normed.at(starts[n - 1]))
                    s = scales[:, n % 2, 0:j["cols"]]
                    nc.scalar.activation(s, bank[:, n % 2, 0:j["cols"]], ACT.Ln, bias=con("eps", 1), scale=j["inv"])
                    act.drain()
                    nc.scalar.activation(s, s, ACT.Exp, scale=-0.5).then_inc(scale_ready.sem, 1)

            def tensor(pe):
                for n, j in enumerate(jobs):
                    if n >= 2:
                        pe.wait_ge(scale_ready.sem, scale_ready.at(n - 1))
                    for k in range(j["tiles"]):
                        q = starts[n] + k
                        pe.wait_ge(square_ready.sem, square_ready.at(q + 1))
                        nc.tensor.matmul(bank[:, n % 2, 0:j["cols"]], j["ones"], squares[:, q % 8, 0:j["cols"]],
                                         start=k == 0, stop=k == j["tiles"] - 1).then_inc(square_summed.sem, 1)

            def vector(dve):
                for n, j in enumerate(jobs):
                    dve.wait_ge(scale_ready.sem, scale_ready.at(n + 1))
                    for k in range(j["tiles"]):
                        ends = j["end"] and j["end"][0] in ("residual", "times")
                        dst = squares[:, (starts[n] + k) % 8, 0:j["cols"]] if ends else j["out"](k)
                        nc.vector.scalar_tensor_tensor(dst, j["src"](k), j["gain"](k), scales[:, n % 2, 0:j["cols"]],
                                                       ALU.mult, ALU.mult).then_inc(normed.sem, 1)

            def gpsimd(pool):
                for n, j in enumerate(jobs):
                    if not j["end"]:
                        continue
                    how, other = j["end"]
                    assert how == "shift" or total <= 8
                    for k in range(j["tiles"]):
                        pool.wait_ge(normed.sem, normed.at(starts[n] + k + 1))
                        if how == "shift":
                            nc.gpsimd.tensor_scalar(j["out"](k), j["out"](k), other(k), None, ALU.add)
                        else:
                            nc.gpsimd.tensor_tensor(j["out"](k), other(k), squares[:, starts[n] + k, 0:j["cols"]],
                                                    ALU.add if how == "residual" else ALU.mult)

            stage(name, tensor=tensor, scalar=scalar, vector=vector, gpsimd=gpsimd, sync=sync)

        def rope(name, jobs, work):
            n_jobs = len(jobs)
            rotated = Signal("rotated", n_jobs)
            by_cos = Signal("by_cos", n_jobs)
            by_sin = Signal("by_sin", n_jobs)
            roped = Signal("roped", n_jobs)

            def tensor(pe):
                for n, (raw, rot, _, _, _) in enumerate(jobs):
                    if n >= 4:
                        pe.wait_ge(by_sin.sem, by_sin.at(n - 3))
                    nc.tensor.matmul(bank[:, n % 4, :], rot, raw, start=True, stop=True).then_inc(rotated.sem, 1)

            def vector(dve):
                for n, (_, _, _, sin, _) in enumerate(jobs):
                    dve.wait_ge(rotated.sem, rotated.at(n + 1))
                    if n >= 2:
                        dve.wait_ge(roped.sem, roped.at(n - 1))
                    nc.vector.tensor_tensor(work[:, 2 + n % 2, :], bank[:, n % 4, :], sin, ALU.mult)\
                        .then_inc(by_sin.sem, 1)

            def gpsimd(pool):
                def cosine(n):
                    raw, _, cos, _, _ = jobs[n]
                    nc.gpsimd.tensor_tensor(work[:, n % 2, :], raw, cos, ALU.mult).then_inc(by_cos.sem, 1)
                cosine(0)
                for n in range(n_jobs):
                    if n + 1 < n_jobs:
                        cosine(n + 1)
                    pool.wait_ge(by_cos.sem, by_cos.at(n + 1))
                    pool.wait_ge(by_sin.sem, by_sin.at(n + 1))
                    nc.gpsimd.tensor_tensor(jobs[n][4], work[:, n % 2, :], work[:, 2 + n % 2, :], ALU.add)\
                        .then_inc(roped.sem, 1)
                    pool.drain()

            stage(name, tensor=tensor, vector=vector, gpsimd=gpsimd)

        def attention(name, turns, units, scale, copies, zeros, read_out, work, sink=None, neg_lam=None, shared_out=False):
            U = len(units[0])
            units = units[0] + units[1]
            N = len(units)
            passes = turns // 2
            total = turns * U
            staged = Signal("staged", turns)
            scored = Signal("scored", total)
            max_ready = Signal("max_ready", total)
            exp_done = Signal("exp_done", total)
            diag_ready = Signal("diag_ready", total)
            turned = [Signal(f"turned{h}", total) for h in range(2)]
            probs_out = [Signal(f"probs_out{h}", total) for h in range(2)]
            summed = Signal("summed", turns)
            sum_read = Signal("sum_read", turns + 2)
            C = len(units[0]["scores"])
            probs, probsT, diag, stat = work

            def score_cols(u):
                return bank[:, 2 * (u % 2):2 * (u % 2) + 2, :].rearrange("p b n -> p (b n)")

            def halves(u):
                k = units[u]["keys"]
                return (0, (k + 1) // 2), ((k + 1) // 2, k)

            def turned_cols(h, n):
                return bank[:, 4 + h, 0:n * P]

            def tensor(pe):
                def scores(i, u):
                    if u % U == 0:
                        pe.wait_ge(staged.sem, staged.at(2 * i + (u // U + 1)))
                    if u >= 2:
                        pe.wait_ge(exp_done.sem, exp_done.at(i * N + (u - 1)))
                    S = score_cols(u)
                    for c, score in enumerate(units[u]["scores"]):
                        for lo, hi, pairs in score(2 * i + u // U):
                            for k, (lhsT, rhs) in enumerate(pairs):
                                last = nc.tensor.matmul(S[:, c * 512 + lo:c * 512 + hi], lhsT, rhs,
                                                        start=k == 0, stop=k == len(pairs) - 1)
                    last.then_inc(scored.sem, 1)

                def transposes(i, u):
                    pe.wait_ge(diag_ready.sem, diag_ready.at(i * N + (u + 1)))
                    for h, (lo, hi) in enumerate(halves(u)):
                        if u > 0:
                            pe.wait_ge(probs_out[h].sem, probs_out[h].at(i * N + u))
                        for j in range(lo, hi):
                            for c in range(C):
                                at = c * 512 + j * P
                                last = nc.tensor.matmul(turned_cols(h, hi - lo)[:, (j - lo) * P:(j - lo + 1) * P],
                                                        probs[:, u % 2, at:at + P], diag[:, u % 2, c, :],
                                                        start=c == 0, stop=c == C - 1)
                        last.then_inc(turned[h].sem, 1)

                def values(i, u):
                    t = u // U
                    if u % U == 0:
                        pe.wait_ge(sum_read.sem, sum_read.at(2 * i + (t + (2 if shared_out else 1))))
                    for h in range(2):
                        pe.wait_ge(probs_out[h].sem, probs_out[h].at(i * N + (u + 1)))
                    for out_ap, lhs in units[u]["values"]:
                        for j, lhsT in enumerate(lhs):
                            last = nc.tensor.matmul(out_ap, lhsT, probsT[:, u % 2, j * P:(j + 1) * P],
                                                    start=j == 0, stop=j == len(lhs) - 1)
                    if u % U == U - 1:
                        last.then_inc(summed.sem, 1)

                with pe.Fori(0, passes) as i:
                    scores(i, 0)
                    scores(i, 1)
                    transposes(i, 0)
                    for u in range(N):
                        if u + 2 < N:
                            scores(i, u + 2)
                        if u + 1 < N:
                            transposes(i, u + 1)
                        values(i, u)

            def scalar(act):
                def exps(i, u):
                    act.wait_ge(max_ready.sem, max_ready.at(i * N + (u + 1)))
                    if u >= 2:
                        act.wait_ge(turned[1].sem, turned[1].at(i * N + (u - 1)))
                    S = score_cols(u)
                    w = units[u]["width"]
                    for c in range(C):
                        last = nc.scalar.activation(probs[:, u % 2, c * 512:c * 512 + w], S[:, c * 512:c * 512 + w],
                                                    ACT.Exp, bias=stat[:, u % 2, 1, c:c + 1], scale=scale,
                                                    accum_out=stat[:, u % 2, 2, c:c + 1])
                    last.then_inc(exp_done.sem, 1)

                def out_half(i, u):
                    act.wait_ge(turned[0].sem, turned[0].at(i * N + (u + 1)))
                    n = halves(u)[0][1]
                    nc.scalar.activation(probsT[:, u % 2, 0:n * P], turned_cols(0, n), ACT.Copy)\
                        .then_inc(probs_out[0].sem, 1)

                with act.Fori(0, passes) as i:
                    exps(i, 0)
                    exps(i, 1)
                    out_half(i, 0)
                    for u in range(N):
                        if u + 1 < N:
                            out_half(i, u + 1)
                        if u + 2 < N:
                            exps(i, u + 2)

            def vector(dve):
                def maxima(i, u):
                    dve.wait_ge(scored.sem, scored.at(i * N + (u + 1)))
                    S = score_cols(u)
                    unit = units[u]
                    for lo, mask in unit["masks"]:
                        nc.vector.tensor_tensor(S[:, lo:lo + P], S[:, lo:lo + P], mask, ALU.add)
                    if unit["sink"] is not None:
                        nc.vector.tensor_copy(S[:, unit["sink"]:unit["sink"] + 1], sink(2 * i + u // U, u % U))
                        dve.drain()
                    view = S.rearrange("p (c n) -> p c n", c=2)[:, 0:2, :] if C == 2 else \
                        S[:, 0:unit["width"]].rearrange("p (c n) -> p c n", c=1)
                    nc.vector.tensor_reduce(stat[:, u % 2, 0, 0:C], view, AX.X, ALU.max, negate=True)
                    dve.drain()
                    nc.vector.tensor_scalar(stat[:, u % 2, 1, 0:C], stat[:, u % 2, 0, 0:C], scale, None, ALU.mult)\
                        .then_inc(max_ready.sem, 1)

                def diagonals(i, u):
                    dve.wait_ge(exp_done.sem, exp_done.at(i * N + (u + 1)))
                    nc.vector.reciprocal(stat[:, u % 2, 3, 0:C], stat[:, u % 2, 2, 0:C])
                    dve.drain()
                    if C == 2:
                        nc.vector.tensor_tensor(stat[:, u % 2, 3, 1:2], stat[:, u % 2, 3, 1:2], neg_lam, ALU.mult)
                        dve.drain()
                    for c in range(C):
                        last = nc.vector.tensor_scalar(diag[:, u % 2, c, :], con("ident"), stat[:, u % 2, 3, c:c + 1],
                                                       None, ALU.mult)
                    last.then_inc(diag_ready.sem, 1)

                def out_half(i, u):
                    dve.wait_ge(turned[1].sem, turned[1].at(i * N + (u + 1)))
                    lo, hi = halves(u)[1]
                    nc.vector.tensor_copy(probsT[:, u % 2, lo * P:hi * P], turned_cols(1, hi - lo))\
                        .then_inc(probs_out[1].sem, 1)

                def turn_out(i, t):
                    dve.wait_ge(summed.sem, summed.at(2 * i + (t + 1)))
                    dst, src = read_out(2 * i + t, t)
                    nc.vector.tensor_copy(dst, src).then_inc(sum_read.sem, 1)

                nc.vector.memset(stat[:, :, :, :], 0.0).then_inc(sum_read.sem, 2)
                dve.drain()
                with dve.Fori(0, passes) as i:
                    maxima(i, 0)
                    maxima(i, 1)
                    diagonals(i, 0)
                    out_half(i, 0)
                    for u in range(N):
                        if u + 1 < N:
                            diagonals(i, u + 1)
                        if shared_out and u == U:
                            turn_out(i, 0)
                        if u + 2 < N:
                            maxima(i, u + 2)
                        if u + 1 < N:
                            out_half(i, u + 1)
                        if not shared_out and u == U:
                            turn_out(i, 0)
                    turn_out(i, 1)

            def gpsimd(pool):
                for z in zeros:
                    nc.gpsimd.memset(z, 0.0)
                pool.drain()
                with pool.Fori(0, passes) as i:
                    for t in range(2):
                        if passes > 1:
                            pool.wait_ge(sum_read.sem, sum_read.at(2 * i + (t + 1)))
                        for n, (dst, src) in enumerate(copies(2 * i + t, t)):
                            if n:
                                pool.drain()
                            last = nc.gpsimd.tensor_copy(dst, src)
                        last.then_inc(staged.sem, 1)

            stage(name, tensor=tensor, scalar=scalar, vector=vector, gpsimd=gpsimd)

        def ffn(name, at, h, conv_w, conv_b, func, on_first, gated, work):
            per_turn = RING
            turns, rest = divmod(FT, per_turn)
            pair_done = Signal("pair_done", FT)
            center_ready = Signal("center_ready", FT)
            banks_free = Signal("banks_free", FT + per_turn)
            acted = Signal("acted", FT)
            gated_ready = Signal("gated", FT + 2)
            first_slab = at // SLAB

            def pair(j):
                return [bank[:, 2 * (j % 4) + s, :] for s in range(2)]

            def loop(eng, body):
                with eng.Fori(0, turns) as it:
                    for j in range(per_turn):
                        body(it * per_turn + j, j)
                for j in range(rest):
                    body(turns * per_turn + j, j)

            def tensor(pe):
                def products(n, j, slab):
                    out_ap = pair(j)
                    pe.wait_ge(banks_free.sem, banks_free.at(n + 1))
                    for s in range(2):
                        for k in range(KT):
                            last = nc.tensor.matmul(out_ap[s], ring[:, slab % RING, s * KT + k, :], h[:, k, :],
                                                    start=k == 0, stop=k == KT - 1)
                            if s == 0 and k == 0:
                                last.then_inc(slab_begun, 1)
                    last.then_inc(pair_done.sem, 1)

                def turn_of(slab, it):
                    turn = slab // RING + 1 + it
                    return turn if layer[0] is None else layer[0] * (B2_SLABS // RING) + turn

                base = ws.base + first_slab
                assert ws.begun == first_slab and not ws.pending
                with pe.Fori(0, turns) as it:
                    for j in range(per_turn):
                        pe.wait_ge(slab_loaded[(base + j) % RING], turn_of(base + j, it) * 16)
                        products(it * per_turn + j, j, base + j)
                for j in range(rest):
                    pe.wait_ge(slab_loaded[(base + j) % RING], turn_of(base + j, turns) * 16)
                    products(turns * per_turn + j, j, base + j)
                ws.begun += FT

            def scalar(act):
                def centers(n, j):
                    act.wait_ge(pair_done.sem, pair_done.at(n + 1))
                    act.wait_ge(gated_ready.sem, gated_ready.at(n + 1))
                    out_ap = pair(j)
                    for s in range(2):
                        col = n + s * FT
                        last = nc.scalar.activation(work[:, j % 2, s, :], out_ap[s], ACT.Identity,
                                                    bias=conv_b(col), scale=conv_w(2 * FT + col))
                    last.then_inc(center_ready.sem, 1)
                    act.wait_ge(banks_free.sem, banks_free.at(n + (1 + per_turn)))
                    s = 0 if on_first else 1
                    nc.scalar.activation(work[:, j % 2, s, :], work[:, j % 2, s, :], func).then_inc(acted.sem, 1)
                loop(act, centers)

            def vector(dve):
                nc.vector.memset(small[:, 255:256], 0.0).then_inc(banks_free.sem, per_turn)

                def taps(n, j):
                    dve.wait_ge(center_ready.sem, center_ready.at(n + 1))
                    out_ap = pair(j)
                    for lo, tap in ((1, 0), (0, 2)):
                        for s in range(2):
                            col = n + (s * FT + tap * 2 * FT)
                            w = work[:, j % 2, s, lo:lo + T - 1]
                            last = nc.vector.scalar_tensor_tensor(w, out_ap[s][:, 1 - lo:T - lo], conv_w(col), w,
                                                                  ALU.mult, ALU.add)
                        if tap == 0:
                            dve.drain()
                    last.then_inc(banks_free.sem, 1)
                loop(dve, taps)

            def gpsimd(pool):
                def gate(n, j):
                    pool.wait_ge(acted.sem, acted.at(n + 1))
                    nc.gpsimd.tensor_tensor(gated(n), work[:, j % 2, 0, :], work[:, j % 2, 1, :], ALU.mult)\
                        .then_inc(gated_ready.sem, 1)
                nc.gpsimd.memset(small[:, 254:255], 0.0).then_inc(gated_ready.sem, 2)
                loop(pool, gate)

            stage(name, tensor=tensor, scalar=scalar, vector=vector, gpsimd=gpsimd)

        def scan_branch(z, q, v, y, lb, work):
            H = C_HEADS
            DIRS = 2
            o_read = Signal("head_read", H + 1)
            values_staged = Signal("values_staged", H)
            logs_ready = [Signal(f"logs_ready{d}", H) for d in range(DIRS)]
            sums_ready = [Signal(f"sums_ready{d}", H) for d in range(DIRS)]
            keys_exp = [Signal(f"keys_exp{d}", H) for d in range(DIRS)]
            keys_ready = [Signal(f"keys_ready{d}", H) for d in range(DIRS)]
            inter_arg = [Signal(f"inter_arg{d}", H) for d in range(DIRS)]
            inter_exp = [Signal(f"inter_exp{d}", H) for d in range(DIRS)]
            inter_ready = [Signal(f"inter_ready{d}", H) for d in range(DIRS)]
            keys_turned = [Signal(f"keys_turned{d}", H) for d in range(DIRS)]
            keys_out = [Signal(f"keys_out{d}", H) for d in range(DIRS)]
            updates_done = [Signal(f"updates_done{d}", H) for d in range(DIRS)]
            states_ready = [Signal(f"states_ready{d}", H) for d in range(DIRS)]
            arg_ready = [Signal(f"arg_ready{d}", LEVELS * H) for d in range(DIRS)]
            decay_ready = [Signal(f"decay_ready{d}", LEVELS * H) for d in range(DIRS)]
            mixed_ready = [Signal(f"mixed_ready{d}", LEVELS * H) for d in range(DIRS)]
            level_done = [Signal(f"level_done{d}", (LEVELS + 1) * H) for d in range(DIRS)]
            masked_ready = [Signal(f"masked_ready{d}", (LEVELS + 1) * H) for d in range(DIRS)]
            intra_done = [Signal(f"intra_done{d}", (LEVELS + 1 - d) * H) for d in range(DIRS)]
            head_done = Signal("head_done", H)
            order = [list(range(CB + TB)), [1, 0] + list(range(CB + TB - 1, CB - 1, -1))]
            t_half, j_half = [1, 0], [0, 1]
            sums, keys, t1, t2 = (work[n] for n in ("sums", "keys", "t1", "t2"))
            mixed, masked = work["mixed"], work["masked"]
            keys_n, states = work["keys_n"], work["states"]
            NB = CB + TB
            queries, vh, tot = work["queries"], work["vh"], work["tot"]
            qh, lbh = work["qh"], tot[:, 0, 0, NB:NB + 1]
            O = bank[:, 0, :]
            turn_bank = bank[:, 3:5, :].rearrange("p b n -> p (b n)")
            update_bank = bank[:, 5:7, :].rearrange("p b n -> p (b n)")

            def head(ap, i):
                return ap[:, bass.ds(i, 1), :].rearrange("p o n -> p (o n)")

            def zed(i, d):
                return z[:, d, bass.ds(i, 1), :].rearrange("p o n -> p (o n)")

            def lb_col(which, i, d):
                return lb[:, which, bass.ds(i + d * H, 1)]

            def split(ap, m):
                return ap.rearrange("p (b h m) -> p b h m", h=2, m=m)

            def scalar(act):
                nc.scalar.activation(tot[:, 0, 0, 0:1], con("one", 1), ACT.Copy).then_inc(o_read.sem, 1)
                with act.Fori(0, H) as i:
                    act.wait_ge(o_read.sem, o_read.at(i + 1))
                    for d in range(DIRS):
                        nc.scalar.activation(t1[:, d, :], zed(i, d), ACT.Abs)
                        nc.scalar.activation(t2[:, d, :], zed(i, d), ACT.Exp, scale=-1.0)
                        act.drain()
                        nc.scalar.activation(t1[:, d, :], t1[:, d, :], ACT.Exp, scale=-1.0)
                        nc.scalar.activation(t2[:, d, :], t2[:, d, :], ACT.Ln, bias=con("one", 1), scale=lb_col(0, i, d))
                        act.drain()
                        nc.scalar.activation(t1[:, d, :], t1[:, d, :], ACT.Ln, bias=con("one", 1))\
                            .then_inc(logs_ready[d].sem, 1)
                    for d in range(DIRS):
                        act.wait_ge(sums_ready[d].sem, sums_ready[d].at(i + 1))
                        nc.scalar.activation(keys[:, d, :], keys[:, d, :], ACT.Exp, scale=-1.0)\
                            .then_inc(keys_exp[d].sem, 1)
                    for d in range(DIRS):
                        act.wait_ge(inter_arg[d].sem, inter_arg[d].at(i + 1))
                        nc.scalar.activation(t1[:, d, :], t1[:, d, :], ACT.Exp)
                        nc.scalar.activation(tot[:, d, 1, 0:NB], tot[:, d, 0, 0:NB], ACT.Exp)
                        nc.scalar.activation(queries[:, d, :], queries[:, d, :], ACT.Exp).then_inc(inter_exp[d].sem, 1)
                    for d in range(DIRS):
                        act.wait_ge(keys_turned[d].sem, keys_turned[d].at(i + 1))
                        nc.scalar.activation(keys_n[:, d, :, :].rearrange("p b n -> p (b n)"), turn_bank[:, 0:NB * P],
                                             ACT.Copy).then_inc(keys_out[d].sem, 1)
                    for l in range(LEVELS):
                        for d in range(DIRS):
                            act.wait_ge(arg_ready[d].sem, arg_ready[d].at(i * LEVELS + (l + 1)))
                            nc.scalar.activation(mixed[:, d, l % 2, :], mixed[:, d, l % 2, :], ACT.Exp)\
                                .then_inc(decay_ready[d].sem, 1)
                    act.wait_ge(head_done.sem, head_done.at(i + 1))
                    nc.scalar.activation(head(y, i), O, ACT.Copy).then_inc(o_read.sem, 1)

            def direction(eng, ops, d, i, q_head, lb_head):
                near, far = (1, 0) if d == 0 else (0, 1)
                edge = CHUNK - 1 if d == 0 else 0
                lat = sums[:, d, CT:ALLT]

                def inter_args():
                    a = split(sums[:, d, :], CHUNK)
                    tn, tf = a[:, :, near, edge:edge + 1], a[:, :, far, edge:edge + 1]
                    both = tot[:, d, 0, 0:NB].rearrange("p (b o) -> p b o", o=1)
                    ops.tensor_tensor(both, tn, tf, ALU.add)
                    k = split(t1[:, d, :], CHUNK)
                    ops.tensor_tensor(k[:, :, near, :], tn.to_broadcast([P, NB, CHUNK]), a[:, :, near, :], ALU.subtract)
                    qx, al = split(queries[:, d, :], CHUNK), split(lat, CHUNK)
                    ops.tensor_copy(qx[:, :, far, :], al[:, :, far, :])
                    ops.tensor_tensor(qx[:, :, near, :], al[:, :, near, :],
                                      al[:, :, far, edge:edge + 1].to_broadcast([P, TB, CHUNK]), ALU.add)
                    eng.drain()
                    ops.tensor_tensor(k[:, :, far, :], both.to_broadcast([P, NB, CHUNK]), a[:, :, far, :], ALU.subtract)\
                        .then_inc(inter_arg[d].sem, 1)

                def keys_scaled():
                    eng.wait_ge(keys_exp[d].sem, keys_exp[d].at(i + 1))
                    ops.tensor_tensor(keys[:, d, :], keys[:, d, :], lb_head.to_broadcast([P, ALLT]), ALU.mult)\
                        .then_inc(keys_ready[d].sem, 1)
                    eng.drain()

                def inter_products():
                    eng.wait_ge(inter_exp[d].sem, inter_exp[d].at(i + 1))
                    ops.tensor_tensor(t1[:, d, :], t1[:, d, :], keys[:, d, :], ALU.mult)
                    ops.tensor_tensor(queries[:, d, :], queries[:, d, :], q_head, ALU.mult)\
                        .then_inc(inter_ready[d].sem, 1)

                def args(l):
                    m = CHUNK >> l
                    nb = T // (2 * m)
                    if l >= 2:
                        eng.wait_ge(level_done[d].sem, level_done[d].at(i * (LEVELS + 1) + (l - 1)))
                    a, x = split(lat, m), split(mixed[:, d, l % 2, :], m)
                    e = m - 1 if d == 0 else 0
                    ref = a[:, :, j_half[d], e:e + 1].to_broadcast([P, nb, m])
                    ops.tensor_tensor(x[:, :, j_half[d], :], ref, a[:, :, j_half[d], :], ALU.subtract)
                    if l == 0:
                        last = ops.tensor_copy(x[:, :, t_half[d], :], a[:, :, t_half[d], :])
                    else:
                        last = ops.tensor_tensor(x[:, :, t_half[d], :], a[:, :, t_half[d], :], ref, ALU.subtract)
                    last.then_inc(arg_ready[d].sem, 1)

                def products(l):
                    m = CHUNK >> l
                    eng.wait_ge(decay_ready[d].sem, decay_ready[d].at(i * LEVELS + (l + 1)))
                    x = split(mixed[:, d, l % 2, :], m)
                    ops.tensor_tensor(x[:, :, t_half[d], :], x[:, :, t_half[d], :],
                                      split(q_head, m)[:, :, t_half[d], :], ALU.mult)
                    ops.tensor_tensor(x[:, :, j_half[d], :], x[:, :, j_half[d], :],
                                      split(keys[:, d, CT:ALLT], m)[:, :, j_half[d], :], ALU.mult)\
                        .then_inc(mixed_ready[d].sem, 1)
                return inter_args, keys_scaled, inter_products, args, products

            def vector(dve):
                with dve.Fori(0, H) as i:
                    dve.wait_ge(o_read.sem, o_read.at(i + 1))
                    inter_args, keys_scaled, inter_products, args, products = direction(dve, nc.vector, 0, i, head(q, i),
                                                                                       lb_col(1, i, 0))
                    for d in range(DIRS):
                        dve.wait_ge(logs_ready[d].sem, logs_ready[d].at(i + 1))
                        nc.vector.scalar_tensor_tensor(keys[:, d, :], zed(i, d), 0.0, t1[:, d, :], ALU.max, ALU.add)
                        dve.drain()
                        nc.vector.scalar_tensor_tensor(t1[:, d, :], zed(i, d), 0.0, t1[:, d, :], ALU.min, ALU.subtract)
                        dve.drain()
                        nc.vector.tensor_tensor(t2[:, d, :], t1[:, d, :], t2[:, d, :], ALU.add)
                        dve.drain()
                        step = 1 if d == 0 else -1
                        nc.vector.tensor_tensor_scan(sums[:, d, ::step], con("reset", ALLT, d * ALLT)[:, ::step],
                                                     t2[:, d, ::step], 0.0, ALU.mult, ALU.add)\
                            .then_inc(sums_ready[d].sem, 1)
                    dve.drain()
                    inter_args()
                    args(0)
                    args(1)
                    keys_scaled()
                    inter_products()
                    for d in range(DIRS):
                        dve.wait_ge(updates_done[d].sem, updates_done[d].at(i + 1))
                        U = update_bank
                        first = order[d][0]
                        nc.vector.tensor_copy(states[:, d, 1, :], U[:, first * P:(first + 1) * P])
                        for n in range(1, NB - 1):
                            b = order[d][n]
                            dve.drain()
                            last = nc.vector.scalar_tensor_tensor(states[:, d, n + 1, :], states[:, d, n, :],
                                                                  tot[:, d, 1, b:b + 1], U[:, b * P:(b + 1) * P],
                                                                  ALU.mult, ALU.add)
                        last.then_inc(states_ready[d].sem, 1)

                    def masks(l):
                        for d in range(DIRS):
                            dve.wait_ge(level_done[d].sem, level_done[d].at(i * (LEVELS + 1) + (l + 1)))
                            if l >= 2:
                                dve.wait_ge(intra_done[d].sem, intra_done[d].at(i * (LEVELS + 1 - d) + (l - 1)))
                            mask = con("levels", P, (d * (LEVELS + 1) + l) * P).rearrange("p (o n) -> p o n", o=1)
                            nc.vector.tensor_tensor(masked[:, d, l % 2, :].rearrange("p (b n) -> p b n", n=P),
                                                    bank[:, 1 + d, :].rearrange("p (b n) -> p b n", n=P),
                                                    mask.to_broadcast([P, TB, P]), ALU.mult)\
                                .then_inc(masked_ready[d].sem, 1)
                    for l in range(LEVELS):
                        products(l)
                        if l >= 1:
                            masks(l - 1)
                        if l + 2 < LEVELS:
                            args(l + 2)
                    masks(LEVELS - 1)
                    masks(LEVELS)

            def gpsimd(pool):
                with pool.Fori(0, H) as i:
                    pool.wait_ge(o_read.sem, o_read.at(i + 1))
                    inter_args, keys_scaled, inter_products, args, products = direction(pool, nc.gpsimd, 1, i, qh, lbh)
                    nc.gpsimd.tensor_copy(vh[:, :, :], v[:, :, bass.ds(i, 1), :].rearrange("p b o n -> p b (o n)"))\
                        .then_inc(values_staged.sem, 1)
                    nc.gpsimd.tensor_copy(qh, head(q, i))
                    nc.gpsimd.tensor_copy(lbh, lb_col(1, i, 1))
                    pool.drain()
                    pool.wait_ge(sums_ready[1].sem, sums_ready[1].at(i + 1))
                    inter_args()
                    args(0)
                    args(1)
                    keys_scaled()
                    inter_products()
                    for l in range(LEVELS):
                        products(l)
                        if l + 2 < LEVELS:
                            args(l + 2)

            def tensor(pe):
                with pe.Fori(0, H) as i:
                    pe.wait_ge(o_read.sem, o_read.at(i + 1))
                    pe.wait_ge(values_staged.sem, values_staged.at(i + 1))
                    for d in range(DIRS):
                        pe.wait_ge(inter_ready[d].sem, inter_ready[d].at(i + 1))
                        if d == 1:
                            pe.wait_ge(keys_out[0].sem, keys_out[0].at(i + 1))
                        for b in range(NB):
                            last = nc.tensor.transpose(turn_bank[:, b * P:(b + 1) * P], t1[:, d, b * P:(b + 1) * P],
                                                       con("ident"))
                        last.then_inc(keys_turned[d].sem, 1)
                    for d in range(DIRS):
                        pe.wait_ge(keys_out[d].sem, keys_out[d].at(i + 1))
                        if d == 1:
                            pe.wait_ge(states_ready[0].sem, states_ready[0].at(i + 1))
                        for b in order[d][0:NB - 1]:
                            last = nc.tensor.matmul(update_bank[:, b * P:(b + 1) * P], keys_n[:, d, b, :], vh[:, b, :],
                                                    start=True, stop=True)
                        last.then_inc(updates_done[d].sem, 1)
                    for d in range(DIRS):
                        pe.wait_ge(states_ready[d].sem, states_ready[d].at(i + 1))
                        for n in range(CB, NB):
                            b = order[d][n] - CB
                            nc.tensor.matmul(O[:, b * P:(b + 1) * P], states[:, d, n, :], queries[:, d, b * P:(b + 1) * P],
                                             start=d == 0 and n == CB, stop=False, skip_group_check=True)

                    def level(l):
                        for d in range(DIRS):
                            if l >= 1:
                                pe.wait_ge(masked_ready[d].sem, masked_ready[d].at(i * (LEVELS + 1) + l))
                            if l < LEVELS:
                                pe.wait_ge(mixed_ready[d].sem, mixed_ready[d].at(i * LEVELS + (l + 1)))
                            else:
                                pe.wait_ge(keys_ready[d].sem, keys_ready[d].at(i + 1))
                            for b in range(TB):
                                c = slice(b * P, (b + 1) * P)
                                if l < LEVELS:
                                    lhsT = rhs = mixed[:, d, l % 2, c]
                                else:
                                    lhsT = keys[:, d, CT + b * P:CT + (b + 1) * P]
                                    rhs = q[:, bass.ds(i, 1), c].rearrange("p o n -> p (o n)")
                                last = nc.tensor.matmul(bank[:, 1 + d, c], lhsT, rhs, start=True, stop=True)
                            last.then_inc(level_done[d].sem, 1)

                    def intra(l):
                        for d in range(DIRS):
                            pe.wait_ge(masked_ready[d].sem, masked_ready[d].at(i * (LEVELS + 1) + (l + 1)))
                            for b in range(TB):
                                c = slice(b * P, (b + 1) * P)
                                end = l == LEVELS and d == 1 and b == TB - 1
                                last = nc.tensor.matmul(O[:, c], vh[:, CB + b, :], masked[:, d, l % 2, c], start=False,
                                                        stop=end, skip_group_check=True)
                            last.then_inc((head_done if end else intra_done[d]).sem, 1)
                    level(0)
                    for l in range(LEVELS):
                        level(l + 1)
                        intra(l)
                    intra(LEVELS)

            stage("scan", tensor=tensor, scalar=scalar, vector=vector, gpsimd=gpsimd)

        inputs_loaded = Signal("inputs_loaded", 16 * 4)
        tables = sb("tables", [P, 4, T])
        COS_MLA, SIN_MLA, COS_DIFF, SIN_DIFF = (tables[:, n, :] for n in range(4))

        phase = stack.enter_context(ExitStack())

        def tmp(name, shape, where=None, dt=F32):
            return (where or phase).enter_context(nc.sbuf_tensor(name, shape, dt))

        ys = tmp("ys", [P, 3, 4, T])
        mod = tmp("mod", [P, MOD_TILES, 2])
        gain_x = tmp("gain_x", [P, KT, 2])
        gain_f = tmp("gain_f", [P, KT])
        sc = tmp("sc", [P, KT, 2])
        lb = tmp("lb", [P, 2, 2 * C_HEADS])
        sink8 = tmp("sink8", [P, 8])

        with ExitStack() as here:
            pos_i = tmp("pos_i", [P, T], here, I32)
            ang = tmp("ang", [P, 4, T], here)
            scr = tmp("scr", [P, 4, 2 * C_HEADS], here)
            c_ready = Signal("c_ready", 1)
            mod_done = Signal("mod_done", 1)
            lb_sub = Signal("lb_sub", 1)
            lb_exp = Signal("lb_exp", 1)
            angles_ready = Signal("angles_ready", 1)
            abs_ready = Signal("abs_ready", 1)
            mod_ready = Signal("mod_ready", 1)

            def sync(sp):
                sp.dma_start(par1[:, :], par1_in).then_inc(inputs_loaded.sem, 16)
                ws.feed(sp, RING)
                sp.dma_start(const[:, :], const_in).then_inc(inputs_loaded.sem, 16)
                sp.dma_start(xT[:, :, :], xT_in).then_inc(inputs_loaded.sem, 16)
                sp.dma_start(pos_i[:, :], pos_in.to_broadcast([P, T])).then_inc(inputs_loaded.sem, 16)

            def scalar(act):
                act.wait_ge(inputs_loaded.sem, 16 * 4)
                nc.scalar.activation(sc[:, :, :].rearrange("p k s -> p (k s)"), p1("c", 2 * KT), ACT.Silu)\
                    .then_inc(c_ready.sem, 1)
                act.wait_ge(lb_sub.sem, lb_sub.at(1))
                nc.scalar.activation(scr[:, 1, :], scr[:, 0, :], ACT.Exp).then_inc(lb_exp.sem, 1)
                act.wait_ge(angles_ready.sem, angles_ready.at(1))
                for n in range(2):
                    nc.scalar.activation(ang[:, 2 + n, :], ang[:, n, :], ACT.Abs)
                act.drain()
                for n in range(2):
                    nc.scalar.activation(tables[:, 2 * n + 1, :], ang[:, n, :], ACT.Sin)
                    nc.scalar.activation(tables[:, 2 * n, :], ang[:, 2 + n, :], ACT.Sin, bias=con("half_pi", 1), scale=-1.0)
                act.drain()

            def tensor(pe):
                pe.wait_ge(c_ready.sem, c_ready.at(1))
                for n in range(MOD_TILES):
                    for k in range(KT):
                        b = B1_AT["mod"] + n * KT + k
                        last = ws.mm(pe, b, bank[:, 0, 2 * n:2 * n + 2], ws.block(b), sc[:, k, :], k == 0, k == KT - 1)
                last.then_inc(mod_done.sem, 1)

            def vector(dve):
                dve.wait_ge(inputs_loaded.sem, 16 * 4)
                nc.vector.tensor_tensor(scr[:, 0, :], p1("lb", 8), p1("lb", 8), ALU.subtract).then_inc(lb_sub.sem, 1)
                nc.vector.tensor_scalar(sink8[:, :], p1("sink", 8), float(HD) ** 0.5, None, ALU.mult)
                nc.vector.tensor_copy(ang[:, 3, :], pos_i[:, :])
                dve.drain()
                two_pi = 2 * np.pi
                parts, left = [], two_pi
                for bits in (7, 15):
                    part = np.floor(left * 2.0 ** bits) / 2.0 ** bits
                    parts.append(float(np.float32(part)))
                    left -= parts[-1]
                parts.append(float(np.float32(left)))
                magic = 1.5 * 2.0 ** 23
                for n in (0, 1):
                    a, r = ang[:, n, :], ang[:, 2, :]
                    nc.vector.tensor_scalar(a, ang[:, 3, :], con("freq", 1, n), None, ALU.mult)
                    dve.drain()
                    nc.vector.tensor_scalar(r, a, 1.0 / two_pi, magic, ALU.mult, ALU.add)
                    dve.drain()
                    nc.vector.tensor_scalar(r, r, magic, None, ALU.subtract)
                    dve.drain()
                    for part in parts:
                        nc.vector.scalar_tensor_tensor(a, r, -part, a, ALU.mult, ALU.add)
                        dve.drain()
                    last = nc.vector.tensor_scalar(a, a, -3.1415925, 3.1415925, ALU.max, ALU.min)
                    dve.drain()
                nc.vector.tensor_copy(ang[:, 2, 0:1], ang[:, 0, 0:1]).then_inc(angles_ready.sem, 1)
                dve.wait_ge(lb_exp.sem, lb_exp.at(1))
                nc.vector.reciprocal(scr[:, 2, :], scr[:, 1, :])
                dve.drain()
                nc.vector.tensor_tensor(scr[:, 1, :], scr[:, 1, :], scr[:, 2, :], ALU.mult)
                dve.drain()
                nc.vector.tensor_tensor(scr[:, 2, :], scr[:, 1, :], scr[:, 1, :], ALU.subtract)
                dve.drain()
                nc.vector.tensor_scalar(lb[:, 0, :], scr[:, 2, :], 0.0, 1.0, ALU.max, ALU.min)
                dve.drain()
                nc.vector.tensor_scalar(lb[:, 1, :], lb[:, 0, :], -1.0, 1.0, ALU.mult, ALU.add)
                dve.wait_ge(mod_done.sem, mod_done.at(1))
                nc.vector.tensor_tensor(mod[:, :, :], bank[:, 0, 0:2 * MOD_TILES].rearrange("p (n s) -> p n s", s=2),
                                        bcast(p1("b_mod", MOD_TILES), 2), ALU.add)
                dve.drain()
                nc.vector.scalar_tensor_tensor(gain_x[:, :, :], mod[:, KT:2 * KT, :], 1.0, bcast(p1("norm_mix", KT), 2),
                                               ALU.add, ALU.mult)
                nc.vector.scalar_tensor_tensor(gain_f[:, :], mod[:, 4 * KT:5 * KT, 0], 1.0, p1("norm_ffn", KT),
                                               ALU.add, ALU.mult).then_inc(mod_ready.sem, 1)

            stage("modulation", tensor=tensor, scalar=scalar, vector=vector, sync=sync)

        with ExitStack() as here:
            hcT = tmp("hcT", [P, KT, CT], here)
            with ExitStack() as norm_scope:
                ctxT = tmp("ctxT", [P, KT, CT], norm_scope)
                squares = tmp("squares1", [P, 8, T], norm_scope)
                scales = tmp("scales1", [P, 2, T], norm_scope)
                ctx_in = Signal("context_loaded", 16)

                def sync(sp):
                    sp.dma_start(ctxT[:, :, :], ctxT_in).then_inc(ctx_in.sem, 16)
                    sp.wait_ge(ctx_in.sem, ctx_in.at(16))
                stage("load_context", sync=sync)
                norms("norm_mix", [
                    dict(src=lambda k: xT[:, k, :], tiles=KT, cols=T, ones=con("ones"), inv=1.0 / D,
                         gain=lambda k: gain_x[:, k, 0:1], out=lambda k: hT[:, k, :],
                         end=("shift", lambda k: mod[:, k, 0:1])),
                    dict(src=lambda k: ctxT[:, k, :], tiles=KT, cols=CT, ones=con("ones"), inv=1.0 / D,
                         gain=lambda k: gain_x[:, k, 1:2], out=lambda k: hcT[:, k, :],
                         end=("shift", lambda k: mod[:, k, 1:2]))], squares, scales)

            def tokens(k, tb):
                return hcT[:, k, tb * P:(tb + 1) * P] if tb < CB else hT[:, k, (tb - CB) * P:(tb - CB + 1) * P]

            def attend(which, b, windowed):
                at = B1_AT[which]
                with ExitStack() as s:
                    qk = tmp(f"qk{which}", [P, 4, T], s)
                    k = tmp(f"k{which}", [P, ALLT], s)
                    v = tmp(f"v{which}", [P, CB + TB, P], s)
                    tiles = [("act", T, weights_still(at + n * KT, KT, lambda kt: hT[:, kt, :]), act_copy(qk[:, n, :]))
                             for n in range(4)]
                    tiles.append(("act", T, weights_still(at + 4 * KT, KT, lambda kt: hT[:, kt, :]), act_copy(k[:, CT:ALLT])))
                    tiles.append(("act", CT, weights_still(at + 4 * KT, KT, lambda kt: hcT[:, kt, :]), act_copy(k[:, 0:CT])))
                    for tb in range(CB + TB):
                        tiles.append(("dve", P, weights_moving(at + 5 * KT, KT, 1, lambda kt, tb=tb: tokens(kt, tb)),
                                      dve_copy(v[:, tb, :])))
                    linear(f"proj{which}", tiles)
                    if not windowed:
                        with ExitStack() as n:
                            squares = tmp("squaresB", [P, 8, T], n)
                            scales = tmp("scalesB", [P, 2, T], n)
                            jobs = [(qk[:, m, :], T, "qn") for m in range(4)] + \
                                [(k[:, CT:ALLT], T, "kn"), (k[:, 0:CT], CT, "kn")]
                            norms("norm_heads", [
                                dict(src=lambda kt, ap=ap: ap, tiles=1, cols=cols, ones=con("ones64"), inv=1.0 / HD,
                                     gain=lambda kt, g=g: p1(g), out=lambda kt, ap=ap: ap, end=None)
                                for ap, cols, g in jobs], squares, scales)
                    with ExitStack() as r:
                        work = tmp(f"rope{which}", [P, 4, T], r)
                        rope(f"rope{which}", [(ap, con("rot1"), con("cos1", T), con("sin1", T), ap)
                                              for ap in [qk[:, m, :] for m in range(4)] + [k[:, CT:ALLT]]], work)
                    with ExitStack() as a:
                        qpad = tmp(f"qpad{which}", [P, 2, 2, T], a)
                        work = (tmp(f"probs{which}", [P, 2, 1024], a), tmp(f"probsT{which}", [P, 2, ALLT], a),
                                tmp(f"diag{which}", [P, 2, 1, P], a), tmp(f"stat{which}", [P, 2, 4, 2], a))
                        units = [[], []]
                        for t, g in ((t, g) for t in range(2) for g in range(2)):
                            for tb in range(TB):
                                lo, hi = (max(0, tb - 1), min(TB, tb + 2)) if windowed else (0, TB)
                                width = CT + (hi - lo) * P
                                key_cols = [(0, CT, 0), (CT, min(width, 512), CT + lo * P)]
                                if width > 512:
                                    key_cols.append((512, width, 512 + lo * P))
                                qs = qpad[:, t, g, tb * P:(tb + 1) * P]
                                masks = []
                                if windowed and lo < tb:
                                    masks.append((CT, con("mask_prev")))
                                if windowed and hi > tb + 1:
                                    masks.append((width - P, con("mask_next")))
                                blocks = list(range(CB)) + [CB + x for x in range(lo, hi)]
                                units[t].append(dict(
                                    scores=[lambda i, qs=qs, kc=key_cols: [(a0, a1, [(qs, k[:, s0:s0 + a1 - a0])])
                                                                           for a0, a1, s0 in kc]],
                                    width=width + (1 if windowed else 0), masks=masks,
                                    sink=width if windowed else None, group=g, keys=width // P,
                                    values=[(bank[g * HD:(g + 1) * HD, 6 + t, tb * P:(tb + 1) * P],
                                             [v[:, x, g * HD:(g + 1) * HD] for x in blocks])]))

                        def copies(i, t):
                            return [(qpad[g * HD:(g + 1) * HD, t, g, :],
                                     qk[g * HD:(g + 1) * HD, bass.ds(i, 1), :].rearrange("p o n -> p (o n)"))
                                    for g in range(2)]
                        attention(f"attend{which}", 4, units, HD ** -0.5, copies,
                                  [qpad[HD:P, :, 0, :], qpad[0:HD, :, 1, :]],
                                  lambda i, t: (ys[:, b, bass.ds(i, 1), :].rearrange("p o n -> p (o n)"), bank[:, 6 + t, :]),
                                  work, sink=lambda i, u: sink8[:, bass.ds(i + 4 * units[0][u]["group"], 1)])

            if upto >= 2:
                attend("A", 0, True)
            if upto >= 3:
                attend("B", 1, False)

            if upto >= 4:
                z = tmp("z", [P, 2, C_HEADS, ALLT], here)
                cq = tmp("cq", [P, C_HEADS, T], here)
                v = tmp("vC", [P, CB + TB, C_HEADS, P], here)
                at = B1_AT["C"]
                tiles = [("act", T, weights_still(at + h * KT, KT, lambda kt: hT[:, kt, :]), act_copy(cq[:, h, :], ACT.Silu))
                         for h in range(C_HEADS)]
                for d in range(2):
                    for h in range(C_HEADS):
                        b = at + (4 + 4 * d + h) * KT
                        tiles.append(("act", T, weights_still(b, KT, lambda kt: hT[:, kt, :]), act_copy(z[:, d, h, CT:ALLT])))
                        tiles.append(("act", CT, weights_still(b, KT, lambda kt: hcT[:, kt, :]), act_copy(z[:, d, h, 0:CT])))
                group = value_group(at + 12 * KT, KT, 4, [lambda kt, tb=tb: tokens(kt, tb) for tb in range(CB + TB)])
                for tb in range(CB + TB):
                    tiles.append(("dve", 512, group, dve_copy(v[:, tb, :, :].rearrange("p h n -> p (h n)"))))
                linear("projC", tiles)
                with ExitStack() as s:
                    work = {n: tmp(f"scan_{n}", [P, 2, ALLT], s) for n in ("sums", "keys", "t1", "t2")}
                    work["states"] = tmp("scan_states", [P, 2, CB + TB, P], s)
                    work["vh"] = tmp("scan_vh", [P, CB + TB, P], s)
                    work["qh"] = hcT[:, 6:8, :].rearrange("p k c -> p (k c)")
                    work["tot"] = tmp("scan_tot", [P, 2, 2, 8], s)
                    work["mixed"] = xT[:, 0:KT // 2, :].rearrange("p (d n) t -> p d n t", d=2)
                    work["masked"] = xT[:, KT // 2:KT, :].rearrange("p (d n) t -> p d n t", d=2)
                    work["keys_n"] = hcT[:, 0:6, :].rearrange("p (d k) c -> p d (k c)", d=2)\
                        .rearrange("p d (b n) -> p d b n", n=P)
                    work["queries"] = work["t2"][:, :, 0:T]
                    scan_branch(z, cq, v, ys[:, 2, :, :], lb, work)

        if upto >= 5:
            with ExitStack() as here:
                cg = tmp("cg", [P, C_HEADS, T], here)
                at = B1_AT["cg"]
                x_again = Signal("x_loaded", 16)

                def load_x(sp):
                    sp.dma_start(xT[:, :, :], xT_in).then_inc(x_again.sem, 16)
                    sp.wait_ge(x_again.sem, x_again.at(16))
                linear("gate_c", [("act", T, weights_still(at + h * KT, KT, lambda kt: hT[:, kt, :]),
                                   act_copy(cg[:, h, :], ACT.Silu)) for h in range(C_HEADS)],
                       sync=load_x)
                squares = tmp("squaresC", [P, 8, T], here)
                scales = tmp("scalesC", [P, 2, T], here)
                norms("norm_c", [dict(src=lambda k, h=h: ys[:, 2, h, :], tiles=1, cols=T, ones=con("ones"), inv=1.0 / P,
                                      gain=lambda k: p1("gn"), out=lambda k, h=h: ys[:, 2, h, :],
                                      end=("times", lambda k, h=h: cg[:, h, :])) for h in range(C_HEADS)],
                      squares, scales)
        if upto >= 6:
            with ExitStack() as here:
                merged = tmp("merged", [P, KT, T], here)
                gates = tmp("gates", [P, 6, T], here)
                part = tmp("part", [P, 2, T], here)
                tiles = []

                def add_branch(n, b):
                    def read_out(dve, ps):
                        g = gates[:, (3 * n + b) % 6, :]
                        if b == 0:
                            return nc.vector.tensor_tensor(merged[:, n, :], ps, g, ALU.mult)
                        nc.vector.tensor_tensor(part[:, b % 2, :], ps, g, ALU.mult)
                        dve.drain()
                        return nc.vector.tensor_tensor(merged[:, n, :], merged[:, n, :], part[:, b % 2, :], ALU.add)
                    return read_out
                for n in range(KT):
                    for b in range(3):
                        at = B1_AT["merge"] + (3 * n + b) * (KT + 4)
                        tiles.append(("act", T, weights_still(at, KT, lambda kt: hT[:, kt, :]),
                                      act_copy(gates[:, (3 * n + b) % 6, :], ACT.Sigmoid)))
                        tiles.append(("dve", T, weights_still(at + KT, 4, lambda kt, b=b: ys[:, b, kt, :]),
                                      add_branch(n, b), len(tiles) - 1))
                linear("merge", tiles)

                def residual(n):
                    return lambda dve, ps: nc.vector.scalar_tensor_tensor(xT[:, n, :], ps, mod[:, 2 * KT + n, 0:1],
                                                                          xT[:, n, :], ALU.mult, ALU.add)
                linear("out", [("dve", T, weights_still(B1_AT["out"] + n * KT, KT, lambda kt: merged[:, kt, :]), residual(n))
                               for n in range(KT)])

        def up_down(which, at, func, on_first, conv_w, conv_b, down_out, work=None):
            with ExitStack() as here:
                gated = tmp(f"gated{which}", [P, FT, T], here)
                if work is None:
                    work = tmp(f"conv{which}", [P, 2, 2, T], here)
                ffn(f"up{which}", at["up"], hT, conv_w, conv_b, func, on_first,
                    lambda n: gated[:, bass.ds(n, 1), :].rearrange("p o n -> p (o n)") if not isinstance(n, int)
                    else gated[:, n, :], work)
                linear(f"down{which}", [("dve", T, weights_still(at["down"] + n * FT, FT, lambda kt: gated[:, kt, :]),
                                         down_out(n)) for n in range(KT)])

        def col(table, start):
            return lambda n: table[:, bass.ds(n + start, 1)] if not isinstance(n, int) else table[:, n + start:n + start + 1]

        if upto >= 7:
            with ExitStack() as here:
                squares = tmp("squaresF", [P, 8, T], here)
                scales = tmp("scalesF", [P, 2, T], here)
                norms("norm_ffn", [dict(src=lambda k: xT[:, k, :], tiles=KT, cols=T, ones=con("ones"), inv=1.0 / D,
                                        gain=lambda k: gain_f[:, k:k + 1], out=lambda k: hT[:, k, :],
                                        end=("shift", lambda k: mod[:, 3 * KT + k, 0:1]))], squares, scales)
            up_down("1", B1_AT, ACT.Silu, False, col(par1, PAR1["conv_w"]), col(par1, PAR1["conv_b"]),
                    lambda n: lambda dve, ps: nc.vector.scalar_tensor_tensor(
                        xT[:, n, :], ps, mod[:, 5 * KT + n, 0:1], xT[:, n, :], ALU.mult, ALU.add))
        phase.close()

        phase = stack.enter_context(ExitStack())
        par2 = tmp("par2", [P, PAR2_W], phase)
        memT = tmp("memT", [P, KT, MEM], phase)
        mix = tmp("mix", [P, KT, T], phase)
        raw = tmp("raw", [P, KT, T], phase)
        squares2 = tmp("squares2", [P, 8, T], phase)
        scales2 = tmp("scales2", [P, 2, T], phase)
        lam = tmp("lam", [P, 2, 32], phase)
        lam_s = tmp("lam_s", [P, 8], phase)

        def p2(name, n=1, at=0):
            return par2[:, PAR2[name] + at:PAR2[name] + at + n]

        def one_norm(name, src, gain, out, tiles=KT, cols=T, ones="ones", width=D, end=None):
            return dict(src=src, tiles=tiles, cols=cols, ones=con(ones), inv=1.0 / width, gain=gain, out=out, end=end)

        memory_loaded = Signal("memory_loaded", 16)

        def load_memory(sp):
            sp.dma_start(memT[:, :, :], memT_in).then_inc(memory_loaded.sem, 16)
            sp.wait_ge(memory_loaded.sem, memory_loaded.at(16))
        if upto >= 7:
            norms("norm_final", [one_norm("x", lambda k: xT[:, k, :], lambda k: p1("norm_final", 1, k),
                                          lambda k: xT[:, k, :])], squares2, scales2, load_memory)

        def layer_body(l):
            params_loaded = Signal("params_loaded", 16)
            lam_dots = Signal("lam_dots", 1)
            lam_exp = Signal("lam_exp", 1)
            neg_lam, gain_sub = lam_s[:, 4:5], lam_s[:, 5:6]

            def sync(sp):
                sp.dma_start(par2[:, :], par2_in[bass.ds(l, 1)].rearrange("o p n -> p (o n)")).then_inc(params_loaded.sem, 16)

            def vector(dve):
                dve.wait_ge(params_loaded.sem, params_loaded.at(16))
                v = p2("lam", 128).rearrange("p (a s n) -> p a s n", a=2, s=2)
                nc.vector.tensor_tensor(lam[:, :, :], v[:, :, 0, :], v[:, :, 1, :], ALU.mult)
                nc.vector.tensor_tensor(gain_sub, p2("sub_g"), p2("one_less_lam"), ALU.mult)
                dve.drain()
                nc.vector.tensor_reduce(lam_s[:, 0:2], lam[:, :, :], AX.X, ALU.add).then_inc(lam_dots.sem, 1)
                dve.wait_ge(lam_exp.sem, lam_exp.at(1))
                nc.vector.tensor_tensor(lam_s[:, 2:3], lam_s[:, 1:2], lam_s[:, 0:1], ALU.subtract)
                dve.drain()
                nc.vector.tensor_tensor(neg_lam, lam_s[:, 2:3], p2("lam_init"), ALU.subtract)

            def scalar(act):
                act.wait_ge(lam_dots.sem, lam_dots.at(1))
                nc.scalar.activation(lam_s[:, 0:2], lam_s[:, 0:2], ACT.Exp).then_inc(lam_exp.sem, 1)
            stage("layer_params", scalar=scalar, vector=vector, sync=sync)

            norms("mix_pre", [one_norm("x", lambda k: xT[:, k, :], lambda k: p2("mix_pre", 1, k), lambda k: hT[:, k, :])],
                  squares2, scales2)
            with ExitStack() as here:
                q = tmp("q2", [P, 8, T], here)
                k = hT
                v = tmp("v2", [P, TB, 4, P], here)
                dq = tmp("dq", [P, 2, T], here)
                dk = tmp("dk", [P, 2, T], here)
                dv = tmp("dv", [P, TB, 2, P], here)
                with ExitStack() as s:
                    low, u = raw[:, 0:6, :], raw[:, 6:8, :]
                    zv = tmp("zv", [P, TB, 256], s)
                    at = B2_AT["in"]
                    dsts = [(low[:, n, :], ACT.Copy) for n in range(6)] + [(u[:, n, :], ACT.Gelu_apprx_tanh) for n in range(2)] + \
                        [(dq[:, n, :], ACT.Copy) for n in range(2)] + [(dk[:, n, :], ACT.Copy) for n in range(2)]
                    tiles = [("act", T, weights_still(at + n * KT, KT, lambda kt: hT[:, kt, :]), act_copy(dst, f))
                             for n, (dst, f) in enumerate(dsts)]
                    for tb in range(TB):
                        tiles.append(("act", 256, weights_moving(at + 12 * KT, KT, 2, lambda kt, tb=tb: hT[:, kt, tb * P:(tb + 1) * P]),
                                      act_copy(zv[:, tb, :], ACT.Gelu_apprx_tanh)))
                    for tb in range(TB):
                        tiles.append(("dve", 256, weights_moving(at + 14 * KT, KT, 2, lambda kt, tb=tb: hT[:, kt, tb * P:(tb + 1) * P]),
                                      dve_copy(dv[:, tb, :, :].rearrange("p h n -> p (h n)"))))
                    linear("in2", tiles)
                    norms("latent", [
                        one_norm("cq", lambda t: low[:, t, :], lambda t: p2("cq_g", 1, t), lambda t: low[:, t, :], 3, T, "ones", 384),
                        one_norm("ckv", lambda t: low[:, 3 + t, :], lambda t: p2("ckv_g", 1, t), lambda t: low[:, 3 + t, :], 2, T,
                                 "ones", 256)], squares2, scales2)
                    rope("rope_keys", [(low[:, 5, :], con("rot_mla"), COS_MLA, SIN_MLA, low[:, 5, :])] +
                         [(x[:, n, :], con("rot_diff"), COS_DIFF, SIN_DIFF, x[:, n, :]) for x in (dq, dk) for n in range(2)],
                         squares2[:, 0:4, :])

                    tiles = [("act", T, weights_still(B2_AT["uq"] + 3 * h, 3, lambda t: low[:, t, :]), act_copy(q[:, h, :]))
                             for h in range(8)]

                    def add_rope_key(h):
                        return lambda dve, ps: nc.vector.tensor_tensor(k[:, h, :], ps, low[:, 5, :], ALU.add)
                    tiles += [("dve", T, weights_still(B2_AT["uk"] + 2 * h, 2, lambda t: low[:, 3 + t, :]), add_rope_key(h))
                              for h in range(8)]
                    tiles += [("act", 512, weights_moving(B2_AT["uv"], 2, 4, lambda t, tb=tb: low[:, 3 + t, tb * P:(tb + 1) * P]),
                               act_copy(v[:, tb, :, :].rearrange("p h n -> p (h n)"))) for tb in range(TB)]
                    linear("up_latent", tiles)
                    rope("rope_queries", [(q[:, h, :], con("rot_mla"), COS_MLA, SIN_MLA, q[:, h, :]) for h in range(8)],
                         squares2[:, 0:4, :])

                    G = 16
                    st = tmp("sgu_stat", [P, 4, G], s)
                    xc = squares2[:, 0:2, :].rearrange("p b n -> p (b n)").rearrange("p (g n) -> p g n", g=G)
                    sq = squares2[:, 2:4, :].rearrange("p b n -> p (b n)").rearrange("p (g n) -> p g n", g=G)
                    centered = Signal("centered", 1)
                    sq_ready = Signal("sgu_square_ready", 1)
                    var_ready = Signal("var_ready", 1)
                    rstd_ready = Signal("rstd_ready", 1)
                    gate_ready = Signal("gate_ready", 1)
                    chunks_mixed = Signal("chunks_mixed", 1)

                    def sgu_tensor(pe):
                        pe.wait_ge(gate_ready.sem, gate_ready.at(1))
                        for tb in range(TB):
                            for g in range(4):
                                last = nc.tensor.matmul(bank[(g % 2) * 64:(g % 2) * 64 + 64, g // 2, tb * P:(tb + 1) * P],
                                                        zv[:, tb, g * 64:(g + 1) * 64], p2("sgu_w", P, g * P),
                                                        start=True, stop=True)
                        last.then_inc(chunks_mixed.sem, 1)

                    def per_group(n):
                        return st[:, n, :].rearrange("p (g o) -> p g o", o=1).to_broadcast([P, G, 64])

                    def sgu_vector(dve):
                        z3 = zv[:, :, :].rearrange("p b (g n) -> p (b g) n", n=64)
                        nc.vector.tensor_reduce(st[:, 0, :], z3, AX.X, ALU.add)
                        dve.drain()
                        nc.vector.tensor_scalar(st[:, 1, :], st[:, 0, :], 1.0 / 64, None, ALU.mult)
                        dve.drain()
                        nc.vector.tensor_tensor(xc, z3, per_group(1), ALU.subtract).then_inc(centered.sem, 1)
                        dve.wait_ge(sq_ready.sem, sq_ready.at(1))
                        nc.vector.tensor_reduce(st[:, 2, :], sq, AX.X, ALU.add).then_inc(var_ready.sem, 1)
                        dve.wait_ge(rstd_ready.sem, rstd_ready.at(1))
                        nc.vector.tensor_tensor(xc, xc, per_group(3), ALU.mult)
                        dve.drain()
                        gains = p2("sgu_g", 256).rearrange("p (o n) -> p o n", o=1).to_broadcast([P, TB, 256])
                        nc.vector.tensor_tensor(zv[:, :, :], xc.rearrange("p (b g) n -> p b (g n)", b=TB), gains, ALU.mult)\
                            .then_inc(gate_ready.sem, 1)
                        dve.wait_ge(chunks_mixed.sem, chunks_mixed.at(1))
                        for n in range(2):
                            y = mix[:, 4 + n, :]
                            b = p2("sgu_b", P, n * P).rearrange("p (o n) -> p o n", o=1).to_broadcast([P, TB, P])
                            nc.vector.tensor_tensor(y.rearrange("p (b n) -> p b n", b=TB),
                                                    bank[:, n, :].rearrange("p (b n) -> p b n", b=TB), b, ALU.add)
                            dve.drain()
                            nc.vector.tensor_tensor(y, y, u[:, n, :], ALU.mult)

                    def sgu_scalar(act):
                        act.wait_ge(centered.sem, centered.at(1))
                        nc.scalar.activation(sq, xc, ACT.Square).then_inc(sq_ready.sem, 1)
                        act.wait_ge(var_ready.sem, var_ready.at(1))
                        nc.scalar.activation(st[:, 3, :], st[:, 2, :], ACT.Ln, bias=con("eps", 1), scale=1.0 / 64)
                        act.drain()
                        nc.scalar.activation(st[:, 3, :], st[:, 3, :], ACT.Exp, scale=-0.5).then_inc(rstd_ready.sem, 1)
                    stage("gating", tensor=sgu_tensor, scalar=sgu_scalar, vector=sgu_vector)

                with ExitStack() as a:
                    qst = tmp("qst", [P, 2, 2, T], a)
                    vst = squares2[:, 6:8, :].rearrange("p t (b n) -> p t b n", n=P)
                    work = (squares2[:, 0:4, :].rearrange("p (u h) n -> p u (h n)", u=2), squares2[:, 4:6, :],
                            tmp("diag2", [P, 2, 2, P], a), tmp("stat2", [P, 2, 4, 2], a))
                    units = [[dict(scores=[lambda i, t=t, g=g, tb=tb: [(0, T, [(qst[:, t, g, tb * P:(tb + 1) * P],
                                                                         k[:, bass.ds(2 * i + g, 1), :].rearrange("p o n -> p (o n)"))])]],
                                  width=T, masks=[], sink=None, keys=TB,
                                  values=[(bank[g * 64:(g + 1) * 64, 6 + t, tb * P:(tb + 1) * P],
                                           [vst[:, t, j, g * 64:(g + 1) * 64] for j in range(TB)])])
                             for g in range(2) for tb in range(TB)] for t in range(2)]
                    attention("latent", 4, units, 96 ** -0.5,
                              lambda i, t: [(qst[:, t, :, :], q[:, bass.ds(2 * i, 2), :]),
                                         (vst[:, t, :, :], v[:, :, bass.ds(i, 1), :].rearrange("p b o n -> p b (o n)"))],
                              [], lambda i, t: (mix[:, bass.ds(i, 1), :].rearrange("p o n -> p (o n)"), bank[:, 6 + t, :]), work)
                    qst4 = raw[:, :, :].rearrange("p (t r) n -> p t r n", t=2)
                    units = [[dict(scores=[lambda i, t=t, g=g, tb=tb, c=c: [(0, T, [(qst4[:, t, 2 * g + c, tb * P:(tb + 1) * P],
                                                                               dk[:, bass.ds(i, 1), :].rearrange("p o n -> p (o n)"))])]
                                          for c in range(2)],
                                  width=T, masks=[], sink=None, keys=TB,
                                  values=[(bank[g * 64:(g + 1) * 64, 6 + t, tb * P:(tb + 1) * P],
                                           [vst[:, t, j, g * 64:(g + 1) * 64] for j in range(TB)])])
                             for g in range(2) for tb in range(TB)] for t in range(2)]
                    attention("differential", 2, units, 32 ** -0.5,
                              lambda i, t: [(qst4[32 * r:32 * r + 32, t, r, :],
                                          dq[32 * r:32 * r + 32, bass.ds(i, 1), :].rearrange("p o n -> p (o n)")) for r in range(4)] +
                              [(vst[:, t, :, :], dv[:, :, bass.ds(i, 1), :].rearrange("p b o n -> p b (o n)"))],
                              [qst4],
                              lambda i, t: (mix[:, bass.ds(i + 6, 1), :].rearrange("p o n -> p (o n)"), bank[:, 6 + t, :]),
                              work, neg_lam=neg_lam)
            norms("sub", [one_norm("o", lambda t, n=n: mix[:, 6 + n, :], lambda t: gain_sub, lambda t, n=n: mix[:, 6 + n, :], 1, T,
                                   "ones64", 64) for n in range(2)], squares2, scales2)

            def project(name, at, src, gain):
                linear(name, [("act", T, weights_still(at + n * KT, KT, lambda kt: src[:, kt, :]), act_copy(raw[:, n, :]))
                              for n in range(KT)])
                post(name, gain)

            def post(name, gain):
                norms(f"{name}_post", [one_norm("o", lambda t: raw[:, t, :], lambda t: p2(gain, 1, t), lambda t: xT[:, t, :],
                                                end=("residual", lambda t: xT[:, t, :]))], squares2, scales2)
            project("mix_out", B2_AT["mix"], mix, "mix_post")

            with ExitStack() as here:
                memn = tmp("memn", [P, KT, MEM], here)
                norms("mem_pre", [one_norm("x", lambda t: xT[:, t, :], lambda t: p2("mem_pre", 1, t), lambda t: hT[:, t, :]),
                                  one_norm("m", lambda t: memT[:, t, :], lambda t: p2("mem_kv", 1, t), lambda t: memn[:, t, :],
                                           KT, MEM)], squares2, scales2)
                k = tmp("mem_k", [P, KT, MEM], here)
                v = tmp("mem_v", [P, 2, 4, 256], here)
                tiles = [("act", T, weights_still(B2_AT["mq"] + n * KT, KT, lambda kt: hT[:, kt, :]), act_copy(raw[:, n, :]))
                         for n in range(KT)]
                tiles += [("dve", MEM, weights_still(B2_AT["mk"] + n * KT, KT, lambda kt: memn[:, kt, :]), dve_copy(k[:, n, :]))
                          for n in range(KT)]
                for half in range(2):
                    group = value_group(B2_AT["mv"] + half * 4 * KT, KT, 4,
                                        [lambda kt, tb=tb: memn[:, kt, tb * P:(tb + 1) * P] for tb in range(2)])
                    for tb in range(2):
                        tiles.append(("act", 512, group,
                                      act_copy(v[:, tb, 2 * half:2 * half + 2, :].rearrange("p h n -> p (h n)"))))
                linear("mem_qkv", tiles)
                with ExitStack() as a:
                    qst = tmp("mem_qst", [P, 2, 2, T], a)
                    vst = tmp("mem_vst", [P, 2, 2, 256], a)
                    work = (tmp("probs3", [P, 2, 1024], a), tmp("probsT3", [P, 2, 256], a),
                            tmp("diag3", [P, 2, 1, P], a), tmp("stat3", [P, 2, 4, 2], a))
                    units = [[dict(scores=[lambda i, t=t, tb=tb: [(0, MEM, [(qst[:, t, e, tb * P:(tb + 1) * P],
                                                                       k[:, bass.ds(2 * i + e, 1), :].rearrange("p o n -> p (o n)"))
                                                                      for e in range(2)])]],
                                  width=MEM, masks=[], sink=None, keys=2,
                                  values=[(bank[:, 6 + e, tb * P:(tb + 1) * P], [vst[:, t, j, e * P:(e + 1) * P] for j in range(2)])
                                          for e in range(2)]) for tb in range(TB)] for t in range(2)]
                    attention("memory", 4, units, 256 ** -0.5,
                              lambda i, t: [(qst[:, t, :, :], raw[:, bass.ds(2 * i, 2), :]),
                                         (vst[:, t, :, :], v[:, :, bass.ds(i, 1), :].rearrange("p b o n -> p b (o n)"))],
                              [], lambda i, t: (mix[:, bass.ds(2 * i, 2), :], bank[:, 6:8, :]), work,
                              shared_out=True)
            project("mem_out", B2_AT["mo"], mix, "mem_post")

            norms("ffn_pre", [one_norm("x", lambda t: xT[:, t, :], lambda t: p2("ffn_pre", 1, t), lambda t: hT[:, t, :])],
                  squares2, scales2)
            up_down("2", B2_AT, ACT.Gelu_apprx_tanh, True, col(par2, PAR2["conv_w"]), col(par2, PAR2["conv_b"]),
                    lambda n: lambda dve, ps: nc.vector.tensor_copy(raw[:, n, :], ps),
                    mix[:, 0:4, :].rearrange("p (u s) n -> p u s n", u=2))
            post("ffn", "ffn_post")

        if upto >= 8:
            ws.base, ws.fed, ws.begun, ws.limit = B1_SLABS, 0, 0, B2_SLABS
            with nc.Fori(0, LAYERS) as l:
                layer[0] = l
                layer_body(l)
            layer[0] = None
            totals = {r: n for r, n in used_here.items() if r.endswith("_2")}
            assert totals == PER_LAYER, totals

        stored = Signal("stored", 16)

        def sync(sp):
            sp.dma_start(out, xT[:, :, :]).then_inc(stored.sem, 16)
            sp.wait_ge(stored.sem, stored.at(16))
        ws.limit = 0
        stage("store", sync=sync)


def constants():
    c = np.zeros((P, CONST_W), np.float32)

    def put(name, a, at=0):
        c[:, CONST[name] + at:CONST[name] + at + a.shape[1]] = a
    p = np.arange(P)
    put("ident", np.eye(P))
    put("ones", np.ones((P, P)))
    put("ones64", (p[:, None] // 64 == p[None, :] // 64) * 1.0)
    rot = np.zeros((P, P))
    rot[p[1::2], p[0::2]] = -1.0
    rot[p[0::2], p[1::2]] = 1.0
    put("rot1", rot)
    rot = np.zeros((P, P))
    for i in range(16):
        rot[64 + 16 + i, 64 + i] = -1.0
        rot[64 + i, 64 + 16 + i] = 1.0
    put("rot_mla", rot)
    rot = np.zeros((P, P))
    for base in range(0, P, 32):
        for i in range(8):
            rot[base + 8 + i, base + i] = -1.0
            rot[base + i, base + 8 + i] = 1.0
    put("rot_diff", rot)
    put("mask_prev", np.where(p[None, :] >= p[:, None], 0.0, NEG_BIG))
    put("mask_next", np.where(p[None, :] <= p[:, None], 0.0, NEG_BIG))
    j, t = p[:, None], p[None, :]
    for d in range(2):
        for l in range(LEVELS + 1):
            if l == LEVELS:
                m = j == t
            else:
                h = CHUNK >> l
                jh, th = (0, 1) if d == 0 else (1, 0)
                m = (j // (2 * h) == t // (2 * h)) & (j // h % 2 == jh) & (t // h % 2 == th)
            put("levels", m * 1.0, (d * (LEVELS + 1) + l) * P)
    tok = np.arange(ALLT)
    put("reset", np.broadcast_to((tok % CHUNK != 0) * 1.0, (P, ALLT)))
    put("reset", np.broadcast_to((tok % CHUNK != CHUNK - 1) * 1.0, (P, ALLT)), ALLT)
    n = np.arange(T)
    half = HD // 4
    inv = (THETA_1 ** (-np.arange(0, 2 * half, 2, dtype=np.float32) / np.float32(2 * half))).astype(np.float32)
    ang = np.concatenate([(n // GRID_W).astype(np.float32)[:, None] * inv, (n % GRID_W).astype(np.float32)[:, None] * inv], 1)
    ang = ang.T[(p % HD) // 2]
    put("cos1", np.cos(ang))
    put("sin1", np.sin(ang))
    freq = np.zeros((P, 2), np.float32)
    inv = (THETA_2 ** (-np.arange(0, 32, 2, dtype=np.float32) / np.float32(32))).astype(np.float32)
    freq[64:96, 0] = np.tile(inv, 2)
    inv = (THETA_2 ** (-np.arange(0, 16, 2, dtype=np.float32) / np.float32(16))).astype(np.float32)
    for base in range(0, P, 32):
        freq[base:base + 16, 1] = np.tile(inv, 2)
    put("freq", freq)
    put("eps", np.full((P, 1), EPS))
    put("half_pi", np.full((P, 1), np.pi / 2))
    put("one", np.ones((P, 1)))
    return c


def weight_stream(w):
    blocks = []

    def still(m, cols, tiles=None):
        for c in cols:
            for k in range(m.shape[0] // P):
                blocks.append(m[k * P:(k + 1) * P, c])

    def padded(m, at):
        full = np.zeros((m.shape[0], P), np.float32)
        full[:, at:at + m.shape[1]] = m
        return full

    def moving(m, n):
        for c in range(0, m.shape[1], n * P):
            for k in range(m.shape[0] // P):
                for e in range(n):
                    blocks.append(m[k * P:(k + 1) * P, c + e * P:c + (e + 1) * P])

    def tiles(n, start=0):
        return [slice(start + c * P, start + (c + 1) * P) for c in range(n)]
    still(w["w_mod"][0], tiles(MOD_TILES))
    w_in = w["w_in"][0]
    pair = [np.r_[g * HD:(g + 1) * HD, (g + 4) * HD:(g + 5) * HD] for g in range(4)]
    for at in (0, 768):
        still(w_in, [at + c for c in pair])
        still(w_in, [slice(at + 512, at + 640), slice(at + 640, at + 768)])
    still(w_in, tiles(12, 1536))
    moving(w_in[:, 3072:3584], 4)
    still(w_in, tiles(4, 3584))
    for n in range(KT):
        for b in range(3):
            still(w_in, [slice(4096 + b * D + n * P, 4096 + b * D + (n + 1) * P)])
            wb = w["w_branch"][0, b]
            if b < 2:
                wb = np.concatenate([wb[c] for c in pair])
            still(wb, tiles(KT)[n:n + 1])
    still(w["w_out"][0], tiles(KT))

    def ffn_blocks(up, down):
        for n in range(FT):
            still(up, [slice(n * P, (n + 1) * P), slice(FF + n * P, FF + (n + 1) * P)])
        still(down, tiles(KT))
    ffn_blocks(w["w_up"][0], w["w_down"][0])
    assert len(blocks) == B1_SLABS * SLAB
    for l in range(LAYERS):
        w_in = w["w_in_2"][l]
        still(w_in, tiles(5))
        still(padded(w_in[:, 640:672], 64), tiles(1))
        still(w_in, tiles(2, 672) + tiles(4, 1184))
        moving(w_in[:, 928:1184], 2)
        moving(w_in[:, 1696:1952], 2)
        uq, ukv = w["mla_w_uq_2"][l], w["mla_w_ukv_2"][l]
        for h in range(8):
            still(padded(uq[:, h * 96:(h + 1) * 96], 0), tiles(1))
        for h in range(8):
            still(padded(ukv[:, h * P:h * P + 64], 0), tiles(1))
        moving(np.concatenate([ukv[:, h * P + 64:(h + 1) * P] for h in range(8)], 1), 4)
        still(w["w_mix_out_2"][l], tiles(KT))
        still(w["mem_w_q_2"][l], tiles(KT))
        still(w["mem_w_kv_2"][l], tiles(KT))
        moving(w["mem_w_kv_2"][l][:, D:], 4)
        still(w["mem_w_o_2"][l], tiles(KT))
        ffn_blocks(w["ffn_w_up_2"][l], w["ffn_w_down_2"][l])
    assert len(blocks) == SLABS * SLAB
    return np.stack(blocks).reshape(SLABS, SLAB, P, P).transpose(0, 2, 1, 3).reshape(SLABS, P, SLAB * P)


def cols(v):
    return np.asarray(v).reshape(-1, P).T


def conv_cols(w):
    return np.concatenate([cols(tap) for tap in w], 1)


def rows(v):
    v = np.asarray(v).reshape(1, -1)
    return np.broadcast_to(v, (P, v.shape[1]))


def table(places, width, fields):
    t = np.zeros((P, width), np.float32)
    for name, a in fields.items():
        t[:, places[name]:places[name] + a.shape[1]] = a
    return t


def host_layout(w):
    w = {k: np.asarray(v) for k, v in w.items()}

    def features_first(a):
        return np.ascontiguousarray(a[0].T.reshape(KT, P, -1).transpose(1, 0, 2))
    both = np.stack([cols(w["c"][0]), cols(w["c_ctx"])], 2).reshape(P, 2 * KT)
    par1 = table(PAR1, PAR1_W, dict(
        c=both, b_mod=cols(w["b_mod"][0]), norm_mix=cols(w["norm_mix"][0]), norm_ffn=cols(w["norm_ffn"][0]),
        qn=cols(np.concatenate([w["qn_b"][0]] * 2)), kn=cols(np.concatenate([w["kn_b"][0]] * 2)),
        lb=np.concatenate([cols(w["lb_fwd"][0]), cols(w["lb_bwd"][0])], 1), gn=cols(w["gn_c"][0]),
        conv_w=conv_cols(w["w_dw"][0]), conv_b=cols(w["b_dw"][0]), norm_final=cols(w["norm_final"]),
        sink=rows(w["sink_a"][0])))
    par2 = []
    for l in range(LAYERS):
        lam_init = 0.8 - 0.6 * np.exp(-0.3 * l)
        par2.append(table(PAR2, PAR2_W, dict(
            mix_pre=cols(w["mix_pre_g_2"][l]), mix_post=cols(w["mix_post_g_2"][l]), cq_g=cols(w["mla_cq_g_2"][l]),
            ckv_g=cols(w["mla_ckv_g_2"][l]), sub_g=cols(np.concatenate([w["diff_sub_g_2"][l]] * 2)),
            mem_pre=cols(w["mem_pre_g_2"][l]), mem_post=cols(w["mem_post_g_2"][l]), mem_kv=cols(w["mem_kv_g_2"][l]),
            ffn_pre=cols(w["ffn_pre_g_2"][l]), ffn_post=cols(w["ffn_post_g_2"][l]),
            conv_w=conv_cols(w["ffn_conv_w_2"][l]), conv_b=cols(w["ffn_conv_b_2"][l]),
            lam=rows(np.concatenate([w[f"diff_lam_{n}_2"][l] for n in ("q1", "k1", "q2", "k2")])),
            lam_init=np.full((P, 1), lam_init, np.float32), one_less_lam=np.full((P, 1), 1.0 - lam_init, np.float32),
            sgu_g=rows(w["sgu_norm_g_2"][l]),
            sgu_b=np.concatenate([np.repeat(w["sgu_b_s_2"][l][2 * n:2 * n + 2], 64, 0) for n in range(2)], 1),
            sgu_w=w["sgu_w_s_2"][l].transpose(2, 0, 1).reshape(P, 4 * P))))
    return {"stream": weight_stream(w), "xT": features_first(w["x"]), "ctxT": features_first(w["ctx"]),
            "memT": features_first(w["mem_2"]), "pos": w["positions_2"], "const": constants(), "par1": par1,
            "par2": np.stack(par2)}


def kernel(**inputs):
    import concourse.bacc as bacc
    from concourse.bass_utils import run_bass_kernel_spmd
    arrays = {f"in_{name}": np.ascontiguousarray(a) for name, a in host_layout(inputs).items()}
    nc = bacc.Bacc("TRN2", target_bir_lowering=False, num_devices=1, dynamic_dma_scratch_size=1024)
    args = [nc.dram_tensor(name, a.shape, mybir.dt.from_np(a.dtype), kind="ExternalInput").ap()
            for name, a in arrays.items()]
    out = nc.dram_tensor("out", (P, KT, T), F32, kind="ExternalOutput").ap()
    build_program(nc, *args, out)
    got = run_bass_kernel_spmd(nc, [arrays], core_ids=[0]).results[0]["out"]
    return np.ascontiguousarray(got.transpose(1, 0, 2).reshape(D, T).T)[None]
```

```python
from contextlib import ExitStack

import numpy as np

import concourse.bass as bass
from concourse import mybir

F32 = mybir.dt.float32
F32R = mybir.dt.float32r
I32 = mybir.dt.int32
ALU = mybir.AluOpType
ACT = mybir.ActivationFunctionType
AX = mybir.AxisListType

P = 128
D = 1024
KT = D // P
T = 512
TB = T // P
CT = 256
CB = CT // P
ALLT = CT + T
FF = 2816
FT = FF // P
HD = 64
EPS = 1e-6
NEG_BIG = -1e30
LAYERS = 2
MEM = 256
GRID_W = 64
THETA_1, THETA_2 = 10000.0, 500000.0
CHUNK = 64
LEVELS = 7
C_HEADS = 4

SLAB = 16
RING = 4
HI = 2
SQUARES = 4
MOD_TILES = 6 * KT
QKV_BLOCKS = 6 * KT
B1_AT = {}
_at = 0
for _name, _n in (("mod", MOD_TILES * KT), ("C", 16 * KT), ("A", QKV_BLOCKS), ("B", QKV_BLOCKS),
                  ("cg", 4 * KT), ("merge", KT * 3 * (KT + 4)), ("out", KT * KT), ("up", 2 * FT * KT),
                  ("down", KT * FT)):
    B1_AT[_name] = _at
    _at += _n
B1_SLABS = _at // SLAB
WHOLE_SLABS = B1_AT["C"] // SLAB
assert WHOLE_SLABS * SLAB == B1_AT["C"]
assert _at == B1_SLABS * SLAB
B2_AT = {}
_at = 0
for _name, _n in (("in", 16 * KT), ("uq", 8 * 3), ("uk", 8 * 2), ("uv", 4 * 2), ("mix", KT * KT),
                  ("mq", KT * KT), ("mk", KT * KT), ("mv", KT * KT), ("mo", KT * KT),
                  ("up", 2 * FT * KT), ("down", KT * FT)):
    B2_AT[_name] = _at
    _at += _n
B2_SLABS = _at // SLAB
assert _at == B2_SLABS * SLAB and B2_SLABS % RING == 0
for _at in (B1_AT["up"], B2_AT["up"]):
    assert _at % SLAB == 0 and 2 * KT == SLAB
SLABS = B1_SLABS + LAYERS * B2_SLABS
PER_LAYER = {'params_loaded_2': 16, 'lam_dots_2': 1, 'lam_exp_2': 1, 'square_ready_2': 63, 'square_summed_2': 63, 'scale_ready_2': 11, 'normed_2': 63, 'upper_ready_2': 37, 'tile_done_2': 84, 'out_by_act_2': 48, 'out_by_dve_2': 28, 'rotated_2': 13, 'by_cos_2': 13, 'by_sin_2': 13, 'roped_2': 13, 'centered_2': 1, 'sgu_square_ready_2': 1, 'var_ready_2': 1, 'rstd_ready_2': 1, 'gate_ready_2': 1, 'chunks_mixed_2': 1, 'staged_2': 10, 'scored_2': 64, 'max_ready_2': 64, 'exp_done_2': 64, 'diag_ready_2': 64, 'turned0_2': 64, 'turned1_2': 64, 'probs_out0_2': 64, 'probs_out1_2': 64, 'summed_2': 10, 'sum_read_2': 16, 'operand_rounded_2': 38, 'operand_split_2': 38, 'memory_loaded_2': 16, 'pair_done_2': 22, 'center_ready_2': 22, 'banks_free_2': 26, 'acted_2': 22, 'gated_2': 24, 'operand_used_2': 22}


def columns(fields):
    at, places = 0, {}
    for name, n in fields:
        places[name] = at
        at += n
    return places, at


CONST, CONST_W = columns([
    ("ident", P), ("ones", P), ("ones64", P), ("rot1", P), ("rot_mla", P), ("rot_diff", P),
    ("mask_prev", P), ("mask_next", P), ("levels", 2 * (LEVELS + 1) * P), ("reset", 2 * ALLT),
    ("freq", 2), ("eps", 1), ("half_pi", 1), ("one", 1)])
PAR1, PAR1_W = columns([
    ("c", 2 * KT), ("b_mod", MOD_TILES), ("norm_mix", KT), ("norm_ffn", KT), ("qn", 1), ("kn", 1),
    ("lb", 2 * C_HEADS), ("gn", 1), ("conv_w", 3 * 2 * FT), ("conv_b", 2 * FT), ("norm_final", KT),
    ("sink", 8)])
PAR2, PAR2_W = columns([
    ("mix_pre", KT), ("mix_post", KT), ("cq_g", 3), ("ckv_g", 2), ("sub_g", 1), ("mem_pre", KT),
    ("mem_post", KT), ("mem_kv", KT), ("ffn_pre", KT), ("ffn_post", KT), ("conv_w", 3 * 2 * FT),
    ("conv_b", 2 * FT), ("lam", 4 * 32), ("lam_init", 1), ("one_less_lam", 1), ("sgu_g", 256),
    ("sgu_b", 2 * P), ("sgu_w", 4 * P)])


def build_program(nc, stream, xT_in, ctxT_in, memT_in, pos_in, const_in, axial_in, par1_in, par2_in, out):
    stack = ExitStack()
    with stack:
        place = {}

        def new(scope, name, shape, dt):
            tensor = scope.enter_context(nc.sbuf_tensor(name, shape, dt))
            place[name] = nc.sbuf_base - int(np.prod(shape[1:])) * 4
            return tensor

        def sb(name, shape, dt=F32):
            return new(stack, name, shape, dt)

        def same_place(name, of, shape, dt):
            return nc.alloc_sbuf_tensor_at(name, shape, dt, offset=place[of])

        ring = sb("ring", [P, RING, SLAB, P])
        ring_lo = same_place("ring_lo", "ring", [P, RING, SLAB, P], F32R)
        ring_hi = sb("ring_hi", [P, HI, SLAB, P], F32R)
        ring_spare = same_place("ring_spare", "ring_hi", [P, HI * SLAB * P], F32)
        xT = sb("xT", [P, KT, T])
        hT = sb("hT", [P, KT, T])
        h_lo = same_place("h_lo", "hT", [P, KT, T], F32R)
        h_hi = sb("h_hi", [P, KT, T], F32R)
        h_spare = same_place("h_spare", "h_hi", [P, KT, T], F32)
        const = sb("const", [P, CONST_W])
        par1 = sb("par1", [P, PAR1_W])
        small = sb("small", [P, 256])
        bank = stack.enter_context(nc.psum_tensor("bank", [P, 8, 512], F32))

        def con(name, n=P, at=0):
            return const[:, CONST[name] + at:CONST[name] + at + n]

        def p1(name, n=1, at=0):
            return par1[:, PAR1[name] + at:PAR1[name] + at + n]

        layer = [None]

        roles, used_here = {}, {}

        class Signal:

            def __init__(self, role, count):
                role = role if layer[0] is None else f"{role}_2"
                if role not in roles:
                    roles[role] = stack.enter_context(nc.semaphore(role))
                self.sem, self.start = roles[role], used_here.get(role, 0)
                self.per_layer = 0 if layer[0] is None else PER_LAYER[role]
                used_here[role] = self.start + count

            def at(self, n):
                n = n + self.start
                return n if layer[0] is None else n + layer[0] * self.per_layer

        slab_loaded = [stack.enter_context(nc.semaphore(f"slab_loaded{r}")) for r in range(RING)]
        slab_begun = stack.enter_context(nc.semaphore("slab_begun"))
        slab_rounded = stack.enter_context(nc.semaphore("slab_rounded"))
        slab_split = stack.enter_context(nc.semaphore("slab_split"))

        class Stream:
            base, fed, begun, pending, rounded, halved = 0, 0, 0, False, 0, 0

            def count(self, slab, turn=0):
                n = self.base + slab + 1 + turn
                return n if layer[0] is None else layer[0] * B2_SLABS + n

            def loads(self, slab, turn=0):
                n = (self.base + slab) // RING + 1 + turn
                return (n if layer[0] is None else layer[0] * (B2_SLABS // RING) + n) * 16

            def begin(self, pe, block, whole):
                slab = block // SLAB
                if slab >= self.begun:
                    assert slab == self.begun
                    if whole:
                        pe.wait_ge(slab_loaded[(self.base + slab) % RING], self.loads(slab))
                    else:
                        pe.wait_ge(slab_split, self.count(slab) - WHOLE_SLABS)
                    self.begun += 1
                    self.pending = True

            def slab(self, slab):
                return ring[:, (self.base + slab) % RING, :, :].rearrange("p b n -> p (b n)")

            def slab_hi(self, slab):
                return ring_hi[:, (self.base + slab) % HI, :, :].rearrange("p b n -> p (b n)")

            def round(self, act, slab, loop=None, j=0):
                g = self.base + slab + j
                turns, slabs = (0, j) if loop is None else (loop, loop * RING + j)
                act.wait_ge(slab_loaded[g % RING], self.loads(slab + j, turns))
                if layer[0] is not None or g >= WHOLE_SLABS + HI:
                    act.wait_ge(slab_begun, self.count(slab, slabs) + (1 - HI))
                nc.scalar.activation(self.slab_hi(slab + j), self.slab(slab + j), ACT.Copy).then_inc(slab_rounded, 1)

            def halve(self, dve, slab, loop=None, j=0):
                slabs = j if loop is None else loop * RING + j
                dve.wait_ge(slab_rounded, self.count(slab, slabs) - WHOLE_SLABS)
                lower = ring_lo[:, (self.base + slab + j) % RING, :, :].rearrange("p b n -> p (b n)")
                nc.vector.tensor_tensor(lower, self.slab(slab + j), self.slab_hi(slab + j).bitcast(F32), ALU.subtract)\
                    .then_inc(slab_split, 1)

            def round_to(self, act, slab, last):
                while self.rounded <= min(slab, last - 1):
                    self.round(act, self.rounded)
                    self.rounded += 1

            def halve_to(self, dve, slab, last):
                while self.halved <= min(slab, last - 1):
                    self.halve(dve, self.halved)
                    self.halved += 1

            def parts(self, b, n=1):
                slab, at = divmod(b, SLAB)
                assert at + n <= SLAB
                return (ring_hi[:, (self.base + slab) % HI, at:at + n, :].rearrange("p b n -> p (b n)"),
                        ring_lo[:, (self.base + slab) % RING, at:at + n, :].rearrange("p b n -> p (b n)"))

            def mm_whole(self, pe, b, out, rhs, start, stop):
                self.begin(pe, b, True)
                slab, at = divmod(b, SLAB)
                ins = nc.tensor.matmul(out, ring[:, (self.base + slab) % RING, at, :], rhs, start=start, stop=stop)
                if self.pending:
                    ins.then_inc(slab_begun, 1)
                    self.pending = False
                return ins

            def mm(self, pe, b, n, out, operand, still, start, stop):
                self.begin(pe, b, False)
                w_hi, w_lo = self.parts(b, n)
                x_hi, x_lo = operand
                for w, x in ((w_hi, x_hi), (w_hi, x_lo), (w_lo, x_hi)):
                    lhsT, rhs = (w, x) if still else (x, w)
                    ins = nc.tensor.matmul(out, lhsT, rhs, start=start and w is w_hi and x is x_hi, stop=stop and w is w_lo)
                    if self.pending:
                        ins.then_inc(slab_begun, 1)
                        self.pending = False
                return ins

            def feed(self, sp, last):
                upto_slab = min(last, self.begun + RING - 1)
                while self.fed < upto_slab:
                    s = self.fed
                    g = self.base + s
                    if layer[0] is not None or g >= RING:
                        v = g - RING + 2
                        sp.wait_ge(slab_begun, v if layer[0] is None else layer[0] * B2_SLABS + v)
                    if layer[0] is None:
                        src = stream[g]
                    else:
                        src = stream[bass.ds(layer[0] * B2_SLABS + g, 1)].rearrange("o p n -> p (o n)")
                    sp.dma_start(ring[:, g % RING, :, :].rearrange("p b n -> p (b n)"), src)\
                        .then_inc(slab_loaded[g % RING], 16)
                    self.fed += 1

        ws = Stream()
        ws.limit, ws.rounded, ws.halved = B1_SLABS, WHOLE_SLABS, WHOLE_SLABS

        def stage(name, tensor=None, scalar=None, vector=None, gpsimd=None, sync=None):
            with nc.Block() as block:
                if tensor:
                    @block.tensor
                    def _(pe):
                        tensor(pe)

                @block.sync
                def _(sp):
                    if sync:
                        sync(sp)
                    ws.feed(sp, ws.limit)
                if scalar:
                    @block.scalar
                    def _(act):
                        scalar(act)
                if vector:
                    @block.vector
                    def _(dve):
                        vector(dve)
                if gpsimd:
                    @block.gpsimd
                    def _(pool):
                        gpsimd(pool)

        def bcast(ap, n):
            return ap.rearrange("p (k o) -> p k o", o=1).to_broadcast([P, ap.shape[1], n])

        class Split:

            def __init__(self, hi, lo, whole=None):
                self.whole, self.hi, self.lo, self.ready, self.waited = whole, hi, lo, None, 0

            def part(self, pe, k, cols=slice(None)):
                if self.ready is not None and k >= self.waited:
                    self.waited = k + 1
                    pe.wait_ge(self.ready.sem, self.ready.at(k + 1))
                return self.hi[:, k, cols], self.lo[:, k, cols]

        def linear(name, tiles, banks=8, sync=None, operands=(), last_split=None):
            n_act = sum(t[0] == "act" for t in tiles)
            limit = ws.limit if last_split is None else last_split
            tile_done = Signal("tile_done", len(tiles))
            out_by = {"act": Signal("out_by_act", n_act),
                      "dve": Signal("out_by_dve", len(tiles) - n_act)}
            rounded = [Signal("operand_rounded", x.hi.shape[1]) for x in operands]
            for x in operands:
                x.ready, x.waited = Signal("operand_split", x.hi.shape[1]), 0
            ordinal, seen = [], {"act": 0, "dve": 0}
            for t in tiles:
                seen[t[0]] += 1
                ordinal.append(seen[t[0]])

            def tensor(pe):
                n = 0
                while n < len(tiles):
                    cols, products = tiles[n][1:3]
                    members = len(products["tokens"])
                    for m in range(n, n + members):
                        if m >= banks:
                            out = out_by[tiles[m - banks][0]]
                            pe.wait_ge(out.sem, out.at(ordinal[m - banks]))
                    outs = [bank[:, m % banks, 0:cols] for m in range(n, n + members)]
                    kts, width = products["kts"], products["width"]
                    for k in range(kts):
                        b = products["at"] + k * width
                        for out_ap, operand in zip(outs, products["tokens"]):
                            last = ws.mm(pe, b, width, out_ap, operand(pe, k), products["still"], k == 0, k == kts - 1)
                            if k == kts - 1:
                                last.then_inc(tile_done.sem, 1)
                    n += members

            def last_slab(products):
                return (products["at"] + products["kts"] * products["width"] - 1) // SLAB

            def first_slab():
                return tiles[0][2]["at"] // SLAB

            def scalar(act):
                ws.round_to(act, first_slab(), limit)
                for x, done in zip(operands, rounded):
                    for k in range(x.hi.shape[1]):
                        nc.scalar.activation(x.hi[:, k, :], x.whole[:, k, :], ACT.Copy).then_inc(done.sem, 1)
                for n, (engine, cols, products, out_fn, *before) in enumerate(tiles):
                    ws.round_to(act, last_slab(products) + 1, limit)
                    if engine == "act":
                        for b in before:
                            act.wait_ge(out_by["dve"].sem, out_by["dve"].at(ordinal[b]))
                        act.wait_ge(tile_done.sem, tile_done.at(n + 1))
                        out_fn(act, bank[:, n % banks, 0:cols]).then_inc(out_by["act"].sem, 1)

            def vector(dve):
                ws.halve_to(dve, first_slab(), limit)
                for x, done in zip(operands, rounded):
                    for k in range(x.hi.shape[1]):
                        dve.wait_ge(done.sem, done.at(k + 1))
                        nc.vector.tensor_tensor(x.lo[:, k, :], x.whole[:, k, :], x.hi[:, k, :].bitcast(F32), ALU.subtract)\
                            .then_inc(x.ready.sem, 1)
                for n, (engine, cols, products, out_fn, *before) in enumerate(tiles):
                    ws.halve_to(dve, last_slab(products) + 1, limit)
                    if engine == "dve":
                        for b in before:
                            dve.wait_ge(out_by["act"].sem, out_by["act"].at(ordinal[b]))
                        dve.wait_ge(tile_done.sem, tile_done.at(n + 1))
                        out_fn(dve, bank[:, n % banks, 0:cols]).then_inc(out_by["dve"].sem, 1)

            stage(name, tensor=tensor, scalar=scalar, vector=vector, sync=sync)

        def split_hi(k):
            return h_hi[:, k, :]

        def split_lo(k):
            return h_lo[:, k, :]

        def weights_still(at, kts, x, cols=slice(None), first=0):
            return dict(at=at, kts=kts, width=1, still=True, tokens=[lambda pe, k: x.part(pe, first + k, cols)])

        def weights_moving(at, kts, n, tokens):
            return dict(at=at, kts=kts, width=n, still=False, tokens=tokens)

        def act_copy(dst, func=ACT.Copy):
            return lambda act, ps: nc.scalar.activation(dst, ps, func)

        def dve_copy(dst):
            return lambda dve, ps: nc.vector.tensor_copy(dst, ps)

        def norms(name, jobs, squares, scales, sync=None, loaded=None):
            total = sum(j["tiles"] for j in jobs)
            square_ready = Signal("square_ready", total)
            square_summed = Signal("square_summed", total)
            scale_ready = Signal("scale_ready", len(jobs))
            normed = Signal("normed", total)
            upper_ready = Signal("upper_ready", sum(j["tiles"] for j in jobs if j["end"] and j["end"][0] == "split"))
            starts = []
            at = 0
            for j in jobs:
                starts.append(at)
                at += j["tiles"]

            def scalar(act):
                def square(n, tiles):
                    j = jobs[n]
                    if loaded and n == loaded[0] and 0 in tiles:
                        act.wait_ge(loaded[1].sem, loaded[1].at(16))
                    for k in tiles:
                        q = starts[n] + k
                        if q >= SQUARES:
                            act.wait_ge(square_summed.sem, square_summed.at(q - SQUARES + 1))
                        nc.scalar.activation(squares[:, q % SQUARES, 0:j["cols"]], j["src"](k), ACT.Square)\
                            .then_inc(square_ready.sem, 1)
                square(0, range(jobs[0]["tiles"]))
                for n, j in enumerate(jobs):
                    ahead = min(jobs[n + 1]["tiles"], SQUARES) if n + 1 < len(jobs) else 0
                    if ahead:
                        square(n + 1, range(ahead))
                    act.wait_ge(square_summed.sem, square_summed.at(starts[n] + j["tiles"]))
                    if n >= 2:
                        act.wait_ge(normed.sem, normed.at(starts[n - 1]))
                    s = scales[:, n % 2, 0:j["cols"]]
                    nc.scalar.activation(s, bank[:, n % 2, 0:j["cols"]], ACT.Ln, bias=con("eps", 1), scale=j["inv"])
                    act.drain()
                    nc.scalar.activation(s, s, ACT.Exp, scale=-0.5).then_inc(scale_ready.sem, 1)
                    if n + 1 < len(jobs):
                        square(n + 1, range(ahead, jobs[n + 1]["tiles"]))
                    if j["end"] and j["end"][0] == "split":
                        _, hi, lo, shift = j["end"]
                        for k in range(j["tiles"]):
                            act.wait_ge(normed.sem, normed.at(starts[n] + k + 1))
                            if shift:
                                up = nc.scalar.activation(hi(k), j["out"](k), ACT.Identity, bias=shift(k))
                            else:
                                up = nc.scalar.activation(hi(k), j["out"](k), ACT.Copy)
                            up.then_inc(upper_ready.sem, 1)

            def tensor(pe):
                for n, j in enumerate(jobs):
                    if n >= 2:
                        pe.wait_ge(scale_ready.sem, scale_ready.at(n - 1))
                    for k in range(j["tiles"]):
                        q = starts[n] + k
                        pe.wait_ge(square_ready.sem, square_ready.at(q + 1))
                        nc.tensor.matmul(bank[:, n % 2, 0:j["cols"]], j["ones"], squares[:, q % SQUARES, 0:j["cols"]],
                                         start=k == 0, stop=k == j["tiles"] - 1).then_inc(square_summed.sem, 1)

            def vector(dve):
                for n, j in enumerate(jobs):
                    dve.wait_ge(scale_ready.sem, scale_ready.at(n + 1))
                    if loaded and n == loaded[0]:
                        dve.wait_ge(loaded[1].sem, loaded[1].at(16))
                    for k in range(j["tiles"]):
                        ends = j["end"] and j["end"][0] in ("residual", "times")
                        dst = j["src"](k) if ends else j["out"](k)
                        nc.vector.scalar_tensor_tensor(dst, j["src"](k), j["gain"](k), scales[:, n % 2, 0:j["cols"]],
                                                       ALU.mult, ALU.mult).then_inc(normed.sem, 1)

                uppers = 0
                for n, j in enumerate(jobs):
                    if j["end"] and j["end"][0] == "split":
                        _, hi, lo, shift = j["end"]
                        for k in range(j["tiles"]):
                            uppers += 1
                            dve.wait_ge(upper_ready.sem, upper_ready.at(uppers))
                            h, up = j["out"](k), hi(k).bitcast(F32)
                            if shift:
                                nc.vector.scalar_tensor_tensor(lo(k), h, shift(k), up, ALU.add, ALU.subtract)
                            else:
                                nc.vector.tensor_tensor(lo(k), h, up, ALU.subtract)

            def gpsimd(pool):
                for n, j in enumerate(jobs):
                    if not j["end"] or j["end"][0] == "split":
                        continue
                    how, other = j["end"]
                    for k in range(j["tiles"]):
                        pool.wait_ge(normed.sem, normed.at(starts[n] + k + 1))
                        nc.gpsimd.tensor_tensor(j["out"](k), other(k), j["src"](k), ALU.add if how == "residual" else ALU.mult)

            stage(name, tensor=tensor, scalar=scalar, vector=vector, gpsimd=gpsimd, sync=sync)

        def rope(name, jobs, work):
            n_jobs = len(jobs)
            rotated = Signal("rotated", n_jobs)
            by_cos = Signal("by_cos", n_jobs)
            by_sin = Signal("by_sin", n_jobs)
            roped = Signal("roped", n_jobs)

            def tensor(pe):
                for n, (raw, rot, _, _, _) in enumerate(jobs):
                    if n >= 4:
                        pe.wait_ge(by_sin.sem, by_sin.at(n - 3))
                    nc.tensor.matmul(bank[:, n % 4, :], rot, raw, start=True, stop=True).then_inc(rotated.sem, 1)

            def vector(dve):
                for n, (_, _, _, sin, _) in enumerate(jobs):
                    dve.wait_ge(rotated.sem, rotated.at(n + 1))
                    if n >= 2:
                        dve.wait_ge(roped.sem, roped.at(n - 1))
                    nc.vector.tensor_tensor(work[:, 2 + n % 2, :], bank[:, n % 4, :], sin, ALU.mult)\
                        .then_inc(by_sin.sem, 1)

            def gpsimd(pool):
                def cosine(n):
                    raw, _, cos, _, _ = jobs[n]
                    nc.gpsimd.tensor_tensor(work[:, n % 2, :], raw, cos, ALU.mult).then_inc(by_cos.sem, 1)
                cosine(0)
                for n in range(n_jobs):
                    if n + 1 < n_jobs:
                        cosine(n + 1)
                    pool.wait_ge(by_cos.sem, by_cos.at(n + 1))
                    pool.wait_ge(by_sin.sem, by_sin.at(n + 1))
                    nc.gpsimd.tensor_tensor(jobs[n][4], work[:, n % 2, :], work[:, 2 + n % 2, :], ALU.add)\
                        .then_inc(roped.sem, 1)
                    pool.drain()

            stage(name, tensor=tensor, vector=vector, gpsimd=gpsimd)

        def attention(name, turns, units, scale, copies, zeros, read_out, work, sink=None, neg_lam=None, shared_out=False):
            U = len(units[0])
            units = units[0] + units[1]
            N = len(units)
            passes = turns // 2
            total = turns * U
            staged = Signal("staged", turns)
            scored = Signal("scored", total)
            max_ready = Signal("max_ready", total)
            exp_done = Signal("exp_done", total)
            diag_ready = Signal("diag_ready", total)
            turned = [Signal(f"turned{h}", total) for h in range(2)]
            probs_out = [Signal(f"probs_out{h}", total) for h in range(2)]
            summed = Signal("summed", turns)
            sum_read = Signal("sum_read", turns + 2)
            C = len(units[0]["scores"])
            probs, probsT, diag, stat = work

            def score_cols(u):
                return bank[:, 2 * (u % 2):2 * (u % 2) + 2, :].rearrange("p b n -> p (b n)")

            def halves(u):
                k = units[u]["keys"]
                return (0, (k + 1) // 2), ((k + 1) // 2, k)

            def turned_cols(h, n):
                return bank[:, 4 + h, 0:n * P]

            def tensor(pe):
                def scores(i, u):
                    if u % U == 0:
                        pe.wait_ge(staged.sem, staged.at(2 * i + (u // U + 1)))
                    if u >= 2:
                        pe.wait_ge(exp_done.sem, exp_done.at(i * N + (u - 1)))
                    S = score_cols(u)
                    for c, score in enumerate(units[u]["scores"]):
                        for lo, hi, pairs in score(2 * i + u // U):
                            for k, (lhsT, rhs) in enumerate(pairs):
                                last = nc.tensor.matmul(S[:, c * 512 + lo:c * 512 + hi], lhsT, rhs,
                                                        start=k == 0, stop=k == len(pairs) - 1)
                    last.then_inc(scored.sem, 1)

                def transposes(i, u):
                    pe.wait_ge(diag_ready.sem, diag_ready.at(i * N + (u + 1)))
                    for h, (lo, hi) in enumerate(halves(u)):
                        if u > 0:
                            pe.wait_ge(probs_out[h].sem, probs_out[h].at(i * N + u))
                        for j in range(lo, hi):
                            for c in range(C):
                                at = c * 512 + j * P
                                last = nc.tensor.matmul(turned_cols(h, hi - lo)[:, (j - lo) * P:(j - lo + 1) * P],
                                                        probs[:, u % 2, at:at + P], diag[:, u % 2, c, :],
                                                        start=c == 0, stop=c == C - 1)
                        last.then_inc(turned[h].sem, 1)

                def values(i, u):
                    t = u // U
                    if u % U == 0:
                        pe.wait_ge(sum_read.sem, sum_read.at(2 * i + (t + (2 if shared_out else 1))))
                    for h in range(2):
                        pe.wait_ge(probs_out[h].sem, probs_out[h].at(i * N + (u + 1)))
                    for out_ap, lhs in units[u]["values"]:
                        for j, lhsT in enumerate(lhs):
                            last = nc.tensor.matmul(out_ap, lhsT, probsT[:, u % 2, j * P:(j + 1) * P],
                                                    start=j == 0, stop=j == len(lhs) - 1)
                    if u % U == U - 1:
                        last.then_inc(summed.sem, 1)

                with pe.Fori(0, passes) as i:
                    scores(i, 0)
                    scores(i, 1)
                    transposes(i, 0)
                    for u in range(N):
                        if u + 2 < N:
                            scores(i, u + 2)
                        if u + 1 < N:
                            transposes(i, u + 1)
                        values(i, u)

            def scalar(act):
                def exps(i, u):
                    act.wait_ge(max_ready.sem, max_ready.at(i * N + (u + 1)))
                    if u >= 2:
                        act.wait_ge(turned[1].sem, turned[1].at(i * N + (u - 1)))
                    S = score_cols(u)
                    w = units[u]["width"]
                    for c in range(C):
                        last = nc.scalar.activation(probs[:, u % 2, c * 512:c * 512 + w], S[:, c * 512:c * 512 + w],
                                                    ACT.Exp, bias=stat[:, u % 2, 1, c:c + 1], scale=scale,
                                                    accum_out=stat[:, u % 2, 2, c:c + 1])
                    last.then_inc(exp_done.sem, 1)

                def out_half(i, u):
                    act.wait_ge(turned[0].sem, turned[0].at(i * N + (u + 1)))
                    n = halves(u)[0][1]
                    nc.scalar.activation(probsT[:, u % 2, 0:n * P], turned_cols(0, n), ACT.Copy)\
                        .then_inc(probs_out[0].sem, 1)

                with act.Fori(0, passes) as i:
                    exps(i, 0)
                    exps(i, 1)
                    out_half(i, 0)
                    for u in range(N):
                        if u + 1 < N:
                            out_half(i, u + 1)
                        if u + 2 < N:
                            exps(i, u + 2)

            def vector(dve):
                def maxima(i, u):
                    dve.wait_ge(scored.sem, scored.at(i * N + (u + 1)))
                    S = score_cols(u)
                    unit = units[u]
                    for lo, mask in unit["masks"]:
                        nc.vector.tensor_tensor(S[:, lo:lo + P], S[:, lo:lo + P], mask, ALU.add)
                    if unit["sink"] is not None:
                        nc.vector.tensor_copy(S[:, unit["sink"]:unit["sink"] + 1], sink(2 * i + u // U, u % U))
                        dve.drain()
                    view = S.rearrange("p (c n) -> p c n", c=2)[:, 0:2, :] if C == 2 else \
                        S[:, 0:unit["width"]].rearrange("p (c n) -> p c n", c=1)
                    nc.vector.tensor_reduce(stat[:, u % 2, 0, 0:C], view, AX.X, ALU.max, negate=True)
                    dve.drain()
                    nc.vector.tensor_scalar(stat[:, u % 2, 1, 0:C], stat[:, u % 2, 0, 0:C], scale, None, ALU.mult)\
                        .then_inc(max_ready.sem, 1)

                def diagonals(i, u):
                    dve.wait_ge(exp_done.sem, exp_done.at(i * N + (u + 1)))
                    nc.vector.reciprocal(stat[:, u % 2, 3, 0:C], stat[:, u % 2, 2, 0:C])
                    dve.drain()
                    if C == 2:
                        nc.vector.tensor_tensor(stat[:, u % 2, 3, 1:2], stat[:, u % 2, 3, 1:2], neg_lam, ALU.mult)
                        dve.drain()
                    for c in range(C):
                        last = nc.vector.tensor_scalar(diag[:, u % 2, c, :], con("ident"), stat[:, u % 2, 3, c:c + 1],
                                                       None, ALU.mult)
                    last.then_inc(diag_ready.sem, 1)

                def out_half(i, u):
                    dve.wait_ge(turned[1].sem, turned[1].at(i * N + (u + 1)))
                    lo, hi = halves(u)[1]
                    nc.vector.tensor_copy(probsT[:, u % 2, lo * P:hi * P], turned_cols(1, hi - lo))\
                        .then_inc(probs_out[1].sem, 1)

                def turn_out(i, t):
                    dve.wait_ge(summed.sem, summed.at(2 * i + (t + 1)))
                    dst, src = read_out(2 * i + t, t)
                    nc.vector.tensor_copy(dst, src).then_inc(sum_read.sem, 1)

                nc.vector.memset(stat[:, :, :, :], 0.0).then_inc(sum_read.sem, 2)
                dve.drain()
                with dve.Fori(0, passes) as i:
                    maxima(i, 0)
                    maxima(i, 1)
                    diagonals(i, 0)
                    out_half(i, 0)
                    for u in range(N):
                        if u + 1 < N:
                            diagonals(i, u + 1)
                        if shared_out and u == U:
                            turn_out(i, 0)
                        if u + 2 < N:
                            maxima(i, u + 2)
                        if u + 1 < N:
                            out_half(i, u + 1)
                        if not shared_out and u == U:
                            turn_out(i, 0)
                    turn_out(i, 1)

            def gpsimd(pool):
                for z in zeros:
                    nc.gpsimd.memset(z, 0.0)
                pool.drain()
                with pool.Fori(0, passes) as i:
                    for t in range(2):
                        if passes > 1:
                            pool.wait_ge(sum_read.sem, sum_read.at(2 * i + (t + 1)))
                        for n, (dst, src) in enumerate(copies(2 * i + t, t)):
                            if n:
                                pool.drain()
                            last = nc.gpsimd.tensor_copy(dst, src)
                        last.then_inc(staged.sem, 1)

            stage(name, tensor=tensor, scalar=scalar, vector=vector, gpsimd=gpsimd)

        def ffn(name, at, h, conv_w, conv_b, func, on_first, gated, work):
            per_turn = RING
            turns, rest = divmod(FT, per_turn)
            pair_done = Signal("pair_done", FT)
            center_ready = Signal("center_ready", FT)
            banks_free = Signal("banks_free", FT + per_turn)
            acted = Signal("acted", FT)
            gated_ready = Signal("gated", FT + 2)
            first_slab = at // SLAB

            def pair(j):
                return [bank[:, 2 * (j % 4) + s, :] for s in range(2)]

            def loop(eng, body, split=None):
                with eng.Fori(0, turns) as it:
                    for j in range(per_turn):
                        if split:
                            split(eng, first_slab, it, j + 1)
                        body(it * per_turn + j, j)
                for j in range(rest):
                    if split:
                        split(eng, first_slab, turns, j + 1)
                    body(turns * per_turn + j, j)

            def tensor(pe):
                def products(n, j, it):
                    out_ap = pair(j)
                    pe.wait_ge(slab_split, ws.count(first_slab, it * per_turn + j) - WHOLE_SLABS)
                    pe.wait_ge(banks_free.sem, banks_free.at(n + 1))
                    for s in range(2):
                        for k in range(KT):
                            w_hi, w_lo = ws.parts((first_slab + j) * SLAB + s * KT + k)
                            x_hi, x_lo = h.part(pe, k)
                            first = nc.tensor.matmul(out_ap[s], w_hi, x_hi, start=k == 0, stop=False)
                            if s == 0 and k == 0:
                                first.then_inc(slab_begun, 1)
                            nc.tensor.matmul(out_ap[s], w_hi, x_lo, start=False, stop=False)
                            last = nc.tensor.matmul(out_ap[s], w_lo, x_hi, start=False, stop=k == KT - 1)
                    last.then_inc(pair_done.sem, 1)

                assert ws.begun == first_slab and not ws.pending
                with pe.Fori(0, turns) as it:
                    for j in range(per_turn):
                        products(it * per_turn + j, j, it)
                for j in range(rest):
                    products(turns * per_turn + j, j, turns)
                ws.begun += FT

            def scalar(act):
                def centers(n, j):
                    act.wait_ge(pair_done.sem, pair_done.at(n + 1))
                    act.wait_ge(gated_ready.sem, gated_ready.at(n + 1))
                    out_ap = pair(j)
                    for s in range(2):
                        col = n + s * FT
                        last = nc.scalar.activation(work[:, j % 2, s, :], out_ap[s], ACT.Identity,
                                                    bias=conv_b(col), scale=conv_w(2 * FT + col))
                    last.then_inc(center_ready.sem, 1)
                    act.wait_ge(banks_free.sem, banks_free.at(n + (1 + per_turn)))
                    s = 0 if on_first else 1
                    nc.scalar.activation(work[:, j % 2, s, :], work[:, j % 2, s, :], func).then_inc(acted.sem, 1)
                ws.round_to(act, first_slab, ws.limit)
                loop(act, centers, ws.round)
                ws.rounded = first_slab + FT + 1

            def vector(dve):
                nc.vector.memset(small[:, 255:256], 0.0).then_inc(banks_free.sem, per_turn)

                def taps(n, j):
                    dve.wait_ge(center_ready.sem, center_ready.at(n + 1))
                    out_ap = pair(j)
                    for lo, tap in ((1, 0), (0, 2)):
                        for s in range(2):
                            col = n + (s * FT + tap * 2 * FT)
                            w = work[:, j % 2, s, lo:lo + T - 1]
                            last = nc.vector.scalar_tensor_tensor(w, out_ap[s][:, 1 - lo:T - lo], conv_w(col), w,
                                                                  ALU.mult, ALU.add)
                        if tap == 0:
                            dve.drain()
                    last.then_inc(banks_free.sem, 1)
                ws.halve_to(dve, first_slab, ws.limit)
                loop(dve, taps, ws.halve)
                ws.halved = first_slab + FT + 1

            def gpsimd(pool):
                def gate(n, j):
                    pool.wait_ge(acted.sem, acted.at(n + 1))
                    nc.gpsimd.tensor_tensor(gated(n), work[:, j % 2, 0, :], work[:, j % 2, 1, :], ALU.mult)\
                        .then_inc(gated_ready.sem, 1)
                nc.gpsimd.memset(small[:, 254:255], 0.0).then_inc(gated_ready.sem, 2)
                loop(pool, gate)

            stage(name, tensor=tensor, scalar=scalar, vector=vector, gpsimd=gpsimd)

        def ffn_down(name, at, x, read_outs):
            places = x.hi.shape[1]
            rounded = Signal("operand_rounded", FT)
            split = Signal("operand_split", FT)
            used = Signal("operand_used", FT)
            sum_done = Signal("tile_done", KT)

            def tensor(pe):
                for k in range(FT):
                    pe.wait_ge(split.sem, split.at(k + 1))
                    parts = x.hi[:, k % places, :], x.lo[:, k, :]
                    for n in range(KT):
                        last = ws.mm(pe, at + k * KT + n, 1, bank[:, n, :], parts, True, k == 0, k == FT - 1)
                        if k == FT - 1:
                            last.then_inc(sum_done.sem, 1)
                    if k < FT - 1:
                        last.then_inc(used.sem, 1)

            def scalar(act):
                def upper(k):
                    if k >= places:
                        act.wait_ge(used.sem, used.at(k - places + 1))
                    nc.scalar.activation(x.hi[:, k % places, :], x.whole[:, k, :], ACT.Copy).then_inc(rounded.sem, 1)
                upper(0)
                upper(1)
                for k in range(FT):
                    if k + 2 < FT:
                        upper(k + 2)
                    ws.round_to(act, (at + k * KT) // SLAB + 1, ws.limit)
                outs(act, "act")

            def vector(dve):
                def lower(k):
                    dve.wait_ge(rounded.sem, rounded.at(k + 1))
                    nc.vector.tensor_tensor(x.lo[:, k, :], x.whole[:, k, :],
                                            x.hi[:, k % places, :].bitcast(F32), ALU.subtract).then_inc(split.sem, 1)
                lower(0)
                lower(1)
                for k in range(FT):
                    if k + 2 < FT:
                        lower(k + 2)
                    ws.halve_to(dve, (at + k * KT) // SLAB + 1, ws.limit)
                outs(dve, "dve")

            def outs(eng, which):
                for n, (engine, read_out) in enumerate(read_outs):
                    if engine == which:
                        eng.wait_ge(sum_done.sem, sum_done.at(n + 1))
                        read_out(eng, bank[:, n, :])

            stage(name, tensor=tensor, scalar=scalar, vector=vector)

        def scan_branch(z, q, v, y, lb, work):
            H = C_HEADS
            DIRS = 2
            o_read = Signal("head_read", H + 1)
            values_staged = Signal("values_staged", H)
            logs_ready = [Signal(f"logs_ready{d}", H) for d in range(DIRS)]
            sums_ready = [Signal(f"sums_ready{d}", H) for d in range(DIRS)]
            keys_exp = [Signal(f"keys_exp{d}", H) for d in range(DIRS)]
            keys_ready = [Signal(f"keys_ready{d}", H) for d in range(DIRS)]
            inter_arg = [Signal(f"inter_arg{d}", H) for d in range(DIRS)]
            inter_exp = [Signal(f"inter_exp{d}", H) for d in range(DIRS)]
            inter_ready = [Signal(f"inter_ready{d}", H) for d in range(DIRS)]
            keys_turned = [Signal(f"keys_turned{d}", H) for d in range(DIRS)]
            keys_out = [Signal(f"keys_out{d}", H) for d in range(DIRS)]
            updates_done = [Signal(f"updates_done{d}", H) for d in range(DIRS)]
            states_ready = [Signal(f"states_ready{d}", H) for d in range(DIRS)]
            arg_ready = [Signal(f"arg_ready{d}", LEVELS * H) for d in range(DIRS)]
            decay_ready = [Signal(f"decay_ready{d}", LEVELS * H) for d in range(DIRS)]
            mixed_ready = [Signal(f"mixed_ready{d}", LEVELS * H) for d in range(DIRS)]
            level_done = [Signal(f"level_done{d}", (LEVELS + 1) * H) for d in range(DIRS)]
            masked_ready = [Signal(f"masked_ready{d}", (LEVELS + 1) * H) for d in range(DIRS)]
            intra_done = [Signal(f"intra_done{d}", (LEVELS + 1 - d) * H) for d in range(DIRS)]
            head_done = Signal("head_done", H)
            order = [list(range(CB + TB)), [1, 0] + list(range(CB + TB - 1, CB - 1, -1))]
            t_half, j_half = [1, 0], [0, 1]
            sums, keys, t1, t2 = (work[n] for n in ("sums", "keys", "t1", "t2"))
            mixed, masked = work["mixed"], work["masked"]
            keys_n, states = work["keys_n"], work["states"]
            NB = CB + TB
            queries, vh, tot = work["queries"], work["vh"], work["tot"]
            qh, lbh = work["qh"], tot[:, 0, 0, NB:NB + 1]
            O = bank[:, 0, :]
            turn_bank = bank[:, 3:5, :].rearrange("p b n -> p (b n)")
            update_bank = bank[:, 5:7, :].rearrange("p b n -> p (b n)")

            def head(ap, i):
                return ap[:, bass.ds(i, 1), :].rearrange("p o n -> p (o n)")

            def zed(i, d):
                return z[:, d, bass.ds(i, 1), :].rearrange("p o n -> p (o n)")

            def lb_col(which, i, d):
                return lb[:, which, bass.ds(i + d * H, 1)]

            def split(ap, m):
                return ap.rearrange("p (b h m) -> p b h m", h=2, m=m)

            def scalar(act):
                nc.scalar.activation(tot[:, 0, 0, 0:1], con("one", 1), ACT.Copy).then_inc(o_read.sem, 1)
                with act.Fori(0, H) as i:
                    act.wait_ge(o_read.sem, o_read.at(i + 1))
                    for d in range(DIRS):
                        nc.scalar.activation(t1[:, d, :], zed(i, d), ACT.Abs)
                        nc.scalar.activation(t2[:, d, :], zed(i, d), ACT.Exp, scale=-1.0)
                        act.drain()
                        nc.scalar.activation(t1[:, d, :], t1[:, d, :], ACT.Exp, scale=-1.0)
                        nc.scalar.activation(t2[:, d, :], t2[:, d, :], ACT.Ln, bias=con("one", 1), scale=lb_col(0, i, d))
                        act.drain()
                        nc.scalar.activation(t1[:, d, :], t1[:, d, :], ACT.Ln, bias=con("one", 1))\
                            .then_inc(logs_ready[d].sem, 1)
                    for d in range(DIRS):
                        act.wait_ge(sums_ready[d].sem, sums_ready[d].at(i + 1))
                        nc.scalar.activation(keys[:, d, :], keys[:, d, :], ACT.Exp, scale=-1.0)\
                            .then_inc(keys_exp[d].sem, 1)
                    for d in range(DIRS):
                        act.wait_ge(inter_arg[d].sem, inter_arg[d].at(i + 1))
                        nc.scalar.activation(t1[:, d, :], t1[:, d, :], ACT.Exp)
                        nc.scalar.activation(tot[:, d, 1, 0:NB], tot[:, d, 0, 0:NB], ACT.Exp)
                        nc.scalar.activation(queries[:, d, :], queries[:, d, :], ACT.Exp).then_inc(inter_exp[d].sem, 1)
                    for d in range(DIRS):
                        act.wait_ge(keys_turned[d].sem, keys_turned[d].at(i + 1))
                        nc.scalar.activation(keys_n[:, d, :, :].rearrange("p b n -> p (b n)"), turn_bank[:, 0:NB * P],
                                             ACT.Copy).then_inc(keys_out[d].sem, 1)
                    for l in range(LEVELS):
                        for d in range(DIRS):
                            act.wait_ge(arg_ready[d].sem, arg_ready[d].at(i * LEVELS + (l + 1)))
                            nc.scalar.activation(mixed[:, d, l % 2, :], mixed[:, d, l % 2, :], ACT.Exp)\
                                .then_inc(decay_ready[d].sem, 1)
                    act.wait_ge(head_done.sem, head_done.at(i + 1))
                    nc.scalar.activation(head(y, i), O, ACT.Copy).then_inc(o_read.sem, 1)

            def direction(eng, ops, d, i, q_head, lb_head):
                near, far = (1, 0) if d == 0 else (0, 1)
                edge = CHUNK - 1 if d == 0 else 0
                lat = sums[:, d, CT:ALLT]

                def inter_args():
                    a = split(sums[:, d, :], CHUNK)
                    tn, tf = a[:, :, near, edge:edge + 1], a[:, :, far, edge:edge + 1]
                    both = tot[:, d, 0, 0:NB].rearrange("p (b o) -> p b o", o=1)
                    ops.tensor_tensor(both, tn, tf, ALU.add)
                    k = split(t1[:, d, :], CHUNK)
                    ops.tensor_tensor(k[:, :, near, :], tn.to_broadcast([P, NB, CHUNK]), a[:, :, near, :], ALU.subtract)
                    qx, al = split(queries[:, d, :], CHUNK), split(lat, CHUNK)
                    ops.tensor_copy(qx[:, :, far, :], al[:, :, far, :])
                    ops.tensor_tensor(qx[:, :, near, :], al[:, :, near, :],
                                      al[:, :, far, edge:edge + 1].to_broadcast([P, TB, CHUNK]), ALU.add)
                    eng.drain()
                    ops.tensor_tensor(k[:, :, far, :], both.to_broadcast([P, NB, CHUNK]), a[:, :, far, :], ALU.subtract)\
                        .then_inc(inter_arg[d].sem, 1)

                def keys_scaled():
                    eng.wait_ge(keys_exp[d].sem, keys_exp[d].at(i + 1))
                    ops.tensor_tensor(keys[:, d, :], keys[:, d, :], lb_head.to_broadcast([P, ALLT]), ALU.mult)\
                        .then_inc(keys_ready[d].sem, 1)
                    eng.drain()

                def inter_products():
                    eng.wait_ge(inter_exp[d].sem, inter_exp[d].at(i + 1))
                    ops.tensor_tensor(t1[:, d, :], t1[:, d, :], keys[:, d, :], ALU.mult)
                    ops.tensor_tensor(queries[:, d, :], queries[:, d, :], q_head, ALU.mult)\
                        .then_inc(inter_ready[d].sem, 1)

                def args(l):
                    m = CHUNK >> l
                    nb = T // (2 * m)
                    if l >= 2:
                        eng.wait_ge(level_done[d].sem, level_done[d].at(i * (LEVELS + 1) + (l - 1)))
                    a, x = split(lat, m), split(mixed[:, d, l % 2, :], m)
                    e = m - 1 if d == 0 else 0
                    ref = a[:, :, j_half[d], e:e + 1].to_broadcast([P, nb, m])
                    ops.tensor_tensor(x[:, :, j_half[d], :], ref, a[:, :, j_half[d], :], ALU.subtract)
                    if l == 0:
                        last = ops.tensor_copy(x[:, :, t_half[d], :], a[:, :, t_half[d], :])
                    else:
                        last = ops.tensor_tensor(x[:, :, t_half[d], :], a[:, :, t_half[d], :], ref, ALU.subtract)
                    last.then_inc(arg_ready[d].sem, 1)

                def products(l):
                    m = CHUNK >> l
                    eng.wait_ge(decay_ready[d].sem, decay_ready[d].at(i * LEVELS + (l + 1)))
                    x = split(mixed[:, d, l % 2, :], m)
                    ops.tensor_tensor(x[:, :, t_half[d], :], x[:, :, t_half[d], :],
                                      split(q_head, m)[:, :, t_half[d], :], ALU.mult)
                    ops.tensor_tensor(x[:, :, j_half[d], :], x[:, :, j_half[d], :],
                                      split(keys[:, d, CT:ALLT], m)[:, :, j_half[d], :], ALU.mult)\
                        .then_inc(mixed_ready[d].sem, 1)
                return inter_args, keys_scaled, inter_products, args, products

            def vector(dve):
                with dve.Fori(0, H) as i:
                    dve.wait_ge(o_read.sem, o_read.at(i + 1))
                    inter_args, keys_scaled, inter_products, args, products = direction(dve, nc.vector, 0, i, head(q, i),
                                                                                       lb_col(1, i, 0))
                    for d in range(DIRS):
                        dve.wait_ge(logs_ready[d].sem, logs_ready[d].at(i + 1))
                        nc.vector.scalar_tensor_tensor(keys[:, d, :], zed(i, d), 0.0, t1[:, d, :], ALU.max, ALU.add)
                        dve.drain()
                        nc.vector.scalar_tensor_tensor(t1[:, d, :], zed(i, d), 0.0, t1[:, d, :], ALU.min, ALU.subtract)
                        dve.drain()
                        nc.vector.tensor_tensor(t2[:, d, :], t1[:, d, :], t2[:, d, :], ALU.add)
                        dve.drain()
                        step = 1 if d == 0 else -1
                        nc.vector.tensor_tensor_scan(sums[:, d, ::step], con("reset", ALLT, d * ALLT)[:, ::step],
                                                     t2[:, d, ::step], 0.0, ALU.mult, ALU.add)\
                            .then_inc(sums_ready[d].sem, 1)
                    dve.drain()
                    inter_args()
                    args(0)
                    args(1)
                    keys_scaled()
                    inter_products()
                    for d in range(DIRS):
                        dve.wait_ge(updates_done[d].sem, updates_done[d].at(i + 1))
                        U = update_bank
                        first = order[d][0]
                        nc.vector.tensor_copy(states[:, d, 1, :], U[:, first * P:(first + 1) * P])
                        for n in range(1, NB - 1):
                            b = order[d][n]
                            dve.drain()
                            last = nc.vector.scalar_tensor_tensor(states[:, d, n + 1, :], states[:, d, n, :],
                                                                  tot[:, d, 1, b:b + 1], U[:, b * P:(b + 1) * P],
                                                                  ALU.mult, ALU.add)
                        last.then_inc(states_ready[d].sem, 1)

                    def masks(l):
                        for d in range(DIRS):
                            dve.wait_ge(level_done[d].sem, level_done[d].at(i * (LEVELS + 1) + (l + 1)))
                            if l >= 2:
                                dve.wait_ge(intra_done[d].sem, intra_done[d].at(i * (LEVELS + 1 - d) + (l - 1)))
                            mask = con("levels", P, (d * (LEVELS + 1) + l) * P).rearrange("p (o n) -> p o n", o=1)
                            nc.vector.tensor_tensor(masked[:, d, l % 2, :].rearrange("p (b n) -> p b n", n=P),
                                                    bank[:, 1 + d, :].rearrange("p (b n) -> p b n", n=P),
                                                    mask.to_broadcast([P, TB, P]), ALU.mult)\
                                .then_inc(masked_ready[d].sem, 1)
                    for l in range(LEVELS):
                        products(l)
                        if l >= 1:
                            masks(l - 1)
                        if l + 2 < LEVELS:
                            args(l + 2)
                    masks(LEVELS - 1)
                    masks(LEVELS)

            def gpsimd(pool):
                with pool.Fori(0, H) as i:
                    pool.wait_ge(o_read.sem, o_read.at(i + 1))
                    inter_args, keys_scaled, inter_products, args, products = direction(pool, nc.gpsimd, 1, i, qh, lbh)
                    nc.gpsimd.tensor_copy(vh[:, :, :], v[:, :, bass.ds(i, 1), :].rearrange("p b o n -> p b (o n)"))\
                        .then_inc(values_staged.sem, 1)
                    nc.gpsimd.tensor_copy(qh, head(q, i))
                    nc.gpsimd.tensor_copy(lbh, lb_col(1, i, 1))
                    pool.drain()
                    pool.wait_ge(sums_ready[1].sem, sums_ready[1].at(i + 1))
                    inter_args()
                    args(0)
                    args(1)
                    keys_scaled()
                    inter_products()
                    for l in range(LEVELS):
                        products(l)
                        if l + 2 < LEVELS:
                            args(l + 2)

            def tensor(pe):
                with pe.Fori(0, H) as i:
                    pe.wait_ge(o_read.sem, o_read.at(i + 1))
                    pe.wait_ge(values_staged.sem, values_staged.at(i + 1))
                    for d in range(DIRS):
                        pe.wait_ge(inter_ready[d].sem, inter_ready[d].at(i + 1))
                        if d == 1:
                            pe.wait_ge(keys_out[0].sem, keys_out[0].at(i + 1))
                        for b in range(NB):
                            last = nc.tensor.transpose(turn_bank[:, b * P:(b + 1) * P], t1[:, d, b * P:(b + 1) * P],
                                                       con("ident"))
                        last.then_inc(keys_turned[d].sem, 1)
                    for d in range(DIRS):
                        pe.wait_ge(keys_out[d].sem, keys_out[d].at(i + 1))
                        if d == 1:
                            pe.wait_ge(states_ready[0].sem, states_ready[0].at(i + 1))
                        for b in order[d][0:NB - 1]:
                            last = nc.tensor.matmul(update_bank[:, b * P:(b + 1) * P], keys_n[:, d, b, :], vh[:, b, :],
                                                    start=True, stop=True)
                        last.then_inc(updates_done[d].sem, 1)
                    for d in range(DIRS):
                        pe.wait_ge(states_ready[d].sem, states_ready[d].at(i + 1))
                        for n in range(CB, NB):
                            b = order[d][n] - CB
                            nc.tensor.matmul(O[:, b * P:(b + 1) * P], states[:, d, n, :], queries[:, d, b * P:(b + 1) * P],
                                             start=d == 0 and n == CB, stop=False, skip_group_check=True)

                    def level(l):
                        for d in range(DIRS):
                            if l >= 1:
                                pe.wait_ge(masked_ready[d].sem, masked_ready[d].at(i * (LEVELS + 1) + l))
                            if l < LEVELS:
                                pe.wait_ge(mixed_ready[d].sem, mixed_ready[d].at(i * LEVELS + (l + 1)))
                            else:
                                pe.wait_ge(keys_ready[d].sem, keys_ready[d].at(i + 1))
                            for b in range(TB):
                                c = slice(b * P, (b + 1) * P)
                                if l < LEVELS:
                                    lhsT = rhs = mixed[:, d, l % 2, c]
                                else:
                                    lhsT = keys[:, d, CT + b * P:CT + (b + 1) * P]
                                    rhs = q[:, bass.ds(i, 1), c].rearrange("p o n -> p (o n)")
                                last = nc.tensor.matmul(bank[:, 1 + d, c], lhsT, rhs, start=True, stop=True)
                            last.then_inc(level_done[d].sem, 1)

                    def intra(l):
                        for d in range(DIRS):
                            pe.wait_ge(masked_ready[d].sem, masked_ready[d].at(i * (LEVELS + 1) + (l + 1)))
                            for b in range(TB):
                                c = slice(b * P, (b + 1) * P)
                                end = l == LEVELS and d == 1 and b == TB - 1
                                last = nc.tensor.matmul(O[:, c], vh[:, CB + b, :], masked[:, d, l % 2, c], start=False,
                                                        stop=end, skip_group_check=True)
                            last.then_inc((head_done if end else intra_done[d]).sem, 1)
                    level(0)
                    for l in range(LEVELS):
                        level(l + 1)
                        intra(l)
                    intra(LEVELS)

            stage("scan", tensor=tensor, scalar=scalar, vector=vector, gpsimd=gpsimd)

        inputs_loaded = Signal("inputs_loaded", 16 * 4)
        tables = sb("tables", [P, 4, T])
        COS_MLA, SIN_MLA, COS_DIFF, SIN_DIFF = (tables[:, n, :] for n in range(4))

        phase = stack.enter_context(ExitStack())

        def tmp(name, shape, where=None, dt=F32):
            return new(where or phase, name, shape, dt)

        yc = tmp("yc", [P, 4, T])
        yc_lo = same_place("yc_lo", "yc", [P, 4, T], F32R)
        hcT = tmp("hcT", [P, KT, CT])
        hc_lo = same_place("hc_lo", "hcT", [P, KT, CT], F32R)
        hc_hi = tmp("hc_hi", [P, KT, CT], None, F32R)
        mod = tmp("mod", [P, MOD_TILES, 2])
        gain_x = tmp("gain_x", [P, KT, 2])
        gain_f = tmp("gain_f", [P, KT])
        sc = tmp("sc", [P, KT, 2])
        lb = tmp("lb", [P, 2, 2 * C_HEADS])
        sink8 = tmp("sink8", [P, 8])

        with ExitStack() as here:
            pos_i = tmp("pos_i", [P, T], here, I32)
            ang = tmp("ang", [P, 4, T], here)
            scr = tmp("scr", [P, 4, 2 * C_HEADS], here)
            c_ready = Signal("c_ready", 1)
            mod_done = Signal("mod_done", 1)
            lb_sub = Signal("lb_sub", 1)
            lb_exp = Signal("lb_exp", 1)
            angles_ready = Signal("angles_ready", 1)
            abs_ready = Signal("abs_ready", 1)
            mod_ready = Signal("mod_ready", 1)

            def sync(sp):
                sp.dma_start(par1[:, :], par1_in).then_inc(inputs_loaded.sem, 16)
                ws.feed(sp, RING)
                sp.dma_start(const[:, :], const_in).then_inc(inputs_loaded.sem, 16)
                sp.dma_start(xT[:, :, :], xT_in).then_inc(inputs_loaded.sem, 16)
                sp.dma_start(pos_i[:, :], pos_in.to_broadcast([P, T])).then_inc(inputs_loaded.sem, 16)

            def scalar(act):
                act.wait_ge(inputs_loaded.sem, 16 * 4)
                nc.scalar.activation(sc[:, :, :].rearrange("p k s -> p (k s)"), p1("c", 2 * KT), ACT.Silu)\
                    .then_inc(c_ready.sem, 1)
                act.wait_ge(lb_sub.sem, lb_sub.at(1))
                nc.scalar.activation(scr[:, 1, :], scr[:, 0, :], ACT.Exp).then_inc(lb_exp.sem, 1)
                act.wait_ge(angles_ready.sem, angles_ready.at(1))
                for n in range(2):
                    nc.scalar.activation(ang[:, 2 + n, :], ang[:, n, :], ACT.Abs)
                act.drain()
                for n in range(2):
                    nc.scalar.activation(tables[:, 2 * n + 1, :], ang[:, n, :], ACT.Sin)
                    nc.scalar.activation(tables[:, 2 * n, :], ang[:, 2 + n, :], ACT.Sin, bias=con("half_pi", 1), scale=-1.0)
                act.drain()

            def tensor(pe):
                pe.wait_ge(c_ready.sem, c_ready.at(1))
                for n in range(MOD_TILES):
                    for k in range(KT):
                        b = B1_AT["mod"] + n * KT + k
                        last = ws.mm_whole(pe, b, bank[:, 0, 2 * n:2 * n + 2], sc[:, k, :], k == 0, k == KT - 1)
                last.then_inc(mod_done.sem, 1)

            def vector(dve):
                dve.wait_ge(inputs_loaded.sem, 16 * 4)
                nc.vector.tensor_tensor(scr[:, 0, :], p1("lb", 8), p1("lb", 8), ALU.subtract).then_inc(lb_sub.sem, 1)
                nc.vector.tensor_scalar(sink8[:, :], p1("sink", 8), float(HD) ** 0.5, None, ALU.mult)
                nc.vector.tensor_copy(ang[:, 3, :], pos_i[:, :])
                dve.drain()
                two_pi = 2 * np.pi
                parts, left = [], two_pi
                for bits in (7, 15):
                    part = np.floor(left * 2.0 ** bits) / 2.0 ** bits
                    parts.append(float(np.float32(part)))
                    left -= parts[-1]
                parts.append(float(np.float32(left)))
                magic = 1.5 * 2.0 ** 23
                for n in (0, 1):
                    a, r = ang[:, n, :], ang[:, 2, :]
                    nc.vector.tensor_scalar(a, ang[:, 3, :], con("freq", 1, n), None, ALU.mult)
                    dve.drain()
                    nc.vector.tensor_scalar(r, a, 1.0 / two_pi, magic, ALU.mult, ALU.add)
                    dve.drain()
                    nc.vector.tensor_scalar(r, r, magic, None, ALU.subtract)
                    dve.drain()
                    for part in parts:
                        nc.vector.scalar_tensor_tensor(a, r, -part, a, ALU.mult, ALU.add)
                        dve.drain()
                    last = nc.vector.tensor_scalar(a, a, -3.1415925, 3.1415925, ALU.max, ALU.min)
                    dve.drain()
                nc.vector.tensor_copy(ang[:, 2, 0:1], ang[:, 0, 0:1]).then_inc(angles_ready.sem, 1)
                dve.wait_ge(lb_exp.sem, lb_exp.at(1))
                nc.vector.reciprocal(scr[:, 2, :], scr[:, 1, :])
                dve.drain()
                nc.vector.tensor_tensor(scr[:, 1, :], scr[:, 1, :], scr[:, 2, :], ALU.mult)
                dve.drain()
                nc.vector.tensor_tensor(scr[:, 2, :], scr[:, 1, :], scr[:, 1, :], ALU.subtract)
                dve.drain()
                nc.vector.tensor_scalar(lb[:, 0, :], scr[:, 2, :], 0.0, 1.0, ALU.max, ALU.min)
                dve.drain()
                nc.vector.tensor_scalar(lb[:, 1, :], lb[:, 0, :], -1.0, 1.0, ALU.mult, ALU.add)
                dve.wait_ge(mod_done.sem, mod_done.at(1))
                nc.vector.tensor_tensor(mod[:, :, :], bank[:, 0, 0:2 * MOD_TILES].rearrange("p (n s) -> p n s", s=2),
                                        bcast(p1("b_mod", MOD_TILES), 2), ALU.add)
                dve.drain()
                nc.vector.scalar_tensor_tensor(gain_x[:, :, :], mod[:, KT:2 * KT, :], 1.0, bcast(p1("norm_mix", KT), 2),
                                               ALU.add, ALU.mult)
                nc.vector.scalar_tensor_tensor(gain_f[:, :], mod[:, 4 * KT:5 * KT, 0], 1.0, p1("norm_ffn", KT),
                                               ALU.add, ALU.mult).then_inc(mod_ready.sem, 1)

            stage("modulation", tensor=tensor, scalar=scalar, vector=vector, sync=sync)

        branches = stack.enter_context(ExitStack())
        with ExitStack() as norm_scope:
            ctxT = tmp("ctxT", [P, KT, CT], norm_scope)
            squares = tmp("squares1", [P, SQUARES, T], norm_scope)
            scales = tmp("scales1", [P, 2, T], norm_scope)
            ctx_in = Signal("context_loaded", 16)

            def sync(sp):
                sp.dma_start(ctxT[:, :, :], ctxT_in).then_inc(ctx_in.sem, 16)
                sp.wait_ge(ctx_in.sem, ctx_in.at(16))
            stage("load_context", sync=sync)
            norms("norm_mix", [
                dict(src=lambda k: xT[:, k, :], tiles=KT, cols=T, ones=con("ones"), inv=1.0 / D,
                     gain=lambda k: gain_x[:, k, 0:1], out=lambda k: hT[:, k, :],
                     end=("split", split_hi, split_lo, lambda k: mod[:, k, 0:1])),
                dict(src=lambda k: ctxT[:, k, :], tiles=KT, cols=CT, ones=con("ones"), inv=1.0 / D,
                     gain=lambda k: gain_x[:, k, 1:2], out=lambda k: hcT[:, k, :],
                     end=("split", lambda k: hc_hi[:, k, :], lambda k: hc_lo[:, k, :], lambda k: mod[:, k, 1:2]))], squares, scales)
        hc = Split(hc_hi, hc_lo)

        def tokens(tb):
            x, at = (hc, tb) if tb < CB else (h, tb - CB)
            return lambda pe, k: x.part(pe, k, slice(at * P, (at + 1) * P))

        def attend(which, b, windowed, sync=None):
            at = B1_AT[which]
            with ExitStack() as s:
                qk = tmp(f"qk{which}", [P, 4, T], s)
                k = tmp(f"k{which}", [P, ALLT], s)
                v = tmp(f"v{which}", [P, CB + TB, P], s)
                tiles = [("act", T, weights_still(at + n * KT, KT, h), act_copy(qk[:, n, :])) for n in range(4)]
                tiles.append(("act", T, weights_still(at + 4 * KT, KT, h), act_copy(k[:, CT:ALLT])))
                tiles.append(("act", CT, weights_still(at + 4 * KT, KT, hc), act_copy(k[:, 0:CT])))
                values = weights_moving(at + 5 * KT, KT, 1, [tokens(tb) for tb in range(CB + TB)])
                for tb in range(CB + TB):
                    tiles.append(("dve", P, values, dve_copy(v[:, tb, :])))
                linear(f"proj{which}", tiles, sync=sync)
                if not windowed:
                    with ExitStack() as n:
                        squares = tmp("squaresB", [P, SQUARES, T], n)
                        scales = tmp("scalesB", [P, 2, T], n)
                        jobs = [(qk[:, m, :], T, "qn") for m in range(4)] + \
                            [(k[:, CT:ALLT], T, "kn"), (k[:, 0:CT], CT, "kn")]
                        norms("norm_heads", [
                            dict(src=lambda kt, ap=ap: ap, tiles=1, cols=cols, ones=con("ones64"), inv=1.0 / HD,
                                 gain=lambda kt, g=g: p1(g), out=lambda kt, ap=ap: ap, end=None)
                            for ap, cols, g in jobs], squares, scales)
                with ExitStack() as r:
                    work = tmp(f"rope{which}", [P, 4, T], r)
                    rope(f"rope{which}", [(ap, con("rot1"), axial[:, 0, :], axial[:, 1, :], ap)
                                          for ap in [qk[:, m, :] for m in range(4)] + [k[:, CT:ALLT]]], work)
                with ExitStack() as a:
                    qpad = tmp(f"qpad{which}", [P, 2, 2, T], a)
                    work = (tmp(f"probs{which}", [P, 2, 1024], a), tmp(f"probsT{which}", [P, 2, ALLT], a),
                            tmp(f"diag{which}", [P, 2, 1, P], a), tmp(f"stat{which}", [P, 2, 4, 2], a))
                    units = [[], []]
                    for t, g in ((t, g) for t in range(2) for g in range(2)):
                        for tb in range(TB):
                            lo, hi = (max(0, tb - 1), min(TB, tb + 2)) if windowed else (0, TB)
                            width = CT + (hi - lo) * P
                            key_cols = [(0, CT, 0), (CT, min(width, 512), CT + lo * P)]
                            if width > 512:
                                key_cols.append((512, width, 512 + lo * P))
                            qs = qpad[:, t, g, tb * P:(tb + 1) * P]
                            masks = []
                            if windowed and lo < tb:
                                masks.append((CT, con("mask_prev")))
                            if windowed and hi > tb + 1:
                                masks.append((width - P, con("mask_next")))
                            blocks = list(range(CB)) + [CB + x for x in range(lo, hi)]
                            units[t].append(dict(
                                scores=[lambda i, qs=qs, kc=key_cols: [(a0, a1, [(qs, k[:, s0:s0 + a1 - a0])])
                                                                       for a0, a1, s0 in kc]],
                                width=width + (1 if windowed else 0), masks=masks,
                                sink=width if windowed else None, group=g, keys=width // P,
                                values=[(bank[g * HD:(g + 1) * HD, 6 + t, tb * P:(tb + 1) * P],
                                         [v[:, x, g * HD:(g + 1) * HD] for x in blocks])]))

                    def copies(i, t):
                        return [(qpad[g * HD:(g + 1) * HD, t, g, :],
                                 qk[g * HD:(g + 1) * HD, bass.ds(i, 1), :].rearrange("p o n -> p (o n)"))
                                for g in range(2)]
                    attention(f"attend{which}", 4, units, HD ** -0.5, copies,
                              [qpad[HD:P, :, 0, :], qpad[0:HD, :, 1, :]],
                              lambda i, t: (yab[:, b, bass.ds(i, 1), :].rearrange("p o n -> p (o n)"), bank[:, 6 + t, :]),
                              work, sink=lambda i, u: sink8[:, bass.ds(i + 4 * units[0][u]["group"], 1)])

        h = Split(h_hi, h_lo)
        with ExitStack() as s:
            z = tmp("z", [P, 2, C_HEADS, ALLT], s)
            cq = tmp("cq", [P, C_HEADS, T], s)
            v = tmp("vC", [P, CB + TB, C_HEADS, P], s)
            at = B1_AT["C"]
            tiles = [("act", T, weights_still(at + n * KT, KT, h), act_copy(cq[:, n, :], ACT.Silu)) for n in range(C_HEADS)]
            for d in range(2):
                for n in range(C_HEADS):
                    b = at + (4 + 4 * d + n) * KT
                    tiles.append(("act", T, weights_still(b, KT, h), act_copy(z[:, d, n, CT:ALLT])))
                    tiles.append(("act", CT, weights_still(b, KT, hc), act_copy(z[:, d, n, 0:CT])))
            values = weights_moving(at + 12 * KT, KT, 4, [tokens(tb) for tb in range(CB + TB)])
            for tb in range(CB + TB):
                tiles.append(("dve", 512, values, dve_copy(v[:, tb, :, :].rearrange("p h n -> p (h n)"))))
            linear("projC", tiles, last_split=B1_AT["A"] // SLAB)
            work = {n: tmp(f"scan_{n}", [P, 2, ALLT], s) for n in ("sums", "keys", "t1", "t2")}
            work["vh"] = tmp("scan_vh", [P, CB + TB, P], s)
            work["tot"] = tmp("scan_tot", [P, 2, 2, 8], s)
            spare = ring_spare
            size = 2 * (CB + TB) * P
            work["keys_n"], work["states"] = (spare[:, m * size:(m + 1) * size].rearrange("p (d b n) -> p d b n", d=2, n=P)
                                              for m in range(2))
            work["qh"] = spare[:, 2 * size:2 * size + T]
            work["mixed"] = xT[:, 0:KT // 2, :].rearrange("p (d n) t -> p d n t", d=2)
            work["masked"] = xT[:, KT // 2:KT, :].rearrange("p (d n) t -> p d n t", d=2)
            work["queries"] = work["t2"][:, :, 0:T]
            scan_branch(z, cq, v, yc, lb, work)

        yab = tmp("yab", [P, 2, 4, T], branches)
        yab_lo = same_place("yab_lo", "yab", [P, 2, 4, T], F32R)
        axial = tmp("axial", [P, 2, T], branches)
        x_again = Signal("x_loaded", 32)

        def load_x(sp):
            sp.dma_start(axial[:, :, :], axial_in).then_inc(x_again.sem, 16)
            sp.dma_start(xT[:, :, :], xT_in).then_inc(x_again.sem, 16)
            sp.wait_ge(x_again.sem, x_again.at(32))
        attend("A", 0, True, load_x)
        attend("B", 1, False)

        with ExitStack() as here:
            cg = tmp("cg", [P, C_HEADS, T], here)
            squares = tmp("squaresC", [P, SQUARES, T], here)
            scales = tmp("scalesC", [P, 2, T], here)
            linear("gate_c", [("act", T, weights_still(B1_AT["cg"] + n * KT, KT, h), act_copy(cg[:, n, :], ACT.Silu))
                              for n in range(C_HEADS)])
            norms("norm_c", [dict(src=lambda k, n=n: yc[:, n, :], tiles=1, cols=T, ones=con("ones"), inv=1.0 / P,
                                  gain=lambda k: p1("gn"), out=lambda k, n=n: yc[:, n, :],
                                  end=("times", lambda k, n=n: cg[:, n, :])) for n in range(C_HEADS)],
                  squares, scales)
        with ExitStack() as here:
            merged = tmp("merged", [P, KT, T], here)
            gates = tmp("gates", [P, 6, T], here)
            part = tmp("part", [P, 2, T], here)
            yb_hi = tmp("yb_hi", [P, 4, T], here, F32R)
            old = [x[:, :, :].rearrange("p (k a) c -> p k (a c)", a=2) for x in (hc_hi, hc_lo)]
            ys = [Split(old[0], yab_lo[:, 0, :, :], yab[:, 0, :, :]), Split(yb_hi, yab_lo[:, 1, :, :], yab[:, 1, :, :]),
                  Split(old[1], yc_lo, yc)]
            tiles = []

            def add_branch(n, b):
                def read_out(dve, ps):
                    g = gates[:, (3 * n + b) % 6, :]
                    if b == 0:
                        return nc.vector.tensor_tensor(merged[:, n, :], ps, g, ALU.mult)
                    nc.vector.tensor_tensor(part[:, b % 2, :], ps, g, ALU.mult)
                    dve.drain()
                    return nc.vector.tensor_tensor(merged[:, n, :], merged[:, n, :], part[:, b % 2, :], ALU.add)
                return read_out
            for n in range(KT):
                for b in range(3):
                    at = B1_AT["merge"] + (3 * n + b) * (KT + 4)
                    tiles.append(("act", T, weights_still(at, KT, h), act_copy(gates[:, (3 * n + b) % 6, :], ACT.Sigmoid)))
                    tiles.append(("dve", T, weights_still(at + KT, 4, ys[b]), add_branch(n, b), len(tiles) - 1))
            linear("merge", tiles, operands=ys)

            def residual(n):
                return lambda dve, ps: nc.vector.scalar_tensor_tensor(xT[:, n, :], ps, mod[:, 2 * KT + n, 0:1],
                                                                      xT[:, n, :], ALU.mult, ALU.add)
            merged_parts = Split(h_hi, same_place("merged_lo", "merged", [P, KT, T], F32R), merged)
            linear("out", [("dve", T, weights_still(B1_AT["out"] + n * KT, KT, merged_parts), residual(n)) for n in range(KT)],
                   operands=[merged_parts])
        branches.close()

        def up_down(which, at, func, on_first, conv_w, conv_b, down_out, work=None):
            with ExitStack() as here:
                gated = tmp(f"gated{which}", [P, FT, T], here)
                if work is None:
                    work = tmp(f"conv{which}", [P, 2, 2, T], here)
                ffn(f"up{which}", at["up"], Split(h_hi, h_lo), conv_w, conv_b, func, on_first,
                    lambda n: gated[:, bass.ds(n, 1), :].rearrange("p o n -> p (o n)") if not isinstance(n, int)
                    else gated[:, n, :], work)
                ffn_down(f"down{which}", at["down"], Split(h_hi, same_place(f"gated_lo{which}", f"gated{which}", [P, FT, T], F32R), gated),
                         [down_out(n) for n in range(KT)])

        def col(table, start):
            return lambda n: table[:, bass.ds(n + start, 1)] if not isinstance(n, int) else table[:, n + start:n + start + 1]

        with ExitStack() as here:
            squares = tmp("squaresF", [P, SQUARES, T], here)
            scales = tmp("scalesF", [P, 2, T], here)
            norms("norm_ffn", [dict(src=lambda k: xT[:, k, :], tiles=KT, cols=T, ones=con("ones"), inv=1.0 / D,
                                    gain=lambda k: gain_f[:, k:k + 1], out=lambda k: hT[:, k, :],
                                    end=("split", split_hi, split_lo, lambda k: mod[:, 3 * KT + k, 0:1]))], squares, scales)
        up_down("1", B1_AT, ACT.Silu, False, col(par1, PAR1["conv_w"]), col(par1, PAR1["conv_b"]),
                lambda n: ("dve", lambda dve, ps: nc.vector.scalar_tensor_tensor(
                    xT[:, n, :], ps, mod[:, 5 * KT + n, 0:1], xT[:, n, :], ALU.mult, ALU.add)))
        phase.close()

        phase = stack.enter_context(ExitStack())
        par2 = tmp("par2", [P, PAR2_W], phase)
        mix = tmp("mix", [P, KT, T], phase)
        mix_lo = same_place("mix_lo", "mix", [P, KT, T], F32R)
        raw = tmp("raw", [P, KT, T], phase)
        squares2 = tmp("squares2", [P, SQUARES, T], phase)
        scales2 = tmp("scales2", [P, 2, T], phase)
        lam = tmp("lam", [P, 2, 32], phase)
        lam_s = tmp("lam_s", [P, 8], phase)

        def p2(name, n=1, at=0):
            return par2[:, PAR2[name] + at:PAR2[name] + at + n]

        def one_norm(name, src, gain, out, tiles=KT, cols=T, ones="ones", width=D, end=None):
            return dict(src=src, tiles=tiles, cols=cols, ones=con(ones), inv=1.0 / width, gain=gain, out=out, end=end)

        norms("norm_final", [one_norm("x", lambda k: xT[:, k, :], lambda k: p1("norm_final", 1, k), lambda k: xT[:, k, :])],
              squares2, scales2)

        def layer_body(l):
            params_loaded = Signal("params_loaded", 16)
            lam_dots = Signal("lam_dots", 1)
            lam_exp = Signal("lam_exp", 1)
            neg_lam, gain_sub = lam_s[:, 4:5], lam_s[:, 5:6]

            def sync(sp):
                sp.dma_start(par2[:, :], par2_in[bass.ds(l, 1)].rearrange("o p n -> p (o n)")).then_inc(params_loaded.sem, 16)

            def vector(dve):
                dve.wait_ge(params_loaded.sem, params_loaded.at(16))
                v = p2("lam", 128).rearrange("p (a s n) -> p a s n", a=2, s=2)
                nc.vector.tensor_tensor(lam[:, :, :], v[:, :, 0, :], v[:, :, 1, :], ALU.mult)
                nc.vector.tensor_tensor(gain_sub, p2("sub_g"), p2("one_less_lam"), ALU.mult)
                dve.drain()
                nc.vector.tensor_reduce(lam_s[:, 0:2], lam[:, :, :], AX.X, ALU.add).then_inc(lam_dots.sem, 1)
                dve.wait_ge(lam_exp.sem, lam_exp.at(1))
                nc.vector.tensor_tensor(lam_s[:, 2:3], lam_s[:, 1:2], lam_s[:, 0:1], ALU.subtract)
                dve.drain()
                nc.vector.tensor_tensor(neg_lam, lam_s[:, 2:3], p2("lam_init"), ALU.subtract)

            def scalar(act):
                act.wait_ge(lam_dots.sem, lam_dots.at(1))
                nc.scalar.activation(lam_s[:, 0:2], lam_s[:, 0:2], ACT.Exp).then_inc(lam_exp.sem, 1)
            stage("layer_params", scalar=scalar, vector=vector, sync=sync)

            norms("mix_pre", [one_norm("x", lambda k: xT[:, k, :], lambda k: p2("mix_pre", 1, k), lambda k: hT[:, k, :],
                                       end=("split", split_hi, split_lo, None))],
                  squares2, scales2)
            with ExitStack() as here:
                q = tmp("q2", [P, 8, T], here)
                k = hT
                v = tmp("v2", [P, TB, 4, P], here)
                dq = tmp("dq", [P, 2, T], here)
                dk = tmp("dk", [P, 2, T], here)
                dv = tmp("dv", [P, TB, 2, P], here)
                with ExitStack() as s:
                    low, u = raw[:, 0:6, :], raw[:, 6:8, :]
                    low_lo = same_place("low_lo", "raw", [P, 6, T], F32R)
                    zv = tmp("zv", [P, TB, 256], s)
                    at = B2_AT["in"]
                    dsts = [(low[:, n, :], ACT.Copy) for n in range(6)] + [(u[:, n, :], ACT.Gelu_apprx_tanh) for n in range(2)] + \
                        [(dq[:, n, :], ACT.Copy) for n in range(2)] + [(dk[:, n, :], ACT.Copy) for n in range(2)]
                    h = Split(h_hi, h_lo)

                    def tokens(x, tb, first=0):
                        return lambda pe, k: x.part(pe, first + k, slice(tb * P, (tb + 1) * P))
                    tiles = [("act", T, weights_still(at + n * KT, KT, h), act_copy(dst, f)) for n, (dst, f) in enumerate(dsts)]
                    gate_in = weights_moving(at + 12 * KT, KT, 2, [tokens(h, tb) for tb in range(TB)])
                    values_in = weights_moving(at + 14 * KT, KT, 2, [tokens(h, tb) for tb in range(TB)])
                    for tb in range(TB):
                        tiles.append(("act", 256, gate_in, act_copy(zv[:, tb, :], ACT.Gelu_apprx_tanh)))
                    for tb in range(TB):
                        tiles.append(("dve", 256, values_in, dve_copy(dv[:, tb, :, :].rearrange("p h n -> p (h n)"))))
                    linear("in2", tiles)
                    norms("latent", [
                        one_norm("cq", lambda t: low[:, t, :], lambda t: p2("cq_g", 1, t), lambda t: low[:, t, :], 3, T, "ones", 384,
                                 ("split", split_hi, lambda t: low_lo[:, t, :], None)),
                        one_norm("ckv", lambda t: low[:, 3 + t, :], lambda t: p2("ckv_g", 1, t), lambda t: low[:, 3 + t, :], 2, T,
                                 "ones", 256, ("split", lambda t: h_hi[:, 3 + t, :],
                                                 lambda t: low_lo[:, 3 + t, :], None))], squares2, scales2)
                    rope("rope_keys", [(low[:, 5, :], con("rot_mla"), COS_MLA, SIN_MLA, low[:, 5, :])] +
                         [(x[:, n, :], con("rot_diff"), COS_DIFF, SIN_DIFF, x[:, n, :]) for x in (dq, dk) for n in range(2)],
                         squares2)

                    lows = Split(h_hi, low_lo)
                    tiles = [("act", T, weights_still(B2_AT["uq"] + 3 * n, 3, lows), act_copy(q[:, n, :])) for n in range(8)]

                    def add_rope_key(n):
                        return lambda dve, ps: nc.vector.tensor_tensor(k[:, n, :], ps, low[:, 5, :], ALU.add)
                    tiles += [("dve", T, weights_still(B2_AT["uk"] + 2 * n, 2, lows, first=3), add_rope_key(n)) for n in range(8)]
                    values_up = weights_moving(B2_AT["uv"], 2, 4, [tokens(lows, tb, 3) for tb in range(TB)])
                    tiles += [("act", 512, values_up, act_copy(v[:, tb, :, :].rearrange("p h n -> p (h n)"))) for tb in range(TB)]
                    linear("up_latent", tiles)
                    rope("rope_queries", [(q[:, h, :], con("rot_mla"), COS_MLA, SIN_MLA, q[:, h, :]) for h in range(8)],
                         squares2)

                    G = 16
                    st = tmp("sgu_stat", [P, 4, G], s)
                    xc = squares2[:, 0:2, :].rearrange("p b n -> p (b n)").rearrange("p (g n) -> p g n", g=G)
                    sq = squares2[:, 2:4, :].rearrange("p b n -> p (b n)").rearrange("p (g n) -> p g n", g=G)
                    centered = Signal("centered", 1)
                    sq_ready = Signal("sgu_square_ready", 1)
                    var_ready = Signal("var_ready", 1)
                    rstd_ready = Signal("rstd_ready", 1)
                    gate_ready = Signal("gate_ready", 1)
                    chunks_mixed = Signal("chunks_mixed", 1)

                    def sgu_tensor(pe):
                        pe.wait_ge(gate_ready.sem, gate_ready.at(1))
                        for tb in range(TB):
                            for g in range(4):
                                last = nc.tensor.matmul(bank[(g % 2) * 64:(g % 2) * 64 + 64, g // 2, tb * P:(tb + 1) * P],
                                                        zv[:, tb, g * 64:(g + 1) * 64], p2("sgu_w", P, g * P),
                                                        start=True, stop=True)
                        last.then_inc(chunks_mixed.sem, 1)

                    def per_group(n):
                        return st[:, n, :].rearrange("p (g o) -> p g o", o=1).to_broadcast([P, G, 64])

                    def sgu_vector(dve):
                        z3 = zv[:, :, :].rearrange("p b (g n) -> p (b g) n", n=64)
                        nc.vector.tensor_reduce(st[:, 0, :], z3, AX.X, ALU.add)
                        dve.drain()
                        nc.vector.tensor_scalar(st[:, 1, :], st[:, 0, :], 1.0 / 64, None, ALU.mult)
                        dve.drain()
                        nc.vector.tensor_tensor(xc, z3, per_group(1), ALU.subtract).then_inc(centered.sem, 1)
                        dve.wait_ge(sq_ready.sem, sq_ready.at(1))
                        nc.vector.tensor_reduce(st[:, 2, :], sq, AX.X, ALU.add).then_inc(var_ready.sem, 1)
                        dve.wait_ge(rstd_ready.sem, rstd_ready.at(1))
                        nc.vector.tensor_tensor(xc, xc, per_group(3), ALU.mult)
                        dve.drain()
                        gains = p2("sgu_g", 256).rearrange("p (o n) -> p o n", o=1).to_broadcast([P, TB, 256])
                        nc.vector.tensor_tensor(zv[:, :, :], xc.rearrange("p (b g) n -> p b (g n)", b=TB), gains, ALU.mult)\
                            .then_inc(gate_ready.sem, 1)
                        dve.wait_ge(chunks_mixed.sem, chunks_mixed.at(1))
                        for n in range(2):
                            y = mix[:, 4 + n, :]
                            b = p2("sgu_b", P, n * P).rearrange("p (o n) -> p o n", o=1).to_broadcast([P, TB, P])
                            nc.vector.tensor_tensor(y.rearrange("p (b n) -> p b n", b=TB),
                                                    bank[:, n, :].rearrange("p (b n) -> p b n", b=TB), b, ALU.add)
                            dve.drain()
                            nc.vector.tensor_tensor(y, y, u[:, n, :], ALU.mult)

                    def sgu_scalar(act):
                        act.wait_ge(centered.sem, centered.at(1))
                        nc.scalar.activation(sq, xc, ACT.Square).then_inc(sq_ready.sem, 1)
                        act.wait_ge(var_ready.sem, var_ready.at(1))
                        nc.scalar.activation(st[:, 3, :], st[:, 2, :], ACT.Ln, bias=con("eps", 1), scale=1.0 / 64)
                        act.drain()
                        nc.scalar.activation(st[:, 3, :], st[:, 3, :], ACT.Exp, scale=-0.5).then_inc(rstd_ready.sem, 1)
                    stage("gating", tensor=sgu_tensor, scalar=sgu_scalar, vector=sgu_vector)

                with ExitStack() as a:
                    spare = h_spare
                    qst = spare[:, 0:4, :].rearrange("p (t g) n -> p t g n", t=2)
                    vst = spare[:, 4:6, :].rearrange("p t (b n) -> p t b n", n=P)
                    work = (squares2[:, :, :].rearrange("p (u h) n -> p u (h n)", u=2), spare[:, 6:8, :],
                            tmp("diag2", [P, 2, 2, P], a), tmp("stat2", [P, 2, 4, 2], a))
                    units = [[dict(scores=[lambda i, t=t, g=g, tb=tb: [(0, T, [(qst[:, t, g, tb * P:(tb + 1) * P],
                                                                         k[:, bass.ds(2 * i + g, 1), :].rearrange("p o n -> p (o n)"))])]],
                                  width=T, masks=[], sink=None, keys=TB,
                                  values=[(bank[g * 64:(g + 1) * 64, 6 + t, tb * P:(tb + 1) * P],
                                           [vst[:, t, j, g * 64:(g + 1) * 64] for j in range(TB)])])
                             for g in range(2) for tb in range(TB)] for t in range(2)]
                    attention("latent", 4, units, 96 ** -0.5,
                              lambda i, t: [(qst[:, t, :, :], q[:, bass.ds(2 * i, 2), :]),
                                         (vst[:, t, :, :], v[:, :, bass.ds(i, 1), :].rearrange("p b o n -> p b (o n)"))],
                              [], lambda i, t: (mix[:, bass.ds(i, 1), :].rearrange("p o n -> p (o n)"), bank[:, 6 + t, :]), work)
                    qst4 = raw[:, :, :].rearrange("p (t r) n -> p t r n", t=2)
                    units = [[dict(scores=[lambda i, t=t, g=g, tb=tb, c=c: [(0, T, [(qst4[:, t, 2 * g + c, tb * P:(tb + 1) * P],
                                                                               dk[:, bass.ds(i, 1), :].rearrange("p o n -> p (o n)"))])]
                                          for c in range(2)],
                                  width=T, masks=[], sink=None, keys=TB,
                                  values=[(bank[g * 64:(g + 1) * 64, 6 + t, tb * P:(tb + 1) * P],
                                           [vst[:, t, j, g * 64:(g + 1) * 64] for j in range(TB)])])
                             for g in range(2) for tb in range(TB)] for t in range(2)]
                    attention("differential", 2, units, 32 ** -0.5,
                              lambda i, t: [(qst4[32 * r:32 * r + 32, t, r, :],
                                          dq[32 * r:32 * r + 32, bass.ds(i, 1), :].rearrange("p o n -> p (o n)")) for r in range(4)] +
                              [(vst[:, t, :, :], dv[:, :, bass.ds(i, 1), :].rearrange("p b o n -> p b (o n)"))],
                              [qst4],
                              lambda i, t: (mix[:, bass.ds(i + 6, 1), :].rearrange("p o n -> p (o n)"), bank[:, 6 + t, :]),
                              work, neg_lam=neg_lam)
            norms("sub", [one_norm("o", lambda t, n=n: mix[:, 6 + n, :], lambda t: gain_sub, lambda t, n=n: mix[:, 6 + n, :], 1, T,
                                   "ones64", 64) for n in range(2)], squares2, scales2)

            def project(name, at, gain):
                x = Split(h_hi, mix_lo, mix)
                linear(name, [("act" if n % 2 else "dve", T, weights_still(at + n * KT, KT, x),
                               act_copy(raw[:, n, :]) if n % 2 else dve_copy(raw[:, n, :])) for n in range(KT)], operands=[x])
                post(name, gain)

            def post(name, gain):
                norms(f"{name}_post", [one_norm("o", lambda t: raw[:, t, :], lambda t: p2(gain, 1, t), lambda t: xT[:, t, :],
                                                end=("residual", lambda t: xT[:, t, :]))], squares2, scales2)
            project("mix_out", B2_AT["mix"], "mix_post")

            with ExitStack() as here:
                k = tmp("mem_k", [P, KT, MEM], here)
                v = tmp("mem_v", [P, 2, 4, 256], here)
                memT = tmp("memT", [P, KT, MEM], here)
                mem_lo = same_place("mem_lo", "memT", [P, KT, MEM], F32R)
                mem_hi = tmp("mem_hi", [P, KT, MEM], here, F32R)
                memory_loaded = Signal("memory_loaded", 16)

                def load_memory(sp):
                    sp.dma_start(memT[:, :, :], memT_in).then_inc(memory_loaded.sem, 16)
                norms("mem_pre", [one_norm("x", lambda t: xT[:, t, :], lambda t: p2("mem_pre", 1, t), lambda t: hT[:, t, :],
                                           end=("split", split_hi, split_lo, None)),
                                  one_norm("m", lambda t: memT[:, t, :], lambda t: p2("mem_kv", 1, t), lambda t: memT[:, t, :],
                                           KT, MEM, end=("split", lambda t: mem_hi[:, t, :], lambda t: mem_lo[:, t, :], None))], squares2, scales2, load_memory,
                      loaded=(1, memory_loaded))
                h, mem = Split(h_hi, h_lo), Split(mem_hi, mem_lo)
                tiles = [("act", T, weights_still(B2_AT["mq"] + n * KT, KT, h), act_copy(raw[:, n, :])) for n in range(KT)]
                tiles += [("dve", MEM, weights_still(B2_AT["mk"] + n * KT, KT, mem), dve_copy(k[:, n, :])) for n in range(KT)]
                for half in range(2):
                    group = weights_moving(B2_AT["mv"] + half * 4 * KT, KT, 4, [tokens(mem, tb) for tb in range(2)])
                    for tb in range(2):
                        tiles.append(("act", 512, group,
                                      act_copy(v[:, tb, 2 * half:2 * half + 2, :].rearrange("p h n -> p (h n)"))))
                linear("mem_qkv", tiles)
                with ExitStack() as a:
                    qst = h_spare[:, 0:4, :].rearrange("p (t e) n -> p t e n", t=2)
                    vst = tmp("mem_vst", [P, 2, 2, 256], a)
                    work = (squares2[:, :, :].rearrange("p (u h) n -> p u (h n)", u=2), tmp("probsT3", [P, 2, 256], a),
                            tmp("diag3", [P, 2, 1, P], a), tmp("stat3", [P, 2, 4, 2], a))
                    units = [[dict(scores=[lambda i, t=t, tb=tb: [(0, MEM, [(qst[:, t, e, tb * P:(tb + 1) * P],
                                                                       k[:, bass.ds(2 * i + e, 1), :].rearrange("p o n -> p (o n)"))
                                                                      for e in range(2)])]],
                                  width=MEM, masks=[], sink=None, keys=2,
                                  values=[(bank[:, 6 + e, tb * P:(tb + 1) * P], [vst[:, t, j, e * P:(e + 1) * P] for j in range(2)])
                                          for e in range(2)]) for tb in range(TB)] for t in range(2)]
                    attention("memory", 4, units, 256 ** -0.5,
                              lambda i, t: [(qst[:, t, :, :], raw[:, bass.ds(2 * i, 2), :]),
                                         (vst[:, t, :, :], v[:, :, bass.ds(i, 1), :].rearrange("p b o n -> p b (o n)"))],
                              [], lambda i, t: (mix[:, bass.ds(2 * i, 2), :], bank[:, 6:8, :]), work,
                              shared_out=True)
            project("mem_out", B2_AT["mo"], "mem_post")

            norms("ffn_pre", [one_norm("x", lambda t: xT[:, t, :], lambda t: p2("ffn_pre", 1, t), lambda t: hT[:, t, :],
                                       end=("split", split_hi, split_lo, None))],
                  squares2, scales2)
            up_down("2", B2_AT, ACT.Gelu_apprx_tanh, True, col(par2, PAR2["conv_w"]), col(par2, PAR2["conv_b"]),
                    lambda n: ("act", act_copy(raw[:, n, :])) if n % 2 else ("dve", dve_copy(raw[:, n, :])),
                    mix[:, 0:4, :].rearrange("p (u s) n -> p u s n", u=2))
            post("ffn", "ffn_post")

        ws.base, ws.fed, ws.begun, ws.rounded, ws.halved, ws.limit = B1_SLABS, 0, 0, 0, 0, B2_SLABS
        with nc.Fori(0, LAYERS) as l:
            layer[0] = l
            layer_body(l)
        layer[0] = None
        totals = {r: n for r, n in used_here.items() if r.endswith("_2")}
        assert totals == PER_LAYER, totals

        stored = Signal("stored", 16)

        def sync(sp):
            sp.dma_start(out, xT[:, :, :]).then_inc(stored.sem, 16)
            sp.wait_ge(stored.sem, stored.at(16))
        ws.limit = 0
        stage("store", sync=sync)


def constants():
    c = np.zeros((P, CONST_W), np.float32)

    def put(name, a, at=0):
        c[:, CONST[name] + at:CONST[name] + at + a.shape[1]] = a
    p = np.arange(P)
    put("ident", np.eye(P))
    put("ones", np.ones((P, P)))
    put("ones64", (p[:, None] // 64 == p[None, :] // 64) * 1.0)
    rot = np.zeros((P, P))
    rot[p[1::2], p[0::2]] = -1.0
    rot[p[0::2], p[1::2]] = 1.0
    put("rot1", rot)
    rot = np.zeros((P, P))
    for i in range(16):
        rot[64 + 16 + i, 64 + i] = -1.0
        rot[64 + i, 64 + 16 + i] = 1.0
    put("rot_mla", rot)
    rot = np.zeros((P, P))
    for base in range(0, P, 32):
        for i in range(8):
            rot[base + 8 + i, base + i] = -1.0
            rot[base + i, base + 8 + i] = 1.0
    put("rot_diff", rot)
    put("mask_prev", np.where(p[None, :] >= p[:, None], 0.0, NEG_BIG))
    put("mask_next", np.where(p[None, :] <= p[:, None], 0.0, NEG_BIG))
    j, t = p[:, None], p[None, :]
    for d in range(2):
        for l in range(LEVELS + 1):
            if l == LEVELS:
                m = j == t
            else:
                h = CHUNK >> l
                jh, th = (0, 1) if d == 0 else (1, 0)
                m = (j // (2 * h) == t // (2 * h)) & (j // h % 2 == jh) & (t // h % 2 == th)
            put("levels", m * 1.0, (d * (LEVELS + 1) + l) * P)
    tok = np.arange(ALLT)
    put("reset", np.broadcast_to((tok % CHUNK != 0) * 1.0, (P, ALLT)))
    put("reset", np.broadcast_to((tok % CHUNK != CHUNK - 1) * 1.0, (P, ALLT)), ALLT)
    freq = np.zeros((P, 2), np.float32)
    inv = (THETA_2 ** (-np.arange(0, 32, 2, dtype=np.float32) / np.float32(32))).astype(np.float32)
    freq[64:96, 0] = np.tile(inv, 2)
    inv = (THETA_2 ** (-np.arange(0, 16, 2, dtype=np.float32) / np.float32(16))).astype(np.float32)
    for base in range(0, P, 32):
        freq[base:base + 16, 1] = np.tile(inv, 2)
    put("freq", freq)
    put("eps", np.full((P, 1), EPS))
    put("half_pi", np.full((P, 1), np.pi / 2))
    put("one", np.ones((P, 1)))
    return c


def axial_tables():
    p, n = np.arange(P), np.arange(T)
    half = HD // 4
    inv = (THETA_1 ** (-np.arange(0, 2 * half, 2, dtype=np.float32) / np.float32(2 * half))).astype(np.float32)
    ang = np.concatenate([(n // GRID_W).astype(np.float32)[:, None] * inv, (n % GRID_W).astype(np.float32)[:, None] * inv], 1)
    ang = ang.T[(p % HD) // 2]
    return np.stack([np.cos(ang), np.sin(ang)], 1)


def weight_stream(w):
    blocks = []

    def still(m, cols, tiles=None):
        for c in cols:
            for k in range(m.shape[0] // P):
                blocks.append(m[k * P:(k + 1) * P, c])

    def padded(m, at):
        full = np.zeros((m.shape[0], P), np.float32)
        full[:, at:at + m.shape[1]] = m
        return full

    def moving(m, n):
        for c in range(0, m.shape[1], n * P):
            for k in range(m.shape[0] // P):
                for e in range(n):
                    blocks.append(m[k * P:(k + 1) * P, c + e * P:c + (e + 1) * P])

    def tiles(n, start=0):
        return [slice(start + c * P, start + (c + 1) * P) for c in range(n)]
    still(w["w_mod"][0], tiles(MOD_TILES))
    w_in = w["w_in"][0]
    pair = [np.r_[g * HD:(g + 1) * HD, (g + 4) * HD:(g + 5) * HD] for g in range(4)]
    still(w_in, tiles(12, 1536))
    moving(w_in[:, 3072:3584], 4)
    for at in (0, 768):
        still(w_in, [at + c for c in pair])
        still(w_in, [slice(at + 512, at + 640), slice(at + 640, at + 768)])
    still(w_in, tiles(4, 3584))
    for n in range(KT):
        for b in range(3):
            still(w_in, [slice(4096 + b * D + n * P, 4096 + b * D + (n + 1) * P)])
            wb = w["w_branch"][0, b]
            if b < 2:
                wb = np.concatenate([wb[c] for c in pair])
            still(wb, tiles(KT)[n:n + 1])
    still(w["w_out"][0], tiles(KT))

    def ffn_blocks(up, down):
        for n in range(FT):
            still(up, [slice(n * P, (n + 1) * P), slice(FF + n * P, FF + (n + 1) * P)])
        moving(down, KT)
    ffn_blocks(w["w_up"][0], w["w_down"][0])
    assert len(blocks) == B1_SLABS * SLAB
    for l in range(LAYERS):
        w_in = w["w_in_2"][l]
        still(w_in, tiles(5))
        still(padded(w_in[:, 640:672], 64), tiles(1))
        still(w_in, tiles(2, 672) + tiles(4, 1184))
        moving(w_in[:, 928:1184], 2)
        moving(w_in[:, 1696:1952], 2)
        uq, ukv = w["mla_w_uq_2"][l], w["mla_w_ukv_2"][l]
        for h in range(8):
            still(padded(uq[:, h * 96:(h + 1) * 96], 0), tiles(1))
        for h in range(8):
            still(padded(ukv[:, h * P:h * P + 64], 0), tiles(1))
        moving(np.concatenate([ukv[:, h * P + 64:(h + 1) * P] for h in range(8)], 1), 4)
        still(w["w_mix_out_2"][l], tiles(KT))
        still(w["mem_w_q_2"][l], tiles(KT))
        still(w["mem_w_kv_2"][l], tiles(KT))
        moving(w["mem_w_kv_2"][l][:, D:], 4)
        still(w["mem_w_o_2"][l], tiles(KT))
        ffn_blocks(w["ffn_w_up_2"][l], w["ffn_w_down_2"][l])
    assert len(blocks) == SLABS * SLAB
    return np.stack(blocks).reshape(SLABS, SLAB, P, P).transpose(0, 2, 1, 3).reshape(SLABS, P, SLAB * P)


def cols(v):
    return np.asarray(v).reshape(-1, P).T


def conv_cols(w):
    return np.concatenate([cols(tap) for tap in w], 1)


def rows(v):
    v = np.asarray(v).reshape(1, -1)
    return np.broadcast_to(v, (P, v.shape[1]))


def table(places, width, fields):
    t = np.zeros((P, width), np.float32)
    for name, a in fields.items():
        t[:, places[name]:places[name] + a.shape[1]] = a
    return t


def host_layout(w):
    w = {k: np.asarray(v) for k, v in w.items()}

    def features_first(a):
        return np.ascontiguousarray(a[0].T.reshape(KT, P, -1).transpose(1, 0, 2))
    both = np.stack([cols(w["c"][0]), cols(w["c_ctx"])], 2).reshape(P, 2 * KT)
    par1 = table(PAR1, PAR1_W, dict(
        c=both, b_mod=cols(w["b_mod"][0]), norm_mix=cols(w["norm_mix"][0]), norm_ffn=cols(w["norm_ffn"][0]),
        qn=cols(np.concatenate([w["qn_b"][0]] * 2)), kn=cols(np.concatenate([w["kn_b"][0]] * 2)),
        lb=np.concatenate([cols(w["lb_fwd"][0]), cols(w["lb_bwd"][0])], 1), gn=cols(w["gn_c"][0]),
        conv_w=conv_cols(w["w_dw"][0]), conv_b=cols(w["b_dw"][0]), norm_final=cols(w["norm_final"]),
        sink=rows(w["sink_a"][0])))
    par2 = []
    for l in range(LAYERS):
        lam_init = 0.8 - 0.6 * np.exp(-0.3 * l)
        par2.append(table(PAR2, PAR2_W, dict(
            mix_pre=cols(w["mix_pre_g_2"][l]), mix_post=cols(w["mix_post_g_2"][l]), cq_g=cols(w["mla_cq_g_2"][l]),
            ckv_g=cols(w["mla_ckv_g_2"][l]), sub_g=cols(np.concatenate([w["diff_sub_g_2"][l]] * 2)),
            mem_pre=cols(w["mem_pre_g_2"][l]), mem_post=cols(w["mem_post_g_2"][l]), mem_kv=cols(w["mem_kv_g_2"][l]),
            ffn_pre=cols(w["ffn_pre_g_2"][l]), ffn_post=cols(w["ffn_post_g_2"][l]),
            conv_w=conv_cols(w["ffn_conv_w_2"][l]), conv_b=cols(w["ffn_conv_b_2"][l]),
            lam=rows(np.concatenate([w[f"diff_lam_{n}_2"][l] for n in ("q1", "k1", "q2", "k2")])),
            lam_init=np.full((P, 1), lam_init, np.float32), one_less_lam=np.full((P, 1), 1.0 - lam_init, np.float32),
            sgu_g=rows(w["sgu_norm_g_2"][l]),
            sgu_b=np.concatenate([np.repeat(w["sgu_b_s_2"][l][2 * n:2 * n + 2], 64, 0) for n in range(2)], 1),
            sgu_w=w["sgu_w_s_2"][l].transpose(2, 0, 1).reshape(P, 4 * P))))
    return {"stream": weight_stream(w), "xT": features_first(w["x"]), "ctxT": features_first(w["ctx"]),
            "memT": features_first(w["mem_2"]), "pos": w["positions_2"], "const": constants(), "axial": axial_tables(), "par1": par1,
            "par2": np.stack(par2)}


def kernel(**inputs):
    import concourse.bacc as bacc
    from concourse.bass_utils import run_bass_kernel_spmd
    arrays = {f"in_{name}": np.ascontiguousarray(a) for name, a in host_layout(inputs).items()}
    nc = bacc.Bacc("TRN2", target_bir_lowering=False, num_devices=1, dynamic_dma_scratch_size=1024)
    args = [nc.dram_tensor(name, a.shape, mybir.dt.from_np(a.dtype), kind="ExternalInput").ap()
            for name, a in arrays.items()]
    out = nc.dram_tensor("out", (P, KT, T), F32, kind="ExternalOutput").ap()
    build_program(nc, *args, out)
    got = run_bass_kernel_spmd(nc, [arrays], core_ids=[0]).results[0]["out"]
    return np.ascontiguousarray(got.transpose(1, 0, 2).reshape(D, T).T)[None]
```

```python
from contextlib import ExitStack

import numpy as np

import concourse.bass as bass
from concourse import mybir

F32 = mybir.dt.float32
F32R = mybir.dt.float32r
I32 = mybir.dt.int32
ALU = mybir.AluOpType
ACT = mybir.ActivationFunctionType
AX = mybir.AxisListType

P = 128
D = 1024
KT = D // P
T = 512
TB = T // P
CT = 256
CB = CT // P
ALLT = CT + T
FF = 2816
FT = FF // P
HD = 64
EPS = 1e-6
NEG_BIG = -1e30
LAYERS = 2
MEM = 256
GRID_W = 64
THETA_1, THETA_2 = 10000.0, 500000.0
CHUNK = 64
LEVELS = 7
C_HEADS = 4

SLAB = 16
RING = 4
HI = 2
SQUARES = 4
MOD_TILES = 6 * KT
QKV_BLOCKS = 6 * KT
B1_AT = {}
_at = 0
for _name, _n in (("mod", MOD_TILES * KT), ("C", 16 * KT), ("A", QKV_BLOCKS), ("B", QKV_BLOCKS),
                  ("cg", 4 * KT), ("merge", KT * 3 * (KT + 4)), ("out", KT * KT), ("up", 2 * FT * KT),
                  ("down", KT * FT)):
    B1_AT[_name] = _at
    _at += _n
B1_SLABS = _at // SLAB
WHOLE_SLABS = B1_AT["C"] // SLAB
assert WHOLE_SLABS * SLAB == B1_AT["C"]
assert _at == B1_SLABS * SLAB
B2_AT = {}
_at = 0
for _name, _n in (("in", 16 * KT), ("uq", 8 * 3), ("uk", 8 * 2), ("uv", 4 * 2), ("mix", KT * KT),
                  ("mq", KT * KT), ("mk", KT * KT), ("mv", KT * KT), ("mo", KT * KT),
                  ("up", 2 * FT * KT), ("down", KT * FT)):
    B2_AT[_name] = _at
    _at += _n
B2_SLABS = _at // SLAB
assert _at == B2_SLABS * SLAB and B2_SLABS % RING == 0
for _at in (B1_AT["up"], B2_AT["up"]):
    assert _at % SLAB == 0 and 2 * KT == SLAB
SLABS = B1_SLABS + LAYERS * B2_SLABS
PER_LAYER = {'params_loaded_2': 16, 'square_ready_2': 63, 'square_summed_2': 63, 'scale_ready_2': 11, 'normed_2': 63, 'upper_ready_2': 37, 'lower_ready_2': 25, 'lower_by_pool_2': 12, 'tile_done_2': 84, 'out_by_act_2': 40, 'out_by_dve_2': 20, 'rotated_2': 13, 'by_sin_2': 13, 'roped_2': 13, 'centered_2': 1, 'sgu_square_ready_2': 1, 'var_ready_2': 1, 'rstd_ready_2': 1, 'gate_ready_2': 1, 'chunks_mixed_2': 1, 'lam_dots_2': 1, 'lam_exp_2': 1, 'staged_2': 10, 'scored_2': 64, 'max_ready_2': 64, 'exp_done_2': 64, 'inverse_ready_2': 64, 'probs_ready_2': 64, 'turned0_2': 64, 'turned1_2': 64, 'probs_out0_2': 64, 'probs_out1_2': 64, 'summed_2': 10, 'sum_read_2': 16, 'scaled_2': 16, 'first_out_2': 3, 'operand_rounded_2': 38, 'operand_split_2': 38, 'memory_loaded_2': 16, 'pair_done_2': 22, 'center_ready_2': 22, 'banks_free_2': 26, 'acted_2': 22, 'gated_2': 24, 'operand_used_2': 22}


def columns(fields):
    at, places = 0, {}
    for name, n in fields:
        places[name] = at
        at += n
    return places, at


CONST, CONST_W = columns([
    ("ident", P), ("ones", P), ("ones64", P), ("rot1", P), ("rot_mla", P), ("rot_diff", P),
    ("mask_prev", P), ("mask_next", P), ("levels", 2 * (LEVELS + 1) * P), ("reset", 2 * ALLT),
    ("freq", 2), ("eps", 1), ("half_pi", 1), ("one", 1)])
PAR1, PAR1_W = columns([
    ("c", 2 * KT), ("b_mod", MOD_TILES), ("norm_mix", KT), ("norm_ffn", KT), ("qn", 1), ("kn", 1),
    ("lb", 2 * C_HEADS), ("gn", 1), ("conv_w", 3 * 2 * FT), ("conv_b", 2 * FT), ("norm_final", KT),
    ("sink", 8)])
PAR2, PAR2_W = columns([
    ("mix_pre", KT), ("mix_post", KT), ("cq_g", 3), ("ckv_g", 2), ("sub_g", 1), ("mem_pre", KT),
    ("mem_post", KT), ("mem_kv", KT), ("ffn_pre", KT), ("ffn_post", KT), ("conv_w", 3 * 2 * FT),
    ("conv_b", 2 * FT), ("lam", 4 * 32), ("lam_init", 1), ("one_less_lam", 1), ("sgu_g", 256),
    ("sgu_b", 2 * P), ("sgu_w", 4 * P)])


def build_program(nc, stream, xT_in, ctxT_in, memT_in, pos_in, const_in, axial_in, par1_in, par2_in, out):
    stack = ExitStack()
    with stack:
        place = {}

        def new(scope, name, shape, dt):
            tensor = scope.enter_context(nc.sbuf_tensor(name, shape, dt))
            place[name] = nc.sbuf_base - int(np.prod(shape[1:])) * 4
            return tensor

        def sb(name, shape, dt=F32):
            return new(stack, name, shape, dt)

        def same_place(name, of, shape, dt):
            return nc.alloc_sbuf_tensor_at(name, shape, dt, offset=place[of])

        ring = sb("ring", [P, RING, SLAB, P])
        ring_lo = same_place("ring_lo", "ring", [P, RING, SLAB, P], F32R)
        ring_hi = sb("ring_hi", [P, HI, SLAB, P], F32R)
        ring_spare = same_place("ring_spare", "ring_hi", [P, HI * SLAB * P], F32)
        xT = sb("xT", [P, KT, T])
        hT = sb("hT", [P, KT, T])
        h_lo = same_place("h_lo", "hT", [P, KT, T], F32R)
        h_hi = sb("h_hi", [P, KT, T], F32R)
        h_spare = same_place("h_spare", "h_hi", [P, KT, T], F32)
        const = sb("const", [P, CONST_W])
        par1 = sb("par1", [P, PAR1_W])
        small = sb("small", [P, 256])
        bank = stack.enter_context(nc.psum_tensor("bank", [P, 8, 512], F32))

        def con(name, n=P, at=0):
            return const[:, CONST[name] + at:CONST[name] + at + n]

        def p1(name, n=1, at=0):
            return par1[:, PAR1[name] + at:PAR1[name] + at + n]

        layer = [None]

        roles, used_here = {}, {}

        class Signal:

            def __init__(self, role, count):
                role = role if layer[0] is None else f"{role}_2"
                if role not in roles:
                    roles[role] = stack.enter_context(nc.semaphore(role))
                self.sem, self.start = roles[role], used_here.get(role, 0)
                self.per_layer = 0 if layer[0] is None else PER_LAYER[role]
                used_here[role] = self.start + count

            def at(self, n):
                n = n + self.start
                return n if layer[0] is None else n + layer[0] * self.per_layer

        slab_loaded = [stack.enter_context(nc.semaphore(f"slab_loaded{r}")) for r in range(RING)]
        slab_begun = stack.enter_context(nc.semaphore("slab_begun"))
        slab_rounded = stack.enter_context(nc.semaphore("slab_rounded"))
        slab_split = stack.enter_context(nc.semaphore("slab_split"))

        class Stream:
            base, fed, begun, pending, rounded, halved = 0, 0, 0, False, 0, 0

            def count(self, slab, turn=0):
                n = self.base + slab + 1 + turn
                return n if layer[0] is None else layer[0] * B2_SLABS + n

            def loads(self, slab, turn=0):
                n = (self.base + slab) // RING + 1 + turn
                return (n if layer[0] is None else layer[0] * (B2_SLABS // RING) + n) * 16

            def begin(self, pe, block, whole):
                slab = block // SLAB
                if slab >= self.begun:
                    assert slab == self.begun
                    if whole:
                        pe.wait_ge(slab_loaded[(self.base + slab) % RING], self.loads(slab))
                    else:
                        pe.wait_ge(slab_split, self.count(slab) - WHOLE_SLABS)
                    self.begun += 1
                    self.pending = True

            def slab(self, slab):
                return ring[:, (self.base + slab) % RING, :, :].rearrange("p b n -> p (b n)")

            def slab_hi(self, slab):
                return ring_hi[:, (self.base + slab) % HI, :, :].rearrange("p b n -> p (b n)")

            def round(self, act, slab, loop=None, j=0):
                g = self.base + slab + j
                turns, slabs = (0, j) if loop is None else (loop, loop * RING + j)
                act.wait_ge(slab_loaded[g % RING], self.loads(slab + j, turns))
                if layer[0] is not None or g >= WHOLE_SLABS + HI:
                    act.wait_ge(slab_begun, self.count(slab, slabs) + (1 - HI))
                nc.scalar.activation(self.slab_hi(slab + j), self.slab(slab + j), ACT.Copy).then_inc(slab_rounded, 1)

            def halve(self, dve, slab, loop=None, j=0):
                slabs = j if loop is None else loop * RING + j
                dve.wait_ge(slab_rounded, self.count(slab, slabs) - WHOLE_SLABS)
                lower = ring_lo[:, (self.base + slab + j) % RING, :, :].rearrange("p b n -> p (b n)")
                nc.vector.tensor_tensor(lower, self.slab(slab + j), self.slab_hi(slab + j).bitcast(F32), ALU.subtract)\
                    .then_inc(slab_split, 1)

            def round_to(self, act, slab, last):
                while self.rounded <= min(slab, last - 1):
                    self.round(act, self.rounded)
                    self.rounded += 1

            def halve_to(self, dve, slab, last):
                while self.halved <= min(slab, last - 1):
                    self.halve(dve, self.halved)
                    self.halved += 1

            def parts(self, b, n=1):
                slab, at = divmod(b, SLAB)
                assert at + n <= SLAB
                return (ring_hi[:, (self.base + slab) % HI, at:at + n, :].rearrange("p b n -> p (b n)"),
                        ring_lo[:, (self.base + slab) % RING, at:at + n, :].rearrange("p b n -> p (b n)"))

            def mm_whole(self, pe, b, out, lhsT, start, stop):
                self.begin(pe, b, True)
                slab, at = divmod(b, SLAB)
                w = ring[:, (self.base + slab) % RING, at:at + 4, :].rearrange("p b n -> p (b n)")
                ins = nc.tensor.matmul(out, lhsT, w, start=start, stop=stop)
                if self.pending:
                    ins.then_inc(slab_begun, 1)
                    self.pending = False
                return ins

            def mm(self, pe, b, n, out, operand, still, start, stop):
                self.begin(pe, b, False)
                w_hi, w_lo = self.parts(b, n)
                x_hi, x_lo = operand
                for w, x in ((w_hi, x_hi), (w_hi, x_lo), (w_lo, x_hi)):
                    lhsT, rhs = (w, x) if still else (x, w)
                    ins = nc.tensor.matmul(out, lhsT, rhs, start=start and w is w_hi and x is x_hi, stop=stop and w is w_lo)
                    if self.pending:
                        ins.then_inc(slab_begun, 1)
                        self.pending = False
                return ins

            def feed(self, sp, last):
                upto_slab = min(last, self.begun + RING - 1)
                while self.fed < upto_slab:
                    s = self.fed
                    g = self.base + s
                    if layer[0] is not None or g >= RING:
                        v = g - RING + 2
                        sp.wait_ge(slab_begun, v if layer[0] is None else layer[0] * B2_SLABS + v)
                    if layer[0] is None:
                        src = stream[g]
                    else:
                        src = stream[bass.ds(layer[0] * B2_SLABS + g, 1)].rearrange("o p n -> p (o n)")
                    sp.dma_start(ring[:, g % RING, :, :].rearrange("p b n -> p (b n)"), src)\
                        .then_inc(slab_loaded[g % RING], 16)
                    self.fed += 1

        ws = Stream()
        ws.limit, ws.rounded, ws.halved = B1_SLABS, WHOLE_SLABS, WHOLE_SLABS

        def stage(name, tensor=None, scalar=None, vector=None, gpsimd=None, sync=None):
            with nc.Block() as block:
                if tensor:
                    @block.tensor
                    def _(pe):
                        tensor(pe)

                @block.sync
                def _(sp):
                    if sync:
                        sync(sp)
                    ws.feed(sp, ws.limit)
                if scalar:
                    @block.scalar
                    def _(act):
                        scalar(act)
                if vector:
                    @block.vector
                    def _(dve):
                        vector(dve)
                if gpsimd:
                    @block.gpsimd
                    def _(pool):
                        gpsimd(pool)

        def bcast(ap, n):
            return ap.rearrange("p (k o) -> p k o", o=1).to_broadcast([P, ap.shape[1], n])

        class Split:

            def __init__(self, hi, lo, whole=None):
                self.whole, self.hi, self.lo, self.ready, self.waited, self.base, self.by_turns = whole, hi, lo, None, 0, 0, None

            def part(self, pe, k, cols=slice(None)):
                if self.ready is not None and k >= self.waited:
                    self.waited = k + 1
                    if self.by_turns:
                        done = self.by_turns[k % 2]
                        pe.wait_ge(done.sem, done.at(k // 2 + 1))
                    else:
                        pe.wait_ge(self.ready.sem, self.ready.at(self.base + k + 1))
                return self.hi[:, k, cols], self.lo[:, k, cols]

        def linear(name, tiles, banks=8, sync=None, operands=(), last_split=None, norm=None, also=None, pool_also=None):
            n_act = sum(t[0] == "act" for t in tiles)
            limit = ws.limit if last_split is None else last_split
            tile_done = Signal("tile_done", len(tiles))
            out_by = {"act": Signal("out_by_act", n_act),
                      "dve": Signal("out_by_dve", len(tiles) - n_act)}
            rounded = [Signal("operand_rounded", x.hi.shape[1]) for x in operands]
            for x in operands:
                x.ready, x.waited = Signal("operand_split", x.hi.shape[1]), 0
            ordinal, seen = [], {"act": 0, "dve": 0}
            for t in tiles:
                seen[t[0]] += 1
                ordinal.append(seen[t[0]])

            def tensor(pe):
                if norm:
                    norm.sums(pe, range(1))
                n = 0
                while n < len(tiles):
                    if norm and n == 1:
                        norm.sums(pe, range(1, len(norm.jobs)))
                    cols, products = tiles[n][1:3]
                    members = len(products["tokens"])
                    for m in range(n, n + members):
                        if norm and m in norm.sum_banks:
                            pe.wait_ge(norm.scale_ready.sem, norm.scale_ready.at(len(norm.jobs)))
                        if m >= banks:
                            out = out_by[tiles[m - banks][0]]
                            pe.wait_ge(out.sem, out.at(ordinal[m - banks]))
                    outs = [bank[:, m % banks, 0:cols] for m in range(n, n + members)]
                    kts, width = products["kts"], products["width"]
                    for k in range(kts):
                        b = products["at"] + k * width
                        for out_ap, operand in zip(outs, products["tokens"]):
                            last = ws.mm(pe, b, width, out_ap, operand(pe, k), products["still"], k == 0, k == kts - 1)
                            if k == kts - 1:
                                last.then_inc(tile_done.sem, 1)
                    n += members

            def last_slab(products):
                return (products["at"] + products["kts"] * products["width"] - 1) // SLAB

            def first_slab():
                return tiles[0][2]["at"] // SLAB

            def scalar(act):
                ws.round_to(act, first_slab(), limit)
                if norm:
                    norm.halfway_scalar = lambda act: ws.round_to(act, first_slab() + 1, limit)
                    norm.scalar(act)
                for x, done in zip(operands, rounded):
                    for k in range(x.hi.shape[1]):
                        nc.scalar.activation(x.hi[:, k, :], x.whole[:, k, :], ACT.Copy).then_inc(done.sem, 1)
                for n, (engine, cols, products, out_fn, *before) in enumerate(tiles):
                    ws.round_to(act, last_slab(products) + 1, limit)
                    if also and ("act", n) in also:
                        also["act", n](act)
                    if engine == "act":
                        for b in before:
                            act.wait_ge(out_by["dve"].sem, out_by["dve"].at(ordinal[b]))
                        act.wait_ge(tile_done.sem, tile_done.at(n + 1))
                        out_fn(act, bank[:, n % banks, 0:cols]).then_inc(out_by["act"].sem, 1)

            def vector(dve):
                ws.halve_to(dve, first_slab(), limit)
                if norm:
                    norm.halfway_vector = lambda dve: ws.halve_to(dve, first_slab() + 1, limit)
                    norm.vector(dve)
                for x, done in zip(operands, rounded):
                    for k in range(x.hi.shape[1]):
                        dve.wait_ge(done.sem, done.at(k + 1))
                        nc.vector.tensor_tensor(x.lo[:, k, :], x.whole[:, k, :], x.hi[:, k, :].bitcast(F32), ALU.subtract)\
                            .then_inc(x.ready.sem, 1)
                for n, (engine, cols, products, out_fn, *before) in enumerate(tiles):
                    ws.halve_to(dve, last_slab(products) + 1, limit)
                    if also and ("dve", n) in also:
                        also["dve", n](dve)
                    if engine == "dve":
                        for b in before:
                            dve.wait_ge(out_by["act"].sem, out_by["act"].at(ordinal[b]))
                        dve.wait_ge(tile_done.sem, tile_done.at(n + 1))
                        out_fn(dve, bank[:, n % banks, 0:cols]).then_inc(out_by["dve"].sem, 1)

            def gpsimd(pool):
                if norm:
                    norm.gpsimd(pool)
                if pool_also:
                    pool_also(pool)

            stage(name, tensor=tensor, scalar=scalar, vector=vector, gpsimd=gpsimd, sync=sync or (norm and norm.sync))

        def split_hi(k):
            return h_hi[:, k, :]

        def split_lo(k):
            return h_lo[:, k, :]

        def weights_still(at, kts, x, cols=slice(None), first=0):
            return dict(at=at, kts=kts, width=1, still=True, tokens=[lambda pe, k: x.part(pe, first + k, cols)])

        def weights_moving(at, kts, n, tokens):
            return dict(at=at, kts=kts, width=n, still=False, tokens=tokens)

        def act_copy(dst, func=ACT.Copy):
            return lambda act, ps: nc.scalar.activation(dst, ps, func)

        def dve_copy(dst):
            return lambda dve, ps: nc.vector.tensor_copy(dst, ps)

        class Norms:

            def __init__(self, jobs, squares, scales, sync=None, loaded=None, gains_loaded=None, splits=None):
                self.jobs, self.squares, self.scales, self.sync = jobs, squares, scales, sync
                self.loaded, self.gains_loaded, self.before = loaded, gains_loaded, splits is not None
                self.sum_banks = (6, 7) if self.before else (0, 1)
                self.starts = [sum(j["tiles"] for j in jobs[:n]) for n in range(len(jobs))]
                total = sum(j["tiles"] for j in jobs)
                split = sum(j["tiles"] for j in jobs if j["end"] and j["end"][0] == "split")
                self.square_ready = Signal("square_ready", total)
                self.square_summed = Signal("square_summed", total)
                self.scale_ready = Signal("scale_ready", len(jobs))
                self.normed = Signal("normed", total)
                self.upper_ready = Signal("upper_ready", split)
                self.halved = (jobs[0]["tiles"] + 1) // 2 if splits and jobs[0]["tiles"] == KT and not jobs[0]["end"][3] else 0
                self.lower_ready = Signal("lower_ready", split - self.halved)
                self.lower_by_pool = Signal("lower_by_pool", self.halved)
                for x, first in splits or ():
                    x.ready, x.base, x.waited = self.lower_ready, first - (self.halved if first else 0), 0
                    if self.halved and not first:
                        x.by_turns = (self.lower_ready, self.lower_by_pool)

            def sum_bank(self, n):
                return bank[:, self.sum_banks[n % 2], 0:self.jobs[n]["cols"]]

            def square(self, act, n, tiles):
                j = self.jobs[n]
                if self.loaded and n == self.loaded[0] and 0 in tiles:
                    act.wait_ge(self.loaded[1].sem, self.loaded[1].at(16))
                for k in tiles:
                    q = self.starts[n] + k
                    if q >= SQUARES:
                        act.wait_ge(self.square_summed.sem, self.square_summed.at(q - SQUARES + 1))
                    nc.scalar.activation(self.squares[:, q % SQUARES, 0:j["cols"]], j["src"](k), ACT.Square)\
                        .then_inc(self.square_ready.sem, 1)

            def scalar(self, act):
                jobs, starts = self.jobs, self.starts
                self.square(act, 0, range(jobs[0]["tiles"]))
                for n, j in enumerate(jobs):
                    more = jobs[n + 1]["tiles"] if n + 1 < len(jobs) else 0
                    ahead = 0 if self.before else min(more, SQUARES)
                    if ahead:
                        self.square(act, n + 1, range(ahead))
                    act.wait_ge(self.square_summed.sem, self.square_summed.at(starts[n] + j["tiles"]))
                    if n >= 2:
                        act.wait_ge(self.normed.sem, self.normed.at(starts[n - 1]))
                    s = self.scales[:, n % 2, 0:j["cols"]]
                    nc.scalar.activation(s, self.sum_bank(n), ACT.Ln, bias=con("eps", 1), scale=j["inv"])
                    act.drain()
                    nc.scalar.activation(s, s, ACT.Exp, scale=-0.5).then_inc(self.scale_ready.sem, 1)
                    if j["end"] and j["end"][0] == "split":
                        _, hi, lo, shift = j["end"]
                        for k in range(j["tiles"]):
                            act.wait_ge(self.normed.sem, self.normed.at(starts[n] + k + 1))
                            if shift:
                                up = nc.scalar.activation(hi(k), j["out"](k), ACT.Identity, bias=shift(k))
                            else:
                                up = nc.scalar.activation(hi(k), j["out"](k), ACT.Copy)
                            up.then_inc(self.upper_ready.sem, 1)
                            if n == 0 and k == j["tiles"] - 3 and self.halfway_scalar:
                                self.halfway_scalar(act)
                    if more > ahead:
                        self.square(act, n + 1, range(ahead, more))

            def sums(self, pe, which):
                for n in which:
                    j = self.jobs[n]
                    if n >= 2:
                        pe.wait_ge(self.scale_ready.sem, self.scale_ready.at(n - 1))
                    for k in range(j["tiles"]):
                        q = self.starts[n] + k
                        pe.wait_ge(self.square_ready.sem, self.square_ready.at(q + 1))
                        nc.tensor.matmul(self.sum_bank(n), j["ones"], self.squares[:, q % SQUARES, 0:j["cols"]],
                                         start=k == 0, stop=k == j["tiles"] - 1).then_inc(self.square_summed.sem, 1)

            def vector(self, dve):
                uppers = 0
                for n, j in enumerate(self.jobs):
                    if self.gains_loaded and n == 0:
                        dve.wait_ge(self.gains_loaded.sem, self.gains_loaded.at(16))
                    dve.wait_ge(self.scale_ready.sem, self.scale_ready.at(n + 1))
                    if self.loaded and n == self.loaded[0]:
                        dve.wait_ge(self.loaded[1].sem, self.loaded[1].at(16))
                    split = j["end"] and j["end"][0] == "split"
                    LAG = 2
                    for k in range(j["tiles"] + (LAG if split else 0)):
                        if k < j["tiles"]:
                            dst = j["src"](k) if j["end"] and j["end"][0] == "times" else j["out"](k)
                            nc.vector.scalar_tensor_tensor(dst, j["src"](k), j["gain"](k), self.scales[:, n % 2, 0:j["cols"]],
                                                           ALU.mult, ALU.mult).then_inc(self.normed.sem, 1)
                        if split and k >= LAG:
                            uppers += 1
                        if split and k >= LAG and not (self.halved and n == 0 and (k - LAG) % 2):
                            _, hi, lo, shift = j["end"]
                            dve.wait_ge(self.upper_ready.sem, self.upper_ready.at(uppers))
                            h, up = j["out"](k - LAG), hi(k - LAG).bitcast(F32)
                            if shift:
                                low = nc.vector.scalar_tensor_tensor(lo(k - LAG), h, shift(k - LAG), up, ALU.add, ALU.subtract)
                            else:
                                low = nc.vector.tensor_tensor(lo(k - LAG), h, up, ALU.subtract)
                            low.then_inc(self.lower_ready.sem, 1)
                        if n == 0 and k == j["tiles"] - 1 and self.halfway_vector:
                            self.halfway_vector(dve)

            halfway_scalar = halfway_vector = None

            def gpsimd(self, pool):
                for k in range(1, 2 * self.halved, 2):
                    j = self.jobs[0]
                    pool.wait_ge(self.upper_ready.sem, self.upper_ready.at(k + 1))
                    nc.gpsimd.tensor_tensor(j["end"][2](k), j["out"](k), j["end"][1](k).bitcast(F32), ALU.subtract)\
                        .then_inc(self.lower_by_pool.sem, 1)
                for n, j in enumerate(self.jobs):
                    if j["end"] and j["end"][0] == "times":
                        for k in range(j["tiles"]):
                            pool.wait_ge(self.normed.sem, self.normed.at(self.starts[n] + k + 1))
                            nc.gpsimd.tensor_tensor(j["out"](k), j["end"][1](k), j["src"](k), ALU.mult)

        def norms(name, jobs, squares, scales):
            norm = Norms(jobs, squares, scales)
            stage(name, tensor=lambda pe: norm.sums(pe, range(len(jobs))), scalar=norm.scalar, vector=norm.vector,
                  gpsimd=norm.gpsimd, sync=norm.sync)

        class PostNorm:

            def __init__(self, gain, raw, squares, scales):
                self.gain, self.raw, self.squares, self.scale = gain, raw, squares, scales[:, 0, :]
                self.sum_done = Signal("tile_done", KT)
                self.first_out = Signal("first_out", 1)
                self.square_ready = Signal("square_ready", KT)
                self.square_summed = Signal("square_summed", KT)
                self.scale_ready = Signal("scale_ready", 1)
                self.normed = Signal("normed", KT)

            def square(self, act, n):
                act.wait_ge(self.sum_done.sem, self.sum_done.at(n + 1))
                if n >= SQUARES:
                    act.wait_ge(self.square_summed.sem, self.square_summed.at(n - SQUARES + 1))
                nc.scalar.activation(self.squares[:, n % SQUARES, :], bank[:, n, :], ACT.Square).then_inc(self.square_ready.sem, 1)

            def sum(self, pe, n):
                if n == 0:
                    pe.wait_ge(self.first_out.sem, self.first_out.at(1))
                pe.wait_ge(self.square_ready.sem, self.square_ready.at(n + 1))
                nc.tensor.matmul(bank[:, 0, :], con("ones"), self.squares[:, n % SQUARES, :], start=n == 0, stop=n == KT - 1)\
                    .then_inc(self.square_summed.sem, 1)

            def rms(self, act):
                act.wait_ge(self.square_summed.sem, self.square_summed.at(KT))
                nc.scalar.activation(self.scale, bank[:, 0, :], ACT.Ln, bias=con("eps", 1), scale=1.0 / D)
                act.drain()
                nc.scalar.activation(self.scale, self.scale, ACT.Exp, scale=-0.5).then_inc(self.scale_ready.sem, 1)

            def read_first(self, dve):
                dve.wait_ge(self.square_ready.sem, self.square_ready.at(1))
                nc.vector.tensor_copy(self.raw[:, 0, :], bank[:, 0, :]).then_inc(self.first_out.sem, 1)

            def vector(self, dve):
                dve.wait_ge(self.scale_ready.sem, self.scale_ready.at(1))
                for n in range(KT + 1):
                    if n < KT:
                        src = bank[:, n, :] if n else self.raw[:, 0, :]
                        nc.vector.scalar_tensor_tensor(self.raw[:, n, :], src, self.gain(n), self.scale, ALU.mult, ALU.mult)\
                            .then_inc(self.normed.sem, 1)
                    if n >= 1 and n - 1 not in self.pool_tiles:
                        dve.wait_ge(self.normed.sem, self.normed.at(n))
                        nc.vector.tensor_tensor(xT[:, n - 1, :], xT[:, n - 1, :], self.raw[:, n - 1, :], ALU.add)

            pool_tiles = range(0, KT, 3)

            def gpsimd(self, pool):
                for n in self.pool_tiles:
                    pool.wait_ge(self.normed.sem, self.normed.at(n + 1))
                    nc.gpsimd.tensor_tensor(xT[:, n, :], xT[:, n, :], self.raw[:, n, :], ALU.add)

        def rope(name, jobs, work):
            n_jobs = len(jobs)
            rotated = Signal("rotated", n_jobs)
            by_sin = Signal("by_sin", n_jobs)
            roped = Signal("roped", n_jobs)

            def tensor(pe):
                for n, (raw, rot, _, _, _) in enumerate(jobs):
                    if n >= 4:
                        pe.wait_ge(by_sin.sem, by_sin.at(n - 3))
                    nc.tensor.matmul(bank[:, n % 4, :], rot, raw, start=True, stop=True).then_inc(rotated.sem, 1)

            def vector(dve):
                for n, (raw, _, cos, sin, _) in enumerate(jobs):
                    if n >= 2:
                        dve.wait_ge(roped.sem, roped.at(n - 1))
                    nc.vector.tensor_tensor(work[:, n % 2, :], raw, cos, ALU.mult)
                    dve.wait_ge(rotated.sem, rotated.at(n + 1))
                    nc.vector.tensor_tensor(work[:, 2 + n % 2, :], bank[:, n % 4, :], sin, ALU.mult)\
                        .then_inc(by_sin.sem, 1)

            def gpsimd(pool):
                for n in range(n_jobs):
                    pool.wait_ge(by_sin.sem, by_sin.at(n + 1))
                    nc.gpsimd.tensor_tensor(jobs[n][4], work[:, n % 2, :], work[:, 2 + n % 2, :], ALU.add)\
                        .then_inc(roped.sem, 1)

            stage(name, tensor=tensor, vector=vector, gpsimd=gpsimd)

        def attention(name, turns, units, scale, copies, zeros, read_out, work, sink=None, neg_lam=None, shared_out=False):
            U = len(units[0])
            units = units[0] + units[1]
            N = len(units)
            passes = turns // 2
            total = turns * U
            staged = Signal("staged", turns)
            scored = Signal("scored", total)
            max_ready = Signal("max_ready", total)
            exp_done = Signal("exp_done", total)
            inverse_ready = Signal("inverse_ready", total)
            probs_ready = Signal("probs_ready", total)
            turned = [Signal(f"turned{h}", total) for h in range(2)]
            probs_out = [Signal(f"probs_out{h}", total) for h in range(2)]
            summed = Signal("summed", turns)
            sum_read = Signal("sum_read", turns + 2)
            C = len(units[0]["scores"])
            scaled = Signal("scaled", total) if len(units[0]["scores"]) == 2 else probs_ready
            probs, probsT, stat = work

            def score_cols(u):
                return bank[:, 2 * (u % 2):2 * (u % 2) + 2, :].rearrange("p b n -> p (b n)")

            def halves(u):
                k = units[u]["keys"]
                return (0, (k + 1) // 2), ((k + 1) // 2, k)

            def turned_cols(h, n):
                return bank[:, 4 + h, 0:n * P]

            def tensor(pe):
                def scores(i, u):
                    if u % U == 0:
                        pe.wait_ge(staged.sem, staged.at(2 * i + (u // U + 1)))
                    if u >= 2:
                        pe.wait_ge(exp_done.sem, exp_done.at(i * N + (u - 1)))
                    S = score_cols(u)
                    for c, score in enumerate(units[u]["scores"]):
                        for lo, hi, pairs in score(2 * i + u // U):
                            for k, (lhsT, rhs) in enumerate(pairs):
                                last = nc.tensor.matmul(S[:, c * 512 + lo:c * 512 + hi], lhsT, rhs,
                                                        start=k == 0, stop=k == len(pairs) - 1)
                    last.then_inc(scored.sem, 1)

                def transposes(i, u):
                    pe.wait_ge(probs_ready.sem, probs_ready.at(i * N + (u + 1)))
                    for h, (lo, hi) in enumerate(halves(u)):
                        if u > 0:
                            pe.wait_ge(probs_out[h].sem, probs_out[h].at(i * N + u))
                        for j in range(lo, hi):
                            last = nc.tensor.transpose(turned_cols(h, hi - lo)[:, (j - lo) * P:(j - lo + 1) * P],
                                                       probs[:, u % 2, j * P:(j + 1) * P], con("ident"))
                        last.then_inc(turned[h].sem, 1)

                def values(i, u):
                    t = u // U
                    if u % U == 0:
                        pe.wait_ge(sum_read.sem, sum_read.at(2 * i + (t + (2 if shared_out else 1))))
                    for h in range(2):
                        pe.wait_ge(probs_out[h].sem, probs_out[h].at(i * N + (u + 1)))
                    for out_ap, lhs in units[u]["values"]:
                        for j, lhsT in enumerate(lhs):
                            last = nc.tensor.matmul(out_ap, lhsT, probsT[:, u % 2, j * P:(j + 1) * P],
                                                    start=j == 0, stop=j == len(lhs) - 1)
                    if u % U == U - 1:
                        last.then_inc(summed.sem, 1)

                with pe.Fori(0, passes) as i:
                    scores(i, 0)
                    scores(i, 1)
                    for u in range(N + 1):
                        if u + 2 < N:
                            scores(i, u + 2)
                        if u < N:
                            transposes(i, u)
                        if u >= 1:
                            values(i, u - 1)

            def scalar(act):
                def exps(i, u):
                    act.wait_ge(max_ready.sem, max_ready.at(i * N + (u + 1)))
                    if u >= 2:
                        act.wait_ge(turned[1].sem, turned[1].at(i * N + (u - 1)))
                    S = score_cols(u)
                    w = units[u]["width"]
                    for c in range(C):
                        last = nc.scalar.activation(probs[:, u % 2, c * 512:c * 512 + w], S[:, c * 512:c * 512 + w],
                                                    ACT.Exp, bias=stat[:, u % 2, 1, c:c + 1], scale=scale,
                                                    accum_out=stat[:, u % 2, 2, c:c + 1])
                    last.then_inc(exp_done.sem, 1)

                def out_half(i, u):
                    act.wait_ge(turned[0].sem, turned[0].at(i * N + (u + 1)))
                    n = halves(u)[0][1]
                    nc.scalar.activation(probsT[:, u % 2, 0:n * P], turned_cols(0, n), ACT.Copy)\
                        .then_inc(probs_out[0].sem, 1)

                with act.Fori(0, passes) as i:
                    exps(i, 0)
                    exps(i, 1)
                    for u in range(N):
                        out_half(i, u)
                        if u + 2 < N:
                            exps(i, u + 2)

            def vector(dve):
                def maxima(i, u):
                    dve.wait_ge(scored.sem, scored.at(i * N + (u + 1)))
                    S = score_cols(u)
                    unit = units[u]
                    for lo, mask in unit["masks"]:
                        nc.vector.tensor_tensor(S[:, lo:lo + P], S[:, lo:lo + P], mask, ALU.add)
                    if unit["sink"] is not None:
                        nc.vector.tensor_copy(S[:, unit["sink"]:unit["sink"] + 1], sink(2 * i + u // U, u % U))
                        dve.drain()
                    view = S.rearrange("p (c n) -> p c n", c=2)[:, 0:2, :] if C == 2 else \
                        S[:, 0:unit["width"]].rearrange("p (c n) -> p c n", c=1)
                    nc.vector.tensor_reduce(stat[:, u % 2, 0, 0:C], view, AX.X, ALU.max, negate=True)
                    dve.drain()
                    nc.vector.tensor_scalar(stat[:, u % 2, 1, 0:C], stat[:, u % 2, 0, 0:C], scale, None, ALU.mult)\
                        .then_inc(max_ready.sem, 1)

                def inverses(i, u):
                    dve.wait_ge(exp_done.sem, exp_done.at(i * N + (u + 1)))
                    last = nc.vector.reciprocal(stat[:, u % 2, 3, 0:C], stat[:, u % 2, 2, 0:C])
                    if C == 2:
                        dve.drain()
                        last = nc.vector.tensor_tensor(stat[:, u % 2, 3, 1:2], stat[:, u % 2, 3, 1:2], neg_lam, ALU.mult)
                    last.then_inc(inverse_ready.sem, 1)

                def differences(i, u):
                    dve.wait_ge(scaled.sem, scaled.at(i * N + (u + 1)))
                    nc.vector.tensor_tensor(probs[:, u % 2, 0:512], probs[:, u % 2, 0:512], probs[:, u % 2, 512:1024], ALU.add)\
                        .then_inc(probs_ready.sem, 1)

                def out_half(i, u):
                    dve.wait_ge(turned[1].sem, turned[1].at(i * N + (u + 1)))
                    lo, hi = halves(u)[1]
                    nc.vector.tensor_copy(probsT[:, u % 2, lo * P:hi * P], turned_cols(1, hi - lo))\
                        .then_inc(probs_out[1].sem, 1)

                def turn_out(i, t):
                    dve.wait_ge(summed.sem, summed.at(2 * i + (t + 1)))
                    dst, src = read_out(2 * i + t, t)
                    nc.vector.tensor_copy(dst, src).then_inc(sum_read.sem, 1)

                nc.vector.memset(stat[:, :, :, :], 0.0).then_inc(sum_read.sem, 2)
                dve.drain()
                with dve.Fori(0, passes) as i:
                    maxima(i, 0)
                    inverses(i, 0)
                    maxima(i, 1)
                    for u in range(N):
                        if C == 2:
                            differences(i, u)
                        if u + 1 < N:
                            inverses(i, u + 1)
                        if shared_out and u == U + 1:
                            turn_out(i, 0)
                        if u + 2 < N:
                            maxima(i, u + 2)
                        out_half(i, u)
                        if not shared_out and u == U + 1:
                            turn_out(i, 0)
                    turn_out(i, 1)

            def gpsimd(pool):
                for z in zeros:
                    nc.gpsimd.memset(z, 0.0)
                pool.drain()
                with pool.Fori(0, passes) as i:
                    for t in range(2):
                        if passes > 1:
                            pool.wait_ge(sum_read.sem, sum_read.at(2 * i + (t + 1)))
                        for n, (dst, src) in enumerate(copies(2 * i + t, t)):
                            if n:
                                pool.drain()
                            last = nc.gpsimd.tensor_copy(dst, src)
                        last.then_inc(staged.sem, 1)
                        pool.drain()
                    for u in range(N):
                        pool.wait_ge(inverse_ready.sem, inverse_ready.at(i * N + (u + 1)))
                        for c in range(C):
                            p = probs[:, u % 2, c * 512:c * 512 + units[u]["keys"] * P]
                            last = nc.gpsimd.tensor_tensor(p, p, stat[:, u % 2, 3, c:c + 1].to_broadcast([P, p.shape[1]]), ALU.mult)
                        last.then_inc(scaled.sem, 1)
                    pool.drain()

            stage(name, tensor=tensor, scalar=scalar, vector=vector, gpsimd=gpsimd)

        def ffn(name, at, h, conv_w, conv_b, func, on_first, gated, work, norm):
            per_turn = RING
            turns, rest = divmod(FT, per_turn)
            pair_done = Signal("pair_done", FT)
            center_ready = Signal("center_ready", FT)
            banks_free = Signal("banks_free", FT + per_turn)
            acted = Signal("acted", FT)
            gated_ready = Signal("gated", FT + 2)
            first_slab = at // SLAB

            def pair(j):
                return [bank[:, 2 * (j % 4) + s, :] for s in range(2)]

            def loop(eng, body, split=None):
                for j in range(rest):
                    if split and j:
                        split(eng, first_slab + j + 1)
                    body(j, j)
                with eng.Fori(0, turns) as it:
                    for j in range(per_turn):
                        if split:
                            split(eng, first_slab + rest, it, j + 1)
                        body(it * per_turn + (rest + j), rest + j)

            def tensor(pe):
                def products(n, j):
                    out_ap = pair(j)
                    pe.wait_ge(slab_split, ws.count(first_slab, n) - WHOLE_SLABS)
                    pe.wait_ge(banks_free.sem, banks_free.at(n + 1))
                    for s in range(2):
                        for k in range(KT):
                            w_hi, w_lo = ws.parts((first_slab + j) * SLAB + s * KT + k)
                            x_hi, x_lo = h.part(pe, k)
                            first = nc.tensor.matmul(out_ap[s], w_hi, x_hi, start=k == 0, stop=False)
                            if s == 0 and k == 0:
                                first.then_inc(slab_begun, 1)
                            nc.tensor.matmul(out_ap[s], w_hi, x_lo, start=False, stop=False)
                            last = nc.tensor.matmul(out_ap[s], w_lo, x_hi, start=False, stop=k == KT - 1)
                    last.then_inc(pair_done.sem, 1)

                assert ws.begun == first_slab and not ws.pending
                norm.sums(pe, range(1))
                loop(pe, products)
                ws.begun += FT

            def scalar(act):
                def centers(n, j):
                    act.wait_ge(pair_done.sem, pair_done.at(n + 1))
                    act.wait_ge(gated_ready.sem, gated_ready.at(n + 1))
                    out_ap = pair(j)
                    for s in range(2):
                        col = n + s * FT
                        last = nc.scalar.activation(work[:, j % 2, s, :], out_ap[s], ACT.Identity,
                                                    bias=conv_b(col), scale=conv_w(2 * FT + col))
                    last.then_inc(center_ready.sem, 1)
                    act.wait_ge(banks_free.sem, banks_free.at(n + (1 + per_turn)))
                    s = 0 if on_first else 1
                    nc.scalar.activation(work[:, j % 2, s, :], work[:, j % 2, s, :], func).then_inc(acted.sem, 1)
                ws.round_to(act, first_slab, ws.limit)
                norm.halfway_scalar = lambda act: ws.round(act, first_slab + 1)
                norm.scalar(act)
                loop(act, centers, ws.round)
                ws.rounded = first_slab + FT + 1

            def vector(dve):
                nc.vector.memset(small[:, 255:256], 0.0).then_inc(banks_free.sem, per_turn)

                def taps(n, j):
                    dve.wait_ge(center_ready.sem, center_ready.at(n + 1))
                    out_ap = pair(j)
                    for lo, tap in ((1, 0), (0, 2)):
                        for s in range(2):
                            col = n + (s * FT + tap * 2 * FT)
                            w = work[:, j % 2, s, lo:lo + T - 1]
                            last = nc.vector.scalar_tensor_tensor(w, out_ap[s][:, 1 - lo:T - lo], conv_w(col), w,
                                                                  ALU.mult, ALU.add)
                        if tap == 0:
                            dve.drain()
                    last.then_inc(banks_free.sem, 1)
                ws.halve_to(dve, first_slab, ws.limit)
                norm.halfway_vector = lambda dve: ws.halve(dve, first_slab + 1)
                norm.vector(dve)
                loop(dve, taps, ws.halve)
                ws.halved = first_slab + FT + 1

            def gpsimd(pool):
                def gate(n, j):
                    pool.wait_ge(acted.sem, acted.at(n + 1))
                    nc.gpsimd.tensor_tensor(gated(n), work[:, j % 2, 0, :], work[:, j % 2, 1, :], ALU.mult)\
                        .then_inc(gated_ready.sem, 1)
                norm.gpsimd(pool)
                nc.gpsimd.memset(small[:, 254:255], 0.0).then_inc(gated_ready.sem, 2)
                loop(pool, gate)

            stage(name, tensor=tensor, scalar=scalar, vector=vector, gpsimd=gpsimd)

        def ffn_down(name, at, x, read_outs=(), post=None):
            places = x.hi.shape[1]
            rounded = Signal("operand_rounded", FT)
            split = Signal("operand_split", FT)
            used = Signal("operand_used", FT)
            sum_done = post.sum_done if post else Signal("tile_done", KT)

            def tensor(pe):
                for k in range(FT):
                    pe.wait_ge(split.sem, split.at(k + 1))
                    parts = x.hi[:, k % places, :], x.lo[:, k, :]
                    for n in range(KT):
                        last = ws.mm(pe, at + k * KT + n, 1, bank[:, n, :], parts, True, k == 0, k == FT - 1)
                        if k == FT - 1:
                            last.then_inc(sum_done.sem, 1)
                            if post and n >= 2:
                                post.sum(pe, n - 2)
                    if k < FT - 1:
                        last.then_inc(used.sem, 1)
                if post:
                    post.sum(pe, KT - 2)
                    post.sum(pe, KT - 1)

            def scalar(act):
                def upper(k):
                    if k >= places:
                        act.wait_ge(used.sem, used.at(k - places + 1))
                    nc.scalar.activation(x.hi[:, k % places, :], x.whole[:, k, :], ACT.Copy).then_inc(rounded.sem, 1)
                upper(0)
                upper(1)
                for k in range(FT):
                    if k + 2 < FT:
                        upper(k + 2)
                    ws.round_to(act, (at + k * KT) // SLAB + 1, ws.limit)
                outs(act, "act")
                if post:
                    for n in range(KT):
                        post.square(act, n)
                    post.rms(act)

            def vector(dve):
                def lower(k):
                    dve.wait_ge(rounded.sem, rounded.at(k + 1))
                    nc.vector.tensor_tensor(x.lo[:, k, :], x.whole[:, k, :],
                                            x.hi[:, k % places, :].bitcast(F32), ALU.subtract).then_inc(split.sem, 1)
                lower(0)
                lower(1)
                for k in range(FT):
                    if k + 2 < FT:
                        lower(k + 2)
                    ws.halve_to(dve, (at + k * KT) // SLAB + 1, ws.limit)
                outs(dve, "dve")
                if post:
                    post.read_first(dve)
                    post.vector(dve)

            def outs(eng, which):
                for n, (engine, read_out) in enumerate(read_outs):
                    if engine == which:
                        eng.wait_ge(sum_done.sem, sum_done.at(n + 1))
                        read_out(eng, bank[:, n, :])

            stage(name, tensor=tensor, scalar=scalar, vector=vector, gpsimd=post and post.gpsimd)

        def project(name, at, x, post):
            rounded = Signal("operand_rounded", KT)
            x.ready = Signal("operand_split", KT)

            def tensor(pe):
                for n in range(KT):
                    for k in range(KT):
                        last = ws.mm(pe, at + n * KT + k, 1, bank[:, n, :], x.part(pe, k), True, k == 0, k == KT - 1)
                    last.then_inc(post.sum_done.sem, 1)
                    if n >= 2:
                        post.sum(pe, n - 2)
                post.sum(pe, KT - 2)
                post.sum(pe, KT - 1)

            def scalar(act):
                ws.round_to(act, at // SLAB, ws.limit)
                for k in range(KT):
                    nc.scalar.activation(x.hi[:, k, :], x.whole[:, k, :], ACT.Copy).then_inc(rounded.sem, 1)
                for n in range(KT):
                    ws.round_to(act, (at + n * KT + KT - 1) // SLAB + 1, ws.limit)
                    post.square(act, n)
                post.rms(act)

            def vector(dve):
                ws.halve_to(dve, at // SLAB, ws.limit)
                for k in range(KT):
                    dve.wait_ge(rounded.sem, rounded.at(k + 1))
                    nc.vector.tensor_tensor(x.lo[:, k, :], x.whole[:, k, :], x.hi[:, k, :].bitcast(F32), ALU.subtract)\
                        .then_inc(x.ready.sem, 1)
                for n in range(KT):
                    ws.halve_to(dve, (at + n * KT + KT - 1) // SLAB + 1, ws.limit)
                    if n == 0:
                        post.read_first(dve)
                post.vector(dve)

            stage(name, tensor=tensor, scalar=scalar, vector=vector, gpsimd=post.gpsimd)

        def scan_branch(all_keys, all_sums, q, v, y, work):
            H = C_HEADS
            DIRS = 2
            o_read = Signal("head_read", H + 1)
            values_staged = Signal("values_staged", H)
            keys_staged = Signal("keys_staged", H)
            inter_arg = [Signal(f"inter_arg{d}", H) for d in range(DIRS)]
            inter_exp = [Signal(f"inter_exp{d}", H) for d in range(DIRS)]
            inter_ready = [Signal(f"inter_ready{d}", H) for d in range(DIRS)]
            keys_turned = [Signal(f"keys_turned{d}", H) for d in range(DIRS)]
            keys_out = [Signal(f"keys_out{d}", H) for d in range(DIRS)]
            updates_done = [Signal(f"updates_done{d}", H) for d in range(DIRS)]
            states_ready = [Signal(f"states_ready{d}", H) for d in range(DIRS)]
            arg_ready = [Signal(f"arg_ready{d}", LEVELS * H) for d in range(DIRS)]
            decay_ready = [Signal(f"decay_ready{d}", LEVELS * H) for d in range(DIRS)]
            mixed_ready = [Signal(f"mixed_ready{d}", LEVELS * H) for d in range(DIRS)]
            level_done = [Signal(f"level_done{d}", (LEVELS + 1) * H) for d in range(DIRS)]
            masked_ready = [Signal(f"masked_ready{d}", (LEVELS + 1) * H) for d in range(DIRS)]
            intra_done = [Signal(f"intra_done{d}", (LEVELS + 1 - d) * H) for d in range(DIRS)]
            head_done = Signal("head_done", H)
            order = [list(range(CB + TB)), [1, 0] + list(range(CB + TB - 1, CB - 1, -1))]
            t_half, j_half = [1, 0], [0, 1]
            t1 = work["t1"]
            sums1, keys1 = work["sums1"], work["keys1"]
            mixed, masked = work["mixed"], work["masked"]
            keys_n, states = work["keys_n"], work["states"]
            NB = CB + TB
            queries, vh, tot = work["queries"], work["vh"], work["tot"]
            qh = work["qh"]
            O = bank[:, 0, :]
            turn_bank = bank[:, 3:5, :].rearrange("p b n -> p (b n)")
            update_bank = bank[:, 5:7, :].rearrange("p b n -> p (b n)")

            def head(ap, i):
                return ap[:, bass.ds(i, 1), :].rearrange("p o n -> p (o n)")

            def split(ap, m):
                return ap.rearrange("p (b h m) -> p b h m", h=2, m=m)

            def scalar(act):
                nc.scalar.activation(tot[:, 0, 0, 0:1], con("one", 1), ACT.Copy).then_inc(o_read.sem, 1)
                with act.Fori(0, H) as i:
                    act.wait_ge(o_read.sem, o_read.at(i + 1))
                    nc.scalar.activation(sums1, head(all_sums[1], i), ACT.Copy)
                    nc.scalar.activation(keys1, head(all_keys[1], i), ACT.Copy).then_inc(keys_staged.sem, 1)
                    for d in range(DIRS):
                        act.wait_ge(inter_arg[d].sem, inter_arg[d].at(i + 1))
                        nc.scalar.activation(t1[:, d, :], t1[:, d, :], ACT.Exp)
                        nc.scalar.activation(tot[:, d, 1, 0:NB], tot[:, d, 0, 0:NB], ACT.Exp)
                        nc.scalar.activation(queries[:, d, :], queries[:, d, :], ACT.Exp).then_inc(inter_exp[d].sem, 1)
                    for d in range(DIRS):
                        act.wait_ge(keys_turned[d].sem, keys_turned[d].at(i + 1))
                        nc.scalar.activation(keys_n[:, d, :, :].rearrange("p b n -> p (b n)"), turn_bank[:, 0:NB * P],
                                             ACT.Copy).then_inc(keys_out[d].sem, 1)
                    for l in range(LEVELS):
                        for d in range(DIRS):
                            act.wait_ge(arg_ready[d].sem, arg_ready[d].at(i * LEVELS + (l + 1)))
                            nc.scalar.activation(mixed[:, d, l % 2, :], mixed[:, d, l % 2, :], ACT.Exp)\
                                .then_inc(decay_ready[d].sem, 1)
                    act.wait_ge(head_done.sem, head_done.at(i + 1))
                    nc.scalar.activation(head(y, i), O, ACT.Copy).then_inc(o_read.sem, 1)

            def direction(eng, ops, d, i, q_head, sums, keys):
                near, far = (1, 0) if d == 0 else (0, 1)
                edge = CHUNK - 1 if d == 0 else 0
                lat = sums[:, CT:ALLT]

                def inter_args():
                    a = split(sums, CHUNK)
                    tn, tf = a[:, :, near, edge:edge + 1], a[:, :, far, edge:edge + 1]
                    both = tot[:, d, 0, 0:NB].rearrange("p (b o) -> p b o", o=1)
                    ops.tensor_tensor(both, tn, tf, ALU.add)
                    k = split(t1[:, d, :], CHUNK)
                    ops.tensor_tensor(k[:, :, near, :], tn.to_broadcast([P, NB, CHUNK]), a[:, :, near, :], ALU.subtract)
                    qx, al = split(queries[:, d, :], CHUNK), split(lat, CHUNK)
                    ops.tensor_copy(qx[:, :, far, :], al[:, :, far, :])
                    ops.tensor_tensor(qx[:, :, near, :], al[:, :, near, :],
                                      al[:, :, far, edge:edge + 1].to_broadcast([P, TB, CHUNK]), ALU.add)
                    eng.drain()
                    ops.tensor_tensor(k[:, :, far, :], both.to_broadcast([P, NB, CHUNK]), a[:, :, far, :], ALU.subtract)\
                        .then_inc(inter_arg[d].sem, 1)

                def inter_products():
                    eng.wait_ge(inter_exp[d].sem, inter_exp[d].at(i + 1))
                    ops.tensor_tensor(t1[:, d, :], t1[:, d, :], keys, ALU.mult)
                    ops.tensor_tensor(queries[:, d, :], queries[:, d, :], q_head, ALU.mult)\
                        .then_inc(inter_ready[d].sem, 1)

                def args(l):
                    m = CHUNK >> l
                    nb = T // (2 * m)
                    if l >= 2:
                        eng.wait_ge(level_done[d].sem, level_done[d].at(i * (LEVELS + 1) + (l - 1)))
                    a, x = split(lat, m), split(mixed[:, d, l % 2, :], m)
                    e = m - 1 if d == 0 else 0
                    ref = a[:, :, j_half[d], e:e + 1].to_broadcast([P, nb, m])
                    ops.tensor_tensor(x[:, :, j_half[d], :], ref, a[:, :, j_half[d], :], ALU.subtract)
                    if l == 0:
                        last = ops.tensor_copy(x[:, :, t_half[d], :], a[:, :, t_half[d], :])
                    else:
                        last = ops.tensor_tensor(x[:, :, t_half[d], :], a[:, :, t_half[d], :], ref, ALU.subtract)
                    last.then_inc(arg_ready[d].sem, 1)

                def products(l):
                    m = CHUNK >> l
                    eng.wait_ge(decay_ready[d].sem, decay_ready[d].at(i * LEVELS + (l + 1)))
                    x = split(mixed[:, d, l % 2, :], m)
                    ops.tensor_tensor(x[:, :, t_half[d], :], x[:, :, t_half[d], :],
                                      split(q_head, m)[:, :, t_half[d], :], ALU.mult)
                    ops.tensor_tensor(x[:, :, j_half[d], :], x[:, :, j_half[d], :],
                                      split(keys[:, CT:ALLT], m)[:, :, j_half[d], :], ALU.mult)\
                        .then_inc(mixed_ready[d].sem, 1)
                return inter_args, inter_products, args, products

            def vector(dve):
                with dve.Fori(0, H) as i:
                    dve.wait_ge(o_read.sem, o_read.at(i + 1))
                    inter_args, inter_products, args, products = direction(
                        dve, nc.vector, 0, i, head(q, i), head(all_sums[0], i), head(all_keys[0], i))
                    inter_args()
                    args(0)
                    args(1)
                    inter_products()
                    for d in range(DIRS):
                        dve.wait_ge(updates_done[d].sem, updates_done[d].at(i + 1))
                        U = update_bank
                        first = order[d][0]
                        nc.vector.tensor_copy(states[:, d, 1, :], U[:, first * P:(first + 1) * P])
                        for n in range(1, NB - 1):
                            b = order[d][n]
                            dve.drain()
                            last = nc.vector.scalar_tensor_tensor(states[:, d, n + 1, :], states[:, d, n, :],
                                                                  tot[:, d, 1, b:b + 1], U[:, b * P:(b + 1) * P],
                                                                  ALU.mult, ALU.add)
                        last.then_inc(states_ready[d].sem, 1)

                    def masks(l):
                        for d in range(DIRS):
                            dve.wait_ge(level_done[d].sem, level_done[d].at(i * (LEVELS + 1) + (l + 1)))
                            if l >= 2:
                                dve.wait_ge(intra_done[d].sem, intra_done[d].at(i * (LEVELS + 1 - d) + (l - 1)))
                            mask = con("levels", P, (d * (LEVELS + 1) + l) * P).rearrange("p (o n) -> p o n", o=1)
                            nc.vector.tensor_tensor(masked[:, d, l % 2, :].rearrange("p (b n) -> p b n", n=P),
                                                    bank[:, 1 + d, :].rearrange("p (b n) -> p b n", n=P),
                                                    mask.to_broadcast([P, TB, P]), ALU.mult)\
                                .then_inc(masked_ready[d].sem, 1)
                    for l in range(LEVELS):
                        products(l)
                        if l >= 1:
                            masks(l - 1)
                        if l + 2 < LEVELS:
                            args(l + 2)
                    masks(LEVELS - 1)
                    masks(LEVELS)

            def gpsimd(pool):
                with pool.Fori(0, H) as i:
                    pool.wait_ge(o_read.sem, o_read.at(i + 1))
                    inter_args, inter_products, args, products = direction(pool, nc.gpsimd, 1, i, qh, sums1, keys1)
                    nc.gpsimd.tensor_copy(qh, head(q, i))
                    nc.gpsimd.tensor_copy(vh, v[:, :, bass.ds(i, 1), :].rearrange("p b o n -> p b (o n)"))\
                        .then_inc(values_staged.sem, 1)
                    pool.drain()
                    pool.wait_ge(keys_staged.sem, keys_staged.at(i + 1))
                    inter_args()
                    args(0)
                    args(1)
                    inter_products()
                    for l in range(LEVELS):
                        products(l)
                        if l + 2 < LEVELS:
                            args(l + 2)

            def tensor(pe):
                with pe.Fori(0, H) as i:
                    pe.wait_ge(o_read.sem, o_read.at(i + 1))
                    pe.wait_ge(values_staged.sem, values_staged.at(i + 1))
                    for d in range(DIRS):
                        pe.wait_ge(inter_ready[d].sem, inter_ready[d].at(i + 1))
                        if d == 1:
                            pe.wait_ge(keys_out[0].sem, keys_out[0].at(i + 1))
                        for b in range(NB):
                            last = nc.tensor.transpose(turn_bank[:, b * P:(b + 1) * P], t1[:, d, b * P:(b + 1) * P],
                                                       con("ident"))
                        last.then_inc(keys_turned[d].sem, 1)
                    for d in range(DIRS):
                        pe.wait_ge(keys_out[d].sem, keys_out[d].at(i + 1))
                        if d == 1:
                            pe.wait_ge(states_ready[0].sem, states_ready[0].at(i + 1))
                        for b in order[d][0:NB - 1]:
                            last = nc.tensor.matmul(update_bank[:, b * P:(b + 1) * P], keys_n[:, d, b, :], vh[:, b, :],
                                                    start=True, stop=True)
                        last.then_inc(updates_done[d].sem, 1)
                    for d in range(DIRS):
                        pe.wait_ge(states_ready[d].sem, states_ready[d].at(i + 1))
                        for n in range(CB, NB):
                            b = order[d][n] - CB
                            nc.tensor.matmul(O[:, b * P:(b + 1) * P], states[:, d, n, :], queries[:, d, b * P:(b + 1) * P],
                                             start=d == 0 and n == CB, stop=False, skip_group_check=True)

                    def level(l):
                        for d in range(DIRS):
                            if l >= 1:
                                pe.wait_ge(masked_ready[d].sem, masked_ready[d].at(i * (LEVELS + 1) + l))
                            if l < LEVELS:
                                pe.wait_ge(mixed_ready[d].sem, mixed_ready[d].at(i * LEVELS + (l + 1)))
                            for b in range(TB):
                                c = slice(b * P, (b + 1) * P)
                                if l < LEVELS:
                                    lhsT = rhs = mixed[:, d, l % 2, c]
                                else:
                                    lhsT = qh[:, c]
                                    rhs = all_keys[d][:, bass.ds(i, 1), CT + b * P:CT + (b + 1) * P].rearrange("p o n -> p (o n)")
                                last = nc.tensor.matmul(bank[:, 1 + d, c], lhsT, rhs, start=True, stop=True)
                            last.then_inc(level_done[d].sem, 1)

                    def intra(l):
                        for d in range(DIRS):
                            pe.wait_ge(masked_ready[d].sem, masked_ready[d].at(i * (LEVELS + 1) + (l + 1)))
                            for b in range(TB):
                                c = slice(b * P, (b + 1) * P)
                                end = l == LEVELS and d == 1 and b == TB - 1
                                last = nc.tensor.matmul(O[:, c], vh[:, CB + b, :], masked[:, d, l % 2, c], start=False,
                                                        stop=end, skip_group_check=True)
                            last.then_inc((head_done if end else intra_done[d]).sem, 1)
                    level(0)
                    for l in range(LEVELS):
                        level(l + 1)
                        intra(l)
                    intra(LEVELS)

            stage("scan", tensor=tensor, scalar=scalar, vector=vector, gpsimd=gpsimd)

        params_in = Signal("params_in", 16)
        inputs_loaded = Signal("inputs_loaded", 16 * 3)
        tables = sb("tables", [P, 4, T])
        COS_MLA, SIN_MLA, COS_DIFF, SIN_DIFF = (tables[:, n, :] for n in range(4))

        phase = stack.enter_context(ExitStack())

        def tmp(name, shape, where=None, dt=F32):
            return new(where or phase, name, shape, dt)

        yc = tmp("yc", [P, 4, T])
        yc_lo = same_place("yc_lo", "yc", [P, 4, T], F32R)
        hcT = tmp("hcT", [P, KT, CT])
        hc_lo = same_place("hc_lo", "hcT", [P, KT, CT], F32R)
        hc_hi = tmp("hc_hi", [P, KT, CT], None, F32R)
        mod = tmp("mod", [P, MOD_TILES, 2])
        gain_x = tmp("gain_x", [P, KT, 2])
        gain_f = tmp("gain_f", [P, KT])
        sc = tmp("sc", [P, KT, 2])
        lb = tmp("lb", [P, 2, 2 * C_HEADS])
        sink8 = tmp("sink8", [P, 8])

        with ExitStack() as here:
            pos_i = tmp("pos_i", [P, T], here, I32)
            ang = tmp("ang", [P, 4, T], here)
            scr = tmp("scr", [P, 4, 2 * C_HEADS], here)
            c_ready = Signal("c_ready", 1)
            rows = tmp("mod_rows", [2, MOD_TILES * P], here)
            GROUPS = MOD_TILES // 4
            group_done = Signal("group_done", GROUPS)
            rows_ready = Signal("rows_ready", GROUPS)
            mod_done = Signal("mod_done", 1)
            lb_sub = Signal("lb_sub", 1)
            lb_exp = Signal("lb_exp", 1)
            angles_ready = Signal("angles_ready", 1)
            abs_ready = Signal("abs_ready", 1)
            mod_ready = Signal("mod_ready", 1)

            def sync(sp):
                sp.dma_start(par1[:, :], par1_in).then_inc(params_in.sem, 16)
                ws.feed(sp, RING)
                sp.dma_start(const[:, :], const_in).then_inc(inputs_loaded.sem, 16)
                sp.dma_start(xT[:, :, :], xT_in).then_inc(inputs_loaded.sem, 16)
                sp.dma_start(pos_i[:, :], pos_in.to_broadcast([P, T])).then_inc(inputs_loaded.sem, 16)

            def scalar(act):
                act.wait_ge(params_in.sem, 16)
                nc.scalar.activation(sc[:, :, :].rearrange("p k s -> p (k s)"), p1("c", 2 * KT), ACT.Silu)\
                    .then_inc(c_ready.sem, 1)
                act.wait_ge(lb_sub.sem, lb_sub.at(1))
                nc.scalar.activation(scr[:, 1, :], scr[:, 0, :], ACT.Exp).then_inc(lb_exp.sem, 1)
                act.wait_ge(angles_ready.sem, angles_ready.at(1))
                for n in range(2):
                    nc.scalar.activation(ang[:, 2 + n, :], ang[:, n, :], ACT.Abs)
                act.drain()
                for n in range(2):
                    nc.scalar.activation(tables[:, 2 * n + 1, :], ang[:, n, :], ACT.Sin)
                    nc.scalar.activation(tables[:, 2 * n, :], ang[:, 2 + n, :], ACT.Sin, bias=con("half_pi", 1), scale=-1.0)
                act.drain()
                for g in range(GROUPS):
                    act.wait_ge(group_done.sem, group_done.at(g + 1))
                    nc.scalar.activation(rows[:, g * 512:(g + 1) * 512], bank[0:2, 1 + g % 4, :], ACT.Copy)\
                        .then_inc(rows_ready.sem, 1)

            def tensor(pe):
                def turn(g):
                    pe.wait_ge(rows_ready.sem, rows_ready.at(g + 1))
                    for e in range(4):
                        n = 4 * g + e
                        last = nc.tensor.transpose(bank[:, 0, 2 * n:2 * n + 2], rows[:, n * P:(n + 1) * P], con("ident", 2)[0:2, :])
                    return last
                pe.wait_ge(c_ready.sem, c_ready.at(1))
                for g in range(GROUPS):
                    if g >= 4:
                        pe.wait_ge(rows_ready.sem, rows_ready.at(g - 3))
                    for k in range(KT):
                        b = B1_AT["mod"] + (g * KT + k) * 4
                        last = ws.mm_whole(pe, b, bank[0:2, 1 + g % 4, :], sc[:, k, :], k == 0, k == KT - 1)
                    last.then_inc(group_done.sem, 1)
                    if g == 2:
                        pe.wait_ge(inputs_loaded.sem, 16 * 3)
                    if g >= 2:
                        turn(g - 2)
                turn(GROUPS - 2)
                turn(GROUPS - 1).then_inc(mod_done.sem, 1)

            def vector(dve):
                dve.wait_ge(params_in.sem, 16)
                dve.wait_ge(inputs_loaded.sem, 16 * 3)
                nc.vector.tensor_tensor(scr[:, 0, :], p1("lb", 8), p1("lb", 8), ALU.subtract).then_inc(lb_sub.sem, 1)
                nc.vector.tensor_scalar(sink8[:, :], p1("sink", 8), float(HD) ** 0.5, None, ALU.mult)
                nc.vector.tensor_copy(ang[:, 3, :], pos_i[:, :])
                dve.drain()
                two_pi = 2 * np.pi
                parts, left = [], two_pi
                for bits in (7, 15):
                    part = np.floor(left * 2.0 ** bits) / 2.0 ** bits
                    parts.append(float(np.float32(part)))
                    left -= parts[-1]
                parts.append(float(np.float32(left)))
                magic = 1.5 * 2.0 ** 23
                for n in (0, 1):
                    a, r = ang[:, n, :], ang[:, 2, :]
                    nc.vector.tensor_scalar(a, ang[:, 3, :], con("freq", 1, n), None, ALU.mult)
                    dve.drain()
                    nc.vector.tensor_scalar(r, a, 1.0 / two_pi, magic, ALU.mult, ALU.add)
                    dve.drain()
                    nc.vector.tensor_scalar(r, r, magic, None, ALU.subtract)
                    dve.drain()
                    for part in parts:
                        nc.vector.scalar_tensor_tensor(a, r, -part, a, ALU.mult, ALU.add)
                        dve.drain()
                    last = nc.vector.tensor_scalar(a, a, -3.1415925, 3.1415925, ALU.max, ALU.min)
                    dve.drain()
                nc.vector.tensor_copy(ang[:, 2, 0:1], ang[:, 0, 0:1]).then_inc(angles_ready.sem, 1)
                dve.wait_ge(lb_exp.sem, lb_exp.at(1))
                nc.vector.reciprocal(scr[:, 2, :], scr[:, 1, :])
                dve.drain()
                nc.vector.tensor_tensor(scr[:, 1, :], scr[:, 1, :], scr[:, 2, :], ALU.mult)
                dve.drain()
                nc.vector.tensor_tensor(scr[:, 2, :], scr[:, 1, :], scr[:, 1, :], ALU.subtract)
                dve.drain()
                nc.vector.tensor_scalar(lb[:, 0, :], scr[:, 2, :], 0.0, 1.0, ALU.max, ALU.min)
                dve.drain()
                nc.vector.tensor_scalar(lb[:, 1, :], lb[:, 0, :], -1.0, 1.0, ALU.mult, ALU.add)
                dve.wait_ge(mod_done.sem, mod_done.at(1))
                nc.vector.tensor_tensor(mod[:, :, :], bank[:, 0, 0:2 * MOD_TILES].rearrange("p (n s) -> p n s", s=2),
                                        bcast(p1("b_mod", MOD_TILES), 2), ALU.add)
                dve.drain()
                nc.vector.scalar_tensor_tensor(gain_x[:, :, :], mod[:, KT:2 * KT, :], 1.0, bcast(p1("norm_mix", KT), 2),
                                               ALU.add, ALU.mult)
                nc.vector.scalar_tensor_tensor(gain_f[:, :], mod[:, 4 * KT:5 * KT, 0], 1.0, p1("norm_ffn", KT),
                                               ALU.add, ALU.mult).then_inc(mod_ready.sem, 1)

            stage("modulation", tensor=tensor, scalar=scalar, vector=vector, sync=sync)

        branches = stack.enter_context(ExitStack())
        h, hc = Split(h_hi, h_lo), Split(hc_hi, hc_lo)

        def tokens(tb):
            x, at = (hc, tb) if tb < CB else (h, tb - CB)
            return lambda pe, k: x.part(pe, k, slice(at * P, (at + 1) * P))

        def attend(which, b, windowed, sync=None):
            at = B1_AT[which]
            with ExitStack() as s:
                qk = tmp(f"qk{which}", [P, 4, T], s)
                k = tmp(f"k{which}", [P, ALLT], s)
                v = tmp(f"v{which}", [P, CB + TB, P], s)
                tiles = [("act", T, weights_still(at + n * KT, KT, h), act_copy(qk[:, n, :])) for n in range(4)]
                tiles.append(("act", T, weights_still(at + 4 * KT, KT, h), act_copy(k[:, CT:ALLT])))
                tiles.append(("act", CT, weights_still(at + 4 * KT, KT, hc), act_copy(k[:, 0:CT])))
                values = weights_moving(at + 5 * KT, KT, 1, [tokens(tb) for tb in range(CB + TB)])
                for tb in range(CB + TB):
                    tiles.append(("dve", P, values, dve_copy(v[:, tb, :])))
                linear(f"proj{which}", tiles, sync=sync)
                if not windowed:
                    with ExitStack() as n:
                        squares = tmp("squaresB", [P, SQUARES, T], n)
                        scales = tmp("scalesB", [P, 2, T], n)
                        jobs = [(qk[:, m, :], T, "qn") for m in range(4)] + \
                            [(k[:, CT:ALLT], T, "kn"), (k[:, 0:CT], CT, "kn")]
                        norms("norm_heads", [
                            dict(src=lambda kt, ap=ap: ap, tiles=1, cols=cols, ones=con("ones64"), inv=1.0 / HD,
                                 gain=lambda kt, g=g: p1(g), out=lambda kt, ap=ap: ap, end=None)
                            for ap, cols, g in jobs], squares, scales)
                with ExitStack() as r:
                    work = tmp(f"rope{which}", [P, 4, T], r)
                    rope(f"rope{which}", [(ap, con("rot1"), axial[:, 0, :], axial[:, 1, :], ap)
                                          for ap in [qk[:, m, :] for m in range(4)] + [k[:, CT:ALLT]]], work)
                with ExitStack() as a:
                    qpad = tmp(f"qpad{which}", [P, 2, 2, T], a)
                    work = (tmp(f"probs{which}", [P, 2, 1024], a), tmp(f"probsT{which}", [P, 2, ALLT], a),
                            tmp(f"stat{which}", [P, 2, 4, 2], a))
                    units = [[], []]
                    for t, g in ((t, g) for t in range(2) for g in range(2)):
                        for tb in range(TB):
                            lo, hi = (max(0, tb - 1), min(TB, tb + 2)) if windowed else (0, TB)
                            width = CT + (hi - lo) * P
                            key_cols = [(0, CT, 0), (CT, min(width, 512), CT + lo * P)]
                            if width > 512:
                                key_cols.append((512, width, 512 + lo * P))
                            qs = qpad[:, t, g, tb * P:(tb + 1) * P]
                            masks = []
                            if windowed and lo < tb:
                                masks.append((CT, con("mask_prev")))
                            if windowed and hi > tb + 1:
                                masks.append((width - P, con("mask_next")))
                            blocks = list(range(CB)) + [CB + x for x in range(lo, hi)]
                            units[t].append(dict(
                                scores=[lambda i, qs=qs, kc=key_cols: [(a0, a1, [(qs, k[:, s0:s0 + a1 - a0])])
                                                                       for a0, a1, s0 in kc]],
                                width=width + (1 if windowed else 0), masks=masks,
                                sink=width if windowed else None, group=g, keys=width // P,
                                values=[(bank[g * HD:(g + 1) * HD, 6 + t, tb * P:(tb + 1) * P],
                                         [v[:, x, g * HD:(g + 1) * HD] for x in blocks])]))

                    def copies(i, t):
                        return [(qpad[g * HD:(g + 1) * HD, t, g, :],
                                 qk[g * HD:(g + 1) * HD, bass.ds(i, 1), :].rearrange("p o n -> p (o n)"))
                                for g in range(2)]
                    attention(f"attend{which}", 4, units, HD ** -0.5, copies,
                              [qpad[HD:P, :, 0, :], qpad[0:HD, :, 1, :]],
                              lambda i, t: (yab[:, b, bass.ds(i, 1), :].rearrange("p o n -> p (o n)"), bank[:, 6 + t, :]),
                              work, sink=lambda i, u: sink8[:, bass.ds(i + 4 * units[0][u]["group"], 1)])

        with ExitStack() as s:
            z = tmp("z", [P, 2, C_HEADS, ALLT], s)
            cq = tmp("cq", [P, C_HEADS, T], s)
            v = tmp("vC", [P, CB + TB, C_HEADS, P], s)
            at = B1_AT["C"]
            ROWS = 2 * C_HEADS
            in_x = xT[:, :, :].rearrange("p k t -> p (k t)")
            sums = [in_x[:, 0:C_HEADS * ALLT].rearrange("p (n t) -> p n t", n=C_HEADS), tmp("scan_sums", [P, C_HEADS, ALLT], s)]
            logs = tmp("scan_logs", [P, 2, 2, ALLT], s)
            logs_ready = Signal("logs_ready", ROWS)
            softplus_ready = Signal("softplus_ready", ROWS)
            sums_ready = Signal("sums_ready", ROWS)
            keys_exp = Signal("keys_exp", ROWS)

            def row_of(r):
                return r // C_HEADS, r % C_HEADS

            def row_keys(act, r):
                d, n = row_of(r)
                act.wait_ge(softplus_ready.sem, softplus_ready.at(r + 1))
                nc.scalar.activation(z[:, d, n, :], z[:, d, n, :], ACT.Exp, scale=-1.0).then_inc(keys_exp.sem, 1)

            def row_logs(act, r):
                d, n = row_of(r)
                l1, l2 = logs[:, 0, r % 2, :], logs[:, 1, r % 2, :]
                if r >= 2:
                    act.wait_ge(sums_ready.sem, sums_ready.at(r - 1))
                act.drain()
                nc.scalar.activation(l1, z[:, d, n, :], ACT.Abs)
                nc.scalar.activation(l2, z[:, d, n, :], ACT.Exp, scale=-1.0)
                act.drain()
                nc.scalar.activation(l1, l1, ACT.Exp, scale=-1.0)
                if r >= 1:
                    row_keys(act, r - 1)
                act.drain()
                nc.scalar.activation(l2, l2, ACT.Ln, bias=con("one", 1), scale=lb[:, 0, r:r + 1])
                nc.scalar.activation(l1, l1, ACT.Ln, bias=con("one", 1)).then_inc(logs_ready.sem, 1)

            def row_sums(dve, r):
                d, n = row_of(r)
                l1, l2, zr, sr = logs[:, 0, r % 2, :], logs[:, 1, r % 2, :], z[:, d, n, :], sums[d][:, n, :]
                dve.wait_ge(logs_ready.sem, logs_ready.at(r + 1))
                nc.vector.scalar_tensor_tensor(sr, zr, 0.0, l1, ALU.min, ALU.subtract)
                dve.drain()
                nc.vector.scalar_tensor_tensor(zr, zr, 0.0, l1, ALU.max, ALU.add).then_inc(softplus_ready.sem, 1)
                nc.vector.tensor_tensor(l2, sr, l2, ALU.add)
                dve.drain()
                step = 1 if d == 0 else -1
                nc.vector.tensor_tensor_scan(sr[:, ::step], con("reset", ALLT, d * ALLT)[:, ::step], l2[:, ::step], 0.0,
                                             ALU.mult, ALU.add).then_inc(sums_ready.sem, 1)

            def rows_scaled(pool):
                for r in range(ROWS):
                    d, n = row_of(r)
                    pool.wait_ge(keys_exp.sem, keys_exp.at(r + 1))
                    nc.gpsimd.tensor_scalar(z[:, d, n, :], z[:, d, n, :], lb[:, 1, r:r + 1], None, ALU.mult)

            tiles = [("act", T, weights_still(at + n * KT, KT, h), act_copy(cq[:, n, :], ACT.Silu)) for n in range(C_HEADS)]
            also = {}
            for r in range(ROWS):
                d, n = row_of(r)
                b = at + (4 + r) * KT
                if r >= 1:
                    also["dve", len(tiles)] = lambda dve, r=r: row_sums(dve, r - 1)
                tiles.append(("act", T, weights_still(b, KT, h), act_copy(z[:, d, n, CT:ALLT])))
                tiles.append(("act", CT, weights_still(b, KT, hc), act_copy(z[:, d, n, 0:CT])))
                also["act", len(tiles)] = lambda act, r=r: row_logs(act, r)
            also["dve", len(tiles)] = lambda dve: row_sums(dve, ROWS - 1)
            also["act", len(tiles) + 1] = lambda act: row_keys(act, ROWS - 1)
            values = weights_moving(at + 12 * KT, KT, 4, [tokens(tb) for tb in range(CB + TB)])
            for tb in range(CB + TB):
                tiles.append(("dve", 512, values, dve_copy(v[:, tb, :, :].rearrange("p h n -> p (h n)"))))
            ctxT = same_place("ctxT", "vC", [P, KT, CT], F32)
            squares = same_place("squares1", "scan_logs", [P, SQUARES, T], F32)
            scales = nc.alloc_sbuf_tensor_at("scales1", [P, 2, T], F32, offset=place["scan_logs"] + SQUARES * T * 4)
            ctx_in = Signal("context_loaded", 16)

            def load_context(sp):
                sp.dma_start(ctxT[:, :, :], ctxT_in).then_inc(ctx_in.sem, 16)
            norm = Norms([
                dict(src=lambda k: xT[:, k, :], tiles=KT, cols=T, ones=con("ones"), inv=1.0 / D,
                     gain=lambda k: gain_x[:, k, 0:1], out=lambda k: hT[:, k, :],
                     end=("split", split_hi, split_lo, lambda k: mod[:, k, 0:1])),
                dict(src=lambda k: ctxT[:, k, :], tiles=KT, cols=CT, ones=con("ones"), inv=1.0 / D,
                     gain=lambda k: gain_x[:, k, 1:2], out=lambda k: hcT[:, k, :],
                     end=("split", lambda k: hc_hi[:, k, :], lambda k: hc_lo[:, k, :], lambda k: mod[:, k, 1:2]))],
                squares, scales, load_context, loaded=(1, ctx_in), splits=[(h, 0), (hc, KT)])
            after_c = B1_AT["A"] // SLAB
            ws.limit = after_c + 1
            linear("projC", tiles, last_split=after_c, norm=norm, also=also, pool_also=rows_scaled)
            h.ready = hc.ready = None
            free = [(after_c + 1 + m) % RING for m in range(RING - 1)]
            work = {}
            work["keys1"], work["sums1"] = (ring[:, free[0], :, :].rearrange("p b n -> p (b n)")[:, m * ALLT:(m + 1) * ALLT]
                                            for m in range(2))
            work["mixed"], work["masked"] = (ring[:, free[1 + m], :, :].rearrange("p (d n a) c -> p d n (a c)", d=2, n=2)
                                             for m in range(2))
            size = 2 * (CB + TB) * P
            work["keys_n"], work["states"] = (ring_spare[:, m * size:(m + 1) * size].rearrange("p (d b n) -> p d b n", d=2, n=P)
                                              for m in range(2))
            work["qh"] = ring_spare[:, 2 * size:2 * size + T]
            work["vh"] = in_x[:, C_HEADS * ALLT:C_HEADS * ALLT + (CB + TB) * P].rearrange("p (b n) -> p b n", n=P)
            work["tot"] = tmp("scan_tot", [P, 2, 2, 8], s)
            work["t1"], work["queries"] = logs[:, 0, :, :], logs[:, 1, :, 0:T]
            scan_branch([z[:, d, :, :] for d in range(2)], sums, cq, v, yc, work)
            ws.limit = B1_SLABS

        yab = tmp("yab", [P, 2, 4, T], branches)
        yab_lo = same_place("yab_lo", "yab", [P, 2, 4, T], F32R)
        axial = tmp("axial", [P, 2, T], branches)
        x_again = Signal("x_loaded", 32)

        def load_x(sp):
            sp.dma_start(axial[:, :, :], axial_in).then_inc(x_again.sem, 16)
            sp.dma_start(xT[:, :, :], xT_in).then_inc(x_again.sem, 16)
            sp.wait_ge(x_again.sem, x_again.at(32))
        attend("A", 0, True, load_x)
        attend("B", 1, False)

        with ExitStack() as here:
            cg = tmp("cg", [P, C_HEADS, T], here)
            squares = tmp("squaresC", [P, SQUARES, T], here)
            scales = tmp("scalesC", [P, 2, T], here)
            linear("gate_c", [("act", T, weights_still(B1_AT["cg"] + n * KT, KT, h), act_copy(cg[:, n, :], ACT.Silu))
                              for n in range(C_HEADS)])
            norms("norm_c", [dict(src=lambda k, n=n: yc[:, n, :], tiles=1, cols=T, ones=con("ones"), inv=1.0 / P,
                                  gain=lambda k: p1("gn"), out=lambda k, n=n: yc[:, n, :],
                                  end=("times", lambda k, n=n: cg[:, n, :])) for n in range(C_HEADS)],
                  squares, scales)
        with ExitStack() as here:
            merged = tmp("merged", [P, KT, T], here)
            gates = tmp("gates", [P, 6, T], here)
            part = tmp("part", [P, 2, T], here)
            yb_hi = tmp("yb_hi", [P, 4, T], here, F32R)
            old = [x[:, :, :].rearrange("p (k a) c -> p k (a c)", a=2) for x in (hc_hi, hc_lo)]
            ys = [Split(old[0], yab_lo[:, 0, :, :], yab[:, 0, :, :]), Split(yb_hi, yab_lo[:, 1, :, :], yab[:, 1, :, :]),
                  Split(old[1], yc_lo, yc)]
            tiles = []

            def add_branch(n, b):
                def read_out(dve, ps):
                    g = gates[:, (3 * n + b) % 6, :]
                    if b == 0:
                        return nc.vector.tensor_tensor(merged[:, n, :], ps, g, ALU.mult)
                    nc.vector.tensor_tensor(part[:, b % 2, :], ps, g, ALU.mult)
                    dve.drain()
                    return nc.vector.tensor_tensor(merged[:, n, :], merged[:, n, :], part[:, b % 2, :], ALU.add)
                return read_out
            for n in range(KT):
                for b in range(3):
                    at = B1_AT["merge"] + (3 * n + b) * (KT + 4)
                    tiles.append(("act", T, weights_still(at, KT, h), act_copy(gates[:, (3 * n + b) % 6, :], ACT.Sigmoid)))
                    tiles.append(("dve", T, weights_still(at + KT, 4, ys[b]), add_branch(n, b), len(tiles) - 1))
            linear("merge", tiles, operands=ys)

            def residual(n):
                return lambda dve, ps: nc.vector.scalar_tensor_tensor(xT[:, n, :], ps, mod[:, 2 * KT + n, 0:1],
                                                                      xT[:, n, :], ALU.mult, ALU.add)
            merged_parts = Split(h_hi, same_place("merged_lo", "merged", [P, KT, T], F32R), merged)
            linear("out", [("dve", T, weights_still(B1_AT["out"] + n * KT, KT, merged_parts), residual(n)) for n in range(KT)],
                   operands=[merged_parts])
        branches.close()

        def up_down(which, at, func, on_first, conv_w, conv_b, norm_of, down_out=None, post=None, work=None):
            with ExitStack() as here:
                gated = tmp(f"gated{which}", [P, FT, T], here)
                if work is None:
                    work = tmp(f"conv{which}", [P, 2, 2, T], here)
                h = Split(h_hi, h_lo)
                ffn(f"up{which}", at["up"], h, conv_w, conv_b, func, on_first,
                    lambda n: gated[:, bass.ds(n, 1), :].rearrange("p o n -> p (o n)") if not isinstance(n, int)
                    else gated[:, n, :], work, norm_of(h))
                ffn_down(f"down{which}", at["down"], Split(h_hi, same_place(f"gated_lo{which}", f"gated{which}", [P, FT, T], F32R),
                                                           gated), [down_out(n) for n in range(KT)] if down_out else (), post and post())

        def col(table, start):
            return lambda n: table[:, bass.ds(n + start, 1)] if not isinstance(n, int) else table[:, n + start:n + start + 1]

        with ExitStack() as here:
            squares = tmp("squaresF", [P, SQUARES, T], here)
            scales = tmp("scalesF", [P, 2, T], here)
            up_down("1", B1_AT, ACT.Silu, False, col(par1, PAR1["conv_w"]), col(par1, PAR1["conv_b"]),
                    lambda h: Norms([dict(src=lambda k: xT[:, k, :], tiles=KT, cols=T, ones=con("ones"), inv=1.0 / D,
                                          gain=lambda k: gain_f[:, k:k + 1], out=lambda k: hT[:, k, :],
                                          end=("split", split_hi, split_lo, lambda k: mod[:, 3 * KT + k, 0:1]))],
                                    squares, scales, splits=[(h, 0)]),
                    lambda n: ("dve", lambda dve, ps: nc.vector.scalar_tensor_tensor(
                        xT[:, n, :], ps, mod[:, 5 * KT + n, 0:1], xT[:, n, :], ALU.mult, ALU.add)))
        phase.close()

        phase = stack.enter_context(ExitStack())
        par2 = tmp("par2", [P, PAR2_W], phase)
        mix = tmp("mix", [P, KT, T], phase)
        mix_lo = same_place("mix_lo", "mix", [P, KT, T], F32R)
        raw = tmp("raw", [P, KT, T], phase)
        squares2 = tmp("squares2", [P, SQUARES, T], phase)
        scales2 = tmp("scales2", [P, 2, T], phase)
        lam = tmp("lam", [P, 2, 32], phase)
        lam_s = tmp("lam_s", [P, 8], phase)

        def p2(name, n=1, at=0):
            return par2[:, PAR2[name] + at:PAR2[name] + at + n]

        def one_norm(name, src, gain, out, tiles=KT, cols=T, ones="ones", width=D, end=None):
            return dict(src=src, tiles=tiles, cols=cols, ones=con(ones), inv=1.0 / width, gain=gain, out=out, end=end)

        norms("norm_final", [one_norm("x", lambda k: xT[:, k, :], lambda k: p1("norm_final", 1, k), lambda k: xT[:, k, :])],
              squares2, scales2)

        def layer_body(l):
            params_loaded = Signal("params_loaded", 16)
            neg_lam, gain_sub = lam_s[:, 4:5], lam_s[:, 5:6]

            def load_params(sp):
                sp.dma_start(par2[:, :], par2_in[bass.ds(l, 1)].rearrange("o p n -> p (o n)")).then_inc(params_loaded.sem, 16)

            with ExitStack() as here:
                q = tmp("q2", [P, 8, T], here)
                k = hT
                v = tmp("v2", [P, TB, 4, P], here)
                dq = tmp("dq", [P, 2, T], here)
                dk = tmp("dk", [P, 2, T], here)
                dv = tmp("dv", [P, TB, 2, P], here)
                with ExitStack() as s:
                    low, u = raw[:, 0:6, :], raw[:, 6:8, :]
                    low_lo = same_place("low_lo", "raw", [P, 6, T], F32R)
                    zv = tmp("zv", [P, TB, 256], s)
                    at = B2_AT["in"]
                    dsts = [(low[:, n, :], ACT.Copy) for n in range(6)] + [(u[:, n, :], ACT.Gelu_apprx_tanh) for n in range(2)] + \
                        [(dq[:, n, :], ACT.Copy) for n in range(2)] + [(dk[:, n, :], ACT.Copy) for n in range(2)]
                    h = Split(h_hi, h_lo)

                    def tokens(x, tb, first=0):
                        return lambda pe, k: x.part(pe, first + k, slice(tb * P, (tb + 1) * P))
                    tiles = [("act", T, weights_still(at + n * KT, KT, h), act_copy(dst, f)) for n, (dst, f) in enumerate(dsts)]
                    gate_in = weights_moving(at + 12 * KT, KT, 2, [tokens(h, tb) for tb in range(TB)])
                    values_in = weights_moving(at + 14 * KT, KT, 2, [tokens(h, tb) for tb in range(TB)])
                    for tb in range(TB):
                        tiles.append(("act", 256, gate_in, act_copy(zv[:, tb, :], ACT.Gelu_apprx_tanh)))
                    for tb in range(TB):
                        tiles.append(("dve", 256, values_in, dve_copy(dv[:, tb, :, :].rearrange("p h n -> p (h n)"))))
                    norm = Norms([one_norm("x", lambda k: xT[:, k, :], lambda k: p2("mix_pre", 1, k), lambda k: hT[:, k, :],
                                           end=("split", split_hi, split_lo, None))],
                                 squares2, scales2, load_params, gains_loaded=params_loaded, splits=[(h, 0)])
                    linear("in2", tiles, norm=norm)
                    rope("rope_keys", [(low[:, 5, :], con("rot_mla"), COS_MLA, SIN_MLA, low[:, 5, :])] +
                         [(x[:, n, :], con("rot_diff"), COS_DIFF, SIN_DIFF, x[:, n, :]) for x in (dq, dk) for n in range(2)],
                         squares2)

                    lows = Split(h_hi, low_lo)
                    tiles = [("act", T, weights_still(B2_AT["uq"] + 3 * n, 3, lows), act_copy(q[:, n, :])) for n in range(8)]

                    def add_rope_key(n):
                        return lambda dve, ps: nc.vector.tensor_tensor(k[:, n, :], ps, low[:, 5, :], ALU.add)
                    tiles += [("dve", T, weights_still(B2_AT["uk"] + 2 * n, 2, lows, first=3), add_rope_key(n)) for n in range(8)]
                    values_up = weights_moving(B2_AT["uv"], 2, 4, [tokens(lows, tb, 3) for tb in range(TB)])
                    tiles += [("act", 512, values_up, act_copy(v[:, tb, :, :].rearrange("p h n -> p (h n)"))) for tb in range(TB)]
                    norm = Norms([
                        one_norm("cq", lambda t: low[:, t, :], lambda t: p2("cq_g", 1, t), lambda t: low[:, t, :], 3, T, "ones", 384,
                                 ("split", split_hi, lambda t: low_lo[:, t, :], None)),
                        one_norm("ckv", lambda t: low[:, 3 + t, :], lambda t: p2("ckv_g", 1, t), lambda t: low[:, 3 + t, :], 2, T,
                                 "ones", 256, ("split", lambda t: h_hi[:, 3 + t, :],
                                                 lambda t: low_lo[:, 3 + t, :], None))], squares2, scales2, splits=[(lows, 0)])
                    linear("up_latent", tiles, norm=norm)
                    rope("rope_queries", [(q[:, h, :], con("rot_mla"), COS_MLA, SIN_MLA, q[:, h, :]) for h in range(8)],
                         squares2)

                    G = 16
                    st = tmp("sgu_stat", [P, 4, G], s)
                    xc = squares2[:, 0:2, :].rearrange("p b n -> p (b n)").rearrange("p (g n) -> p g n", g=G)
                    sq = squares2[:, 2:4, :].rearrange("p b n -> p (b n)").rearrange("p (g n) -> p g n", g=G)
                    centered = Signal("centered", 1)
                    sq_ready = Signal("sgu_square_ready", 1)
                    var_ready = Signal("var_ready", 1)
                    rstd_ready = Signal("rstd_ready", 1)
                    gate_ready = Signal("gate_ready", 1)
                    chunks_mixed = Signal("chunks_mixed", 1)
                    lam_dots = Signal("lam_dots", 1)
                    lam_exp = Signal("lam_exp", 1)

                    def sgu_tensor(pe):
                        pe.wait_ge(gate_ready.sem, gate_ready.at(1))
                        for tb in range(TB):
                            for g in range(4):
                                last = nc.tensor.matmul(bank[(g % 2) * 64:(g % 2) * 64 + 64, g // 2, tb * P:(tb + 1) * P],
                                                        zv[:, tb, g * 64:(g + 1) * 64], p2("sgu_w", P, g * P),
                                                        start=True, stop=True)
                        last.then_inc(chunks_mixed.sem, 1)

                    def per_group(n):
                        return st[:, n, :].rearrange("p (g o) -> p g o", o=1).to_broadcast([P, G, 64])

                    def sgu_vector(dve):
                        pairs = p2("lam", 128).rearrange("p (a s n) -> p a s n", a=2, s=2)
                        nc.vector.tensor_tensor(lam[:, :, :], pairs[:, :, 0, :], pairs[:, :, 1, :], ALU.mult)
                        nc.vector.tensor_tensor(gain_sub, p2("sub_g"), p2("one_less_lam"), ALU.mult)
                        dve.drain()
                        nc.vector.tensor_reduce(lam_s[:, 0:2], lam[:, :, :], AX.X, ALU.add).then_inc(lam_dots.sem, 1)
                        z3 = zv[:, :, :].rearrange("p b (g n) -> p (b g) n", n=64)
                        nc.vector.tensor_reduce(st[:, 0, :], z3, AX.X, ALU.add)
                        dve.drain()
                        nc.vector.tensor_scalar(st[:, 1, :], st[:, 0, :], 1.0 / 64, None, ALU.mult)
                        dve.drain()
                        nc.vector.tensor_tensor(xc, z3, per_group(1), ALU.subtract).then_inc(centered.sem, 1)
                        dve.wait_ge(sq_ready.sem, sq_ready.at(1))
                        nc.vector.tensor_reduce(st[:, 2, :], sq, AX.X, ALU.add).then_inc(var_ready.sem, 1)
                        dve.wait_ge(rstd_ready.sem, rstd_ready.at(1))
                        nc.vector.tensor_tensor(xc, xc, per_group(3), ALU.mult)
                        dve.drain()
                        gains = p2("sgu_g", 256).rearrange("p (o n) -> p o n", o=1).to_broadcast([P, TB, 256])
                        nc.vector.tensor_tensor(zv[:, :, :], xc.rearrange("p (b g) n -> p b (g n)", b=TB), gains, ALU.mult)\
                            .then_inc(gate_ready.sem, 1)
                        dve.wait_ge(lam_exp.sem, lam_exp.at(1))
                        nc.vector.tensor_tensor(lam_s[:, 2:3], lam_s[:, 1:2], lam_s[:, 0:1], ALU.subtract)
                        dve.drain()
                        nc.vector.tensor_tensor(neg_lam, lam_s[:, 2:3], p2("lam_init"), ALU.subtract)
                        dve.wait_ge(chunks_mixed.sem, chunks_mixed.at(1))
                        for n in range(2):
                            y = mix[:, 4 + n, :]
                            b = p2("sgu_b", P, n * P).rearrange("p (o n) -> p o n", o=1).to_broadcast([P, TB, P])
                            nc.vector.tensor_tensor(y.rearrange("p (b n) -> p b n", b=TB),
                                                    bank[:, n, :].rearrange("p (b n) -> p b n", b=TB), b, ALU.add)
                            dve.drain()
                            nc.vector.tensor_tensor(y, y, u[:, n, :], ALU.mult)

                    def sgu_scalar(act):
                        act.wait_ge(lam_dots.sem, lam_dots.at(1))
                        nc.scalar.activation(lam_s[:, 0:2], lam_s[:, 0:2], ACT.Exp).then_inc(lam_exp.sem, 1)
                        act.wait_ge(centered.sem, centered.at(1))
                        nc.scalar.activation(sq, xc, ACT.Square).then_inc(sq_ready.sem, 1)
                        act.wait_ge(var_ready.sem, var_ready.at(1))
                        nc.scalar.activation(st[:, 3, :], st[:, 2, :], ACT.Ln, bias=con("eps", 1), scale=1.0 / 64)
                        act.drain()
                        nc.scalar.activation(st[:, 3, :], st[:, 3, :], ACT.Exp, scale=-0.5).then_inc(rstd_ready.sem, 1)
                    stage("gating", tensor=sgu_tensor, scalar=sgu_scalar, vector=sgu_vector)

                with ExitStack() as a:
                    spare = h_spare
                    qst = spare[:, 0:4, :].rearrange("p (t g) n -> p t g n", t=2)
                    vst = spare[:, 4:6, :].rearrange("p t (b n) -> p t b n", n=P)
                    work = (squares2[:, :, :].rearrange("p (u h) n -> p u (h n)", u=2), spare[:, 6:8, :],
                            tmp("stat2", [P, 2, 4, 2], a))
                    units = [[dict(scores=[lambda i, t=t, g=g, tb=tb: [(0, T, [(qst[:, t, g, tb * P:(tb + 1) * P],
                                                                         k[:, bass.ds(2 * i + g, 1), :].rearrange("p o n -> p (o n)"))])]],
                                  width=T, masks=[], sink=None, keys=TB,
                                  values=[(bank[g * 64:(g + 1) * 64, 6 + t, tb * P:(tb + 1) * P],
                                           [vst[:, t, j, g * 64:(g + 1) * 64] for j in range(TB)])])
                             for g in range(2) for tb in range(TB)] for t in range(2)]
                    attention("latent", 4, units, 96 ** -0.5,
                              lambda i, t: [(qst[:, t, :, :], q[:, bass.ds(2 * i, 2), :]),
                                         (vst[:, t, :, :], v[:, :, bass.ds(i, 1), :].rearrange("p b o n -> p b (o n)"))],
                              [], lambda i, t: (mix[:, bass.ds(i, 1), :].rearrange("p o n -> p (o n)"), bank[:, 6 + t, :]), work)
                    qst4 = raw[:, :, :].rearrange("p (t r) n -> p t r n", t=2)
                    units = [[dict(scores=[lambda i, t=t, g=g, tb=tb, c=c: [(0, T, [(qst4[:, t, 2 * g + c, tb * P:(tb + 1) * P],
                                                                               dk[:, bass.ds(i, 1), :].rearrange("p o n -> p (o n)"))])]
                                          for c in range(2)],
                                  width=T, masks=[], sink=None, keys=TB,
                                  values=[(bank[g * 64:(g + 1) * 64, 6 + t, tb * P:(tb + 1) * P],
                                           [vst[:, t, j, g * 64:(g + 1) * 64] for j in range(TB)])])
                             for g in range(2) for tb in range(TB)] for t in range(2)]
                    attention("differential", 2, units, 32 ** -0.5,
                              lambda i, t: [(qst4[32 * r:32 * r + 32, t, r, :],
                                          dq[32 * r:32 * r + 32, bass.ds(i, 1), :].rearrange("p o n -> p (o n)")) for r in range(4)] +
                              [(vst[:, t, :, :], dv[:, :, bass.ds(i, 1), :].rearrange("p b o n -> p b (o n)"))],
                              [qst4],
                              lambda i, t: (mix[:, bass.ds(i + 6, 1), :].rearrange("p o n -> p (o n)"), bank[:, 6 + t, :]),
                              work, neg_lam=neg_lam)
            norms("sub", [one_norm("o", lambda t, n=n: mix[:, 6 + n, :], lambda t: gain_sub, lambda t, n=n: mix[:, 6 + n, :], 1, T,
                                   "ones64", 64) for n in range(2)], squares2, scales2)

            def post(gain):
                return PostNorm(lambda n: p2(gain, 1, n), raw, squares2, scales2)
            project("mix_out", B2_AT["mix"], Split(h_hi, mix_lo, mix), post("mix_post"))

            with ExitStack() as here:
                k = tmp("mem_k", [P, KT, MEM], here)
                v = tmp("mem_v", [P, 2, 4, 256], here)
                memT = tmp("memT", [P, KT, MEM], here)
                mem_lo = same_place("mem_lo", "memT", [P, KT, MEM], F32R)
                mem_hi = tmp("mem_hi", [P, KT, MEM], here, F32R)
                memory_loaded = Signal("memory_loaded", 16)

                def load_memory(sp):
                    sp.dma_start(memT[:, :, :], memT_in).then_inc(memory_loaded.sem, 16)
                h, mem = Split(h_hi, h_lo), Split(mem_hi, mem_lo)
                tiles = [("act", T, weights_still(B2_AT["mq"] + n * KT, KT, h), act_copy(raw[:, n, :])) for n in range(KT)]
                tiles += [("dve", MEM, weights_still(B2_AT["mk"] + n * KT, KT, mem), dve_copy(k[:, n, :])) for n in range(KT)]
                for half in range(2):
                    group = weights_moving(B2_AT["mv"] + half * 4 * KT, KT, 4, [tokens(mem, tb) for tb in range(2)])
                    for tb in range(2):
                        tiles.append(("act", 512, group,
                                      act_copy(v[:, tb, 2 * half:2 * half + 2, :].rearrange("p h n -> p (h n)"))))
                norm = Norms([one_norm("x", lambda t: xT[:, t, :], lambda t: p2("mem_pre", 1, t), lambda t: hT[:, t, :],
                                           end=("split", split_hi, split_lo, None)),
                                  one_norm("m", lambda t: memT[:, t, :], lambda t: p2("mem_kv", 1, t), lambda t: memT[:, t, :],
                                           KT, MEM, end=("split", lambda t: mem_hi[:, t, :], lambda t: mem_lo[:, t, :], None))], squares2, scales2, load_memory,
                      loaded=(1, memory_loaded), splits=[(h, 0), (mem, KT)])
                linear("mem_qkv", tiles, norm=norm)
                with ExitStack() as a:
                    qst = h_spare[:, 0:4, :].rearrange("p (t e) n -> p t e n", t=2)
                    vst = tmp("mem_vst", [P, 2, 2, 256], a)
                    work = (squares2[:, :, :].rearrange("p (u h) n -> p u (h n)", u=2), tmp("probsT3", [P, 2, 256], a),
                            tmp("stat3", [P, 2, 4, 2], a))
                    units = [[dict(scores=[lambda i, t=t, tb=tb: [(0, MEM, [(qst[:, t, e, tb * P:(tb + 1) * P],
                                                                       k[:, bass.ds(2 * i + e, 1), :].rearrange("p o n -> p (o n)"))
                                                                      for e in range(2)])]],
                                  width=MEM, masks=[], sink=None, keys=2,
                                  values=[(bank[:, 6 + e, tb * P:(tb + 1) * P], [vst[:, t, j, e * P:(e + 1) * P] for j in range(2)])
                                          for e in range(2)]) for tb in range(TB)] for t in range(2)]
                    attention("memory", 4, units, 256 ** -0.5,
                              lambda i, t: [(qst[:, t, :, :], raw[:, bass.ds(2 * i, 2), :]),
                                         (vst[:, t, :, :], v[:, :, bass.ds(i, 1), :].rearrange("p b o n -> p b (o n)"))],
                              [], lambda i, t: (mix[:, bass.ds(2 * i, 2), :], bank[:, 6:8, :]), work,
                              shared_out=True)
            project("mem_out", B2_AT["mo"], Split(h_hi, mix_lo, mix), post("mem_post"))

            up_down("2", B2_AT, ACT.Gelu_apprx_tanh, True, col(par2, PAR2["conv_w"]), col(par2, PAR2["conv_b"]),
                    lambda h: Norms([one_norm("x", lambda t: xT[:, t, :], lambda t: p2("ffn_pre", 1, t), lambda t: hT[:, t, :],
                                              end=("split", split_hi, split_lo, None))], squares2, scales2, splits=[(h, 0)]),
                    post=lambda: post("ffn_post"), work=mix[:, 0:4, :].rearrange("p (u s) n -> p u s n", u=2))

        ws.base, ws.fed, ws.begun, ws.rounded, ws.halved, ws.limit = B1_SLABS, 0, 0, 0, 0, B2_SLABS
        with nc.Fori(0, LAYERS) as l:
            layer[0] = l
            layer_body(l)
        layer[0] = None
        totals = {r: n for r, n in used_here.items() if r.endswith("_2")}
        assert totals == PER_LAYER, totals

        stored = Signal("stored", 16)

        def sync(sp):
            sp.dma_start(out, xT[:, :, :]).then_inc(stored.sem, 16)
            sp.wait_ge(stored.sem, stored.at(16))
        ws.limit = 0
        stage("store", sync=sync)


def constants():
    c = np.zeros((P, CONST_W), np.float32)

    def put(name, a, at=0):
        c[:, CONST[name] + at:CONST[name] + at + a.shape[1]] = a
    p = np.arange(P)
    put("ident", np.eye(P))
    put("ones", np.ones((P, P)))
    put("ones64", (p[:, None] // 64 == p[None, :] // 64) * 1.0)
    rot = np.zeros((P, P))
    rot[p[1::2], p[0::2]] = -1.0
    rot[p[0::2], p[1::2]] = 1.0
    put("rot1", rot)
    rot = np.zeros((P, P))
    for i in range(16):
        rot[64 + 16 + i, 64 + i] = -1.0
        rot[64 + i, 64 + 16 + i] = 1.0
    put("rot_mla", rot)
    rot = np.zeros((P, P))
    for base in range(0, P, 32):
        for i in range(8):
            rot[base + 8 + i, base + i] = -1.0
            rot[base + i, base + 8 + i] = 1.0
    put("rot_diff", rot)
    put("mask_prev", np.where(p[None, :] >= p[:, None], 0.0, NEG_BIG))
    put("mask_next", np.where(p[None, :] <= p[:, None], 0.0, NEG_BIG))
    j, t = p[:, None], p[None, :]
    for d in range(2):
        for l in range(LEVELS + 1):
            if l == LEVELS:
                m = j == t
            else:
                h = CHUNK >> l
                jh, th = (0, 1) if d == 0 else (1, 0)
                m = (j // (2 * h) == t // (2 * h)) & (j // h % 2 == jh) & (t // h % 2 == th)
            put("levels", m * 1.0, (d * (LEVELS + 1) + l) * P)
    tok = np.arange(ALLT)
    put("reset", np.broadcast_to((tok % CHUNK != 0) * 1.0, (P, ALLT)))
    put("reset", np.broadcast_to((tok % CHUNK != CHUNK - 1) * 1.0, (P, ALLT)), ALLT)
    freq = np.zeros((P, 2), np.float32)
    inv = (THETA_2 ** (-np.arange(0, 32, 2, dtype=np.float32) / np.float32(32))).astype(np.float32)
    freq[64:96, 0] = np.tile(inv, 2)
    inv = (THETA_2 ** (-np.arange(0, 16, 2, dtype=np.float32) / np.float32(16))).astype(np.float32)
    for base in range(0, P, 32):
        freq[base:base + 16, 1] = np.tile(inv, 2)
    put("freq", freq)
    put("eps", np.full((P, 1), EPS))
    put("half_pi", np.full((P, 1), np.pi / 2))
    put("one", np.ones((P, 1)))
    return c


def axial_tables():
    p, n = np.arange(P), np.arange(T)
    half = HD // 4
    inv = (THETA_1 ** (-np.arange(0, 2 * half, 2, dtype=np.float32) / np.float32(2 * half))).astype(np.float32)
    ang = np.concatenate([(n // GRID_W).astype(np.float32)[:, None] * inv, (n % GRID_W).astype(np.float32)[:, None] * inv], 1)
    ang = ang.T[(p % HD) // 2]
    return np.stack([np.cos(ang), np.sin(ang)], 1)


def weight_stream(w):
    blocks = []

    def still(m, cols, tiles=None):
        for c in cols:
            for k in range(m.shape[0] // P):
                blocks.append(m[k * P:(k + 1) * P, c])

    def padded(m, at):
        full = np.zeros((m.shape[0], P), np.float32)
        full[:, at:at + m.shape[1]] = m
        return full

    def moving(m, n):
        for c in range(0, m.shape[1], n * P):
            for k in range(m.shape[0] // P):
                for e in range(n):
                    blocks.append(m[k * P:(k + 1) * P, c + e * P:c + (e + 1) * P])

    def tiles(n, start=0):
        return [slice(start + c * P, start + (c + 1) * P) for c in range(n)]
    moving(w["w_mod"][0], 4)
    w_in = w["w_in"][0]
    pair = [np.r_[g * HD:(g + 1) * HD, (g + 4) * HD:(g + 5) * HD] for g in range(4)]
    still(w_in, tiles(12, 1536))
    moving(w_in[:, 3072:3584], 4)
    for at in (0, 768):
        still(w_in, [at + c for c in pair])
        still(w_in, [slice(at + 512, at + 640), slice(at + 640, at + 768)])
    still(w_in, tiles(4, 3584))
    for n in range(KT):
        for b in range(3):
            still(w_in, [slice(4096 + b * D + n * P, 4096 + b * D + (n + 1) * P)])
            wb = w["w_branch"][0, b]
            if b < 2:
                wb = np.concatenate([wb[c] for c in pair])
            still(wb, tiles(KT)[n:n + 1])
    still(w["w_out"][0], tiles(KT))

    def ffn_blocks(up, down):
        for n in range(FT):
            still(up, [slice(n * P, (n + 1) * P), slice(FF + n * P, FF + (n + 1) * P)])
        moving(down, KT)
    ffn_blocks(w["w_up"][0], w["w_down"][0])
    assert len(blocks) == B1_SLABS * SLAB
    for l in range(LAYERS):
        w_in = w["w_in_2"][l]
        still(w_in, tiles(5))
        still(padded(w_in[:, 640:672], 64), tiles(1))
        still(w_in, tiles(2, 672) + tiles(4, 1184))
        moving(w_in[:, 928:1184], 2)
        moving(w_in[:, 1696:1952], 2)
        uq, ukv = w["mla_w_uq_2"][l], w["mla_w_ukv_2"][l]
        for h in range(8):
            still(padded(uq[:, h * 96:(h + 1) * 96], 0), tiles(1))
        for h in range(8):
            still(padded(ukv[:, h * P:h * P + 64], 0), tiles(1))
        moving(np.concatenate([ukv[:, h * P + 64:(h + 1) * P] for h in range(8)], 1), 4)
        still(w["w_mix_out_2"][l], tiles(KT))
        still(w["mem_w_q_2"][l], tiles(KT))
        still(w["mem_w_kv_2"][l], tiles(KT))
        moving(w["mem_w_kv_2"][l][:, D:], 4)
        still(w["mem_w_o_2"][l], tiles(KT))
        ffn_blocks(w["ffn_w_up_2"][l], w["ffn_w_down_2"][l])
    assert len(blocks) == SLABS * SLAB
    return np.stack(blocks).reshape(SLABS, SLAB, P, P).transpose(0, 2, 1, 3).reshape(SLABS, P, SLAB * P)


def cols(v):
    return np.asarray(v).reshape(-1, P).T


def conv_cols(w):
    return np.concatenate([cols(tap) for tap in w], 1)


def rows(v):
    v = np.asarray(v).reshape(1, -1)
    return np.broadcast_to(v, (P, v.shape[1]))


def table(places, width, fields):
    t = np.zeros((P, width), np.float32)
    for name, a in fields.items():
        t[:, places[name]:places[name] + a.shape[1]] = a
    return t


def host_layout(w):
    w = {k: np.asarray(v) for k, v in w.items()}

    def features_first(a):
        return np.ascontiguousarray(a[0].T.reshape(KT, P, -1).transpose(1, 0, 2))
    both = np.stack([cols(w["c"][0]), cols(w["c_ctx"])], 2).reshape(P, 2 * KT)
    par1 = table(PAR1, PAR1_W, dict(
        c=both, b_mod=cols(w["b_mod"][0]), norm_mix=cols(w["norm_mix"][0]), norm_ffn=cols(w["norm_ffn"][0]),
        qn=cols(np.concatenate([w["qn_b"][0]] * 2)), kn=cols(np.concatenate([w["kn_b"][0]] * 2)),
        lb=np.concatenate([cols(w["lb_fwd"][0]), cols(w["lb_bwd"][0])], 1), gn=cols(w["gn_c"][0]),
        conv_w=conv_cols(w["w_dw"][0]), conv_b=cols(w["b_dw"][0]), norm_final=cols(w["norm_final"]),
        sink=rows(w["sink_a"][0])))
    par2 = []
    for l in range(LAYERS):
        lam_init = 0.8 - 0.6 * np.exp(-0.3 * l)
        par2.append(table(PAR2, PAR2_W, dict(
            mix_pre=cols(w["mix_pre_g_2"][l]), mix_post=cols(w["mix_post_g_2"][l]), cq_g=cols(w["mla_cq_g_2"][l]),
            ckv_g=cols(w["mla_ckv_g_2"][l]), sub_g=cols(np.concatenate([w["diff_sub_g_2"][l]] * 2)),
            mem_pre=cols(w["mem_pre_g_2"][l]), mem_post=cols(w["mem_post_g_2"][l]), mem_kv=cols(w["mem_kv_g_2"][l]),
            ffn_pre=cols(w["ffn_pre_g_2"][l]), ffn_post=cols(w["ffn_post_g_2"][l]),
            conv_w=conv_cols(w["ffn_conv_w_2"][l]), conv_b=cols(w["ffn_conv_b_2"][l]),
            lam=rows(np.concatenate([w[f"diff_lam_{n}_2"][l] for n in ("q1", "k1", "q2", "k2")])),
            lam_init=np.full((P, 1), lam_init, np.float32), one_less_lam=np.full((P, 1), 1.0 - lam_init, np.float32),
            sgu_g=rows(w["sgu_norm_g_2"][l]),
            sgu_b=np.concatenate([np.repeat(w["sgu_b_s_2"][l][2 * n:2 * n + 2], 64, 0) for n in range(2)], 1),
            sgu_w=w["sgu_w_s_2"][l].transpose(2, 0, 1).reshape(P, 4 * P))))
    return {"stream": weight_stream(w), "xT": features_first(w["x"]), "ctxT": features_first(w["ctx"]),
            "memT": features_first(w["mem_2"]), "pos": w["positions_2"], "const": constants(), "axial": axial_tables(), "par1": par1,
            "par2": np.stack(par2)}


def kernel(**inputs):
    import concourse.bacc as bacc
    from concourse.bass_utils import run_bass_kernel_spmd
    arrays = {f"in_{name}": np.ascontiguousarray(a) for name, a in host_layout(inputs).items()}
    nc = bacc.Bacc("TRN2", target_bir_lowering=False, num_devices=1, dynamic_dma_scratch_size=1024)
    args = [nc.dram_tensor(name, a.shape, mybir.dt.from_np(a.dtype), kind="ExternalInput").ap()
            for name, a in arrays.items()]
    out = nc.dram_tensor("out", (P, KT, T), F32, kind="ExternalOutput").ap()
    build_program(nc, *args, out)
    got = run_bass_kernel_spmd(nc, [arrays], core_ids=[0]).results[0]["out"]
    return np.ascontiguousarray(got.transpose(1, 0, 2).reshape(D, T).T)[None]
```
